# Optimizing a Trainium2 kernel written in Bass

```python
import jax, jax.numpy as jnp
from jax import lax
import numpy as np

D_MODEL = 1024
BATCH = 1
SEQ = 512
DEPTH = 2

HEAD_DIM = 64
D_MIX = D_MODEL
D_FF = 2816
PLE_DIM = 256
ROPE_THETA = 10000.0
LN_EPS = 1e-5
RMS_EPS = 1e-6
NEG_INF = -1e30
LOG_FLOOR = 1e-30
ATTN_QBLK = 128
NSA_WIDTH = D_MIX // 4
NSA_HEADS = NSA_WIDTH // HEAD_DIM
NSA_KV = 1
CMP_LEN = 32
CMP_STRIDE = 16
CMP_HID = 256
SEL_BLOCK = 64
SEL_TOPN = 16
SEL_FORCE = 1e4
NSA_WINDOW = 512
NSA_QBLK = SEL_BLOCK
SWA_WIDTH = D_MIX // 4
SWA_HEADS = SWA_WIDTH // HEAD_DIM
SWA_KV = 2
SWA_WINDOW = 128
HGRN_WIDTH = D_MIX // 2
HGRN_HEADS = 4
HGRN_DIM = HGRN_WIDTH // HGRN_HEADS
HGRN_CHUNK = 64
N_IN = (NSA_WIDTH + 6 * NSA_KV * HEAD_DIM + 3 * NSA_HEADS
        + SWA_WIDTH + 2 * SWA_KV * HEAD_DIM + 4 * HGRN_WIDTH)

kernel_name = 'hybrid_nsa_swa_hgrn2_macaron_deepnorm'

def layer_norm(x, g, b):
    xf = x.astype(jnp.float32)
    mu = jnp.mean(xf, axis=-1, keepdims=True)
    var = jnp.mean(jnp.square(xf - mu), axis=-1, keepdims=True)
    return ((xf - mu) * lax.rsqrt(var + LN_EPS) * g + b).astype(x.dtype)

def swiglu(x, w_gu, w_down):
    a, u = jnp.split(x @ w_gu, 2, axis=-1)
    return (jax.nn.silu(a) * u) @ w_down

def rope_tables(S):
    inv = 1.0 / (ROPE_THETA ** (jnp.arange(0, HEAD_DIM, 2, dtype=jnp.float32) / HEAD_DIM))
    ang = jnp.arange(S, dtype=jnp.float32)[:, None] * inv[None, :]
    return jnp.cos(ang), jnp.sin(ang)

def apply_rope(x, cos, sin):
    x1, x2 = jnp.split(x, 2, axis=-1)
    c = cos[None, :, None, :].astype(x.dtype)
    s = sin[None, :, None, :].astype(x.dtype)
    return jnp.concatenate([x1 * c - x2 * s, x1 * s + x2 * c], axis=-1)

def banded_attention(q, k, v, window, sinks=None):
    B, S, Hq, hd = q.shape
    Hk = k.shape[2]
    G = Hq // Hk
    nb = S // ATTN_QBLK
    span = ATTN_QBLK + window
    kp = jnp.pad(k, ((0, 0), (window, 0), (0, 0), (0, 0)))
    vp = jnp.pad(v, ((0, 0), (window, 0), (0, 0), (0, 0)))
    qb = q.reshape(B, nb, ATTN_QBLK, Hk, G, hd).transpose(1, 0, 2, 3, 4, 5)
    rel_k = jnp.arange(span)[None, :] - window
    diff = jnp.arange(ATTN_QBLK)[:, None] - rel_k
    band = (diff >= 0) & (diff < window)
    scale = hd ** -0.5

    def block(args):
        qi, bi = args
        start = bi * ATTN_QBLK
        kk = lax.dynamic_slice_in_dim(kp, start, span, axis=1)
        vv = lax.dynamic_slice_in_dim(vp, start, span, axis=1)
        s = jnp.einsum('bqhgd,bkhd->bhgqk', qi, kk).astype(jnp.float32) * scale
        mask = band & ((start + rel_k) >= 0)
        s = jnp.where(mask, s, NEG_INF)
        if sinks is None:
            pr = jax.nn.softmax(s, axis=-1)
        else:
            sk = jnp.broadcast_to(sinks.astype(jnp.float32).reshape(1, Hk, G, 1, 1), s.shape[:-1] + (1,))
            pr = jax.nn.softmax(jnp.concatenate([s, sk], axis=-1), axis=-1)[..., :-1]
        return jnp.einsum('bhgqk,bkhd->bqhgd', pr.astype(vv.dtype), vv)

    out = lax.map(block, (qb, jnp.arange(nb)))
    return out.transpose(1, 0, 2, 3, 4, 5).reshape(B, S, Hq, hd)

def nsa_mixer(xq, k_cmp, v_cmp, k_slc, v_slc, k_win, v_win, gate_logit,
              cmp_pos, wk1, wk2, wv1, wv2, cos, sin):
    B, S, _ = xq.shape
    dt = xq.dtype
    q = xq.reshape(B, S, NSA_HEADS, HEAD_DIM)
    q_r = apply_rope(q, cos, sin)
    scale = HEAD_DIM ** -0.5
    n_cmp = (S - CMP_LEN) // CMP_STRIDE + 1
    tok = jnp.arange(n_cmp)[:, None] * CMP_STRIDE + jnp.arange(CMP_LEN)[None, :]

    def compress(t, w1, w2):
        blocks = t[:, tok] + cmp_pos
        return jax.nn.silu(blocks.reshape(B, n_cmp, CMP_LEN * HEAD_DIM) @ w1) @ w2

    kc = compress(k_cmp, wk1, wk2)
    vc = compress(v_cmp, wv1, wv2)
    cmp_end = jnp.arange(n_cmp) * CMP_STRIDE + CMP_LEN - 1
    n_sel = S // SEL_BLOCK
    top_n = min(SEL_TOPN, n_sel)
    ci = jnp.arange(n_cmp)[:, None] * CMP_STRIDE
    sj = jnp.arange(n_sel)[None, :] * SEL_BLOCK
    overlap = ((ci < sj + SEL_BLOCK) & (ci + CMP_LEN > sj)).astype(jnp.float32)
    ks = apply_rope(k_slc[:, :, None, :], cos, sin)[:, :, 0].reshape(B, n_sel, SEL_BLOCK, HEAD_DIM)
    vs = v_slc.reshape(B, n_sel, SEL_BLOCK, HEAD_DIM)
    sel_j = jnp.arange(n_sel)
    nq = S // NSA_QBLK
    qc_b = q.reshape(B, nq, NSA_QBLK, NSA_HEADS, HEAD_DIM).transpose(1, 0, 2, 3, 4)
    qs_b = q_r.reshape(B, nq, NSA_QBLK, NSA_HEADS, HEAD_DIM).transpose(1, 0, 2, 3, 4)
    t_b = jnp.arange(S).reshape(nq, NSA_QBLK)

    def block(args):
        qc, qs, t = args
        sc = jnp.einsum('bqhd,bjd->bqhj', qc, kc).astype(jnp.float32) * scale
        cval = cmp_end[None, :] <= t[:, None]
        anyv = jnp.any(cval, axis=-1).astype(jnp.float32)
        sc = jnp.where(cval[None, :, None, :], sc, NEG_INF)
        pc = jax.nn.softmax(sc, axis=-1) * anyv[None, :, None, None]
        o_cmp = jnp.einsum('bqhj,bjd->bqhd', pc.astype(vc.dtype), vc)
        imp = jnp.einsum('bqhj,jn->bqn', pc, overlap)
        blk_t = t // SEL_BLOCK
        forced = (sel_j[None, :] == 0) | (sel_j[None, :] == blk_t[:, None]) | (sel_j[None, :] == blk_t[:, None] - 1)
        causal_blk = sel_j[None, :] <= blk_t[:, None]
        score = jnp.where(forced, SEL_FORCE, jnp.where(causal_blk, imp, -SEL_FORCE))
        _, idx = lax.top_k(score, top_n)
        kg = jax.vmap(lambda kb, ix: kb[ix])(ks, idx)
        vg = jax.vmap(lambda vb, ix: vb[ix])(vs, idx)
        ss = jnp.einsum('bqhd,bqnkd->bqhnk', qs, kg).astype(jnp.float32) * scale
        kpos = idx[..., None] * SEL_BLOCK + jnp.arange(SEL_BLOCK)
        valid = kpos <= t[None, :, None, None]
        ss = jnp.where(valid[:, :, None], ss, NEG_INF)
        ps = jax.nn.softmax(ss.reshape(ss.shape[:3] + (-1,)), axis=-1).reshape(ss.shape)
        o_slc = jnp.einsum('bqhnk,bqnkd->bqhd', ps.astype(vg.dtype), vg)
        return o_cmp, o_slc

    o_cmp, o_slc = lax.map(block, (qc_b, qs_b, t_b))
    o_cmp = o_cmp.transpose(1, 0, 2, 3, 4).reshape(B, S, NSA_HEADS, HEAD_DIM)
    o_slc = o_slc.transpose(1, 0, 2, 3, 4).reshape(B, S, NSA_HEADS, HEAD_DIM)
    kw = apply_rope(k_win.reshape(B, S, NSA_KV, HEAD_DIM), cos, sin)
    o_win = banded_attention(q_r, kw, v_win.reshape(B, S, NSA_KV, HEAD_DIM), NSA_WINDOW)
    g = jax.nn.sigmoid(gate_logit.astype(jnp.float32)).reshape(B, S, NSA_HEADS, 3)
    o = g[..., 0:1] * o_cmp + g[..., 1:2] * o_slc + g[..., 2:3] * o_win
    return o.reshape(B, S, NSA_WIDTH).astype(dt)

def hgrn2_mixer(q, z_f, i_in, g, lb, norm_g):
    B, S, _ = q.shape
    H, Dh, C = HGRN_HEADS, HGRN_DIM, HGRN_CHUNK
    f32 = jnp.float32
    lb = lb.astype(f32).reshape(H, Dh)
    z = z_f.astype(f32).reshape(B, S, H, Dh)
    log_f = jnp.logaddexp(jnp.log(jnp.maximum(lb, LOG_FLOOR)), jnp.log1p(-lb) + jax.nn.log_sigmoid(z))
    k = (1.0 - lb) * jax.nn.sigmoid(-z)
    nC = S // C

    def chunks(t):
        return t.astype(f32).reshape(B, nC, C, H, Dh).transpose(1, 0, 3, 2, 4)

    qc = chunks(q.reshape(B, S, H, Dh))
    kc = chunks(k)
    vc = chunks(i_in.reshape(B, S, H, Dh))
    lfc = chunks(log_f)
    tri = jnp.tril(jnp.ones((C, C), dtype=bool))[None, None, :, :, None]

    def step(state, inp):
        qt, kt, vt, lf = inp
        b = jnp.cumsum(lf, axis=2)
        diff = b[:, :, :, None, :] - b[:, :, None, :, :]
        decay = jnp.where(tri, jnp.exp(jnp.where(tri, diff, 0.0)), 0.0)
        att = jnp.einsum('bhtc,bhsc,bhtsc->bhts', qt, kt, decay)
        o = jnp.einsum('bhts,bhsv->bhtv', att, vt) + jnp.einsum('bhtc,bhcv->bhtv', qt * jnp.exp(b), state)
        b_last = b[:, :, -1:, :]
        new_state = state * jnp.exp(b_last[:, :, 0, :, None]) + jnp.einsum('bhsc,bhsv->bhcv', kt * jnp.exp(b_last - b), vt)
        return new_state, o

    state0 = jnp.zeros((B, H, Dh, Dh), f32)
    _, o = lax.scan(step, state0, (qc, kc, vc, lfc))
    o = o.transpose(1, 0, 3, 2, 4).reshape(B, S, H, Dh)
    o = o * lax.rsqrt(jnp.mean(o * o, axis=-1, keepdims=True) + RMS_EPS)
    o = o.reshape(B, S, HGRN_WIDTH) * norm_g.astype(f32) * jax.nn.silu(g.astype(f32))
    return o.astype(q.dtype)

def token_mix(x, w_in, w_out, cmp_pos, wk1, wk2, wv1, wv2, sinks, lb, norm_g, cos, sin):
    B, S, _ = x.shape
    kvd = NSA_KV * HEAD_DIM
    skv = SWA_KV * HEAD_DIM
    sizes = [NSA_WIDTH, kvd, kvd, kvd, kvd, kvd, kvd, 3 * NSA_HEADS,
             SWA_WIDTH, skv, skv,
             HGRN_WIDTH, HGRN_WIDTH, HGRN_WIDTH, HGRN_WIDTH]
    offs = np.cumsum(sizes)[:-1].tolist()
    (nq, kcm, vcm, ksl, vsl, kwn, vwn, ngl, sq, sk, sv, hq, hf, hi, hg) = jnp.split(x @ w_in, offs, axis=-1)
    o_nsa = nsa_mixer(nq, kcm, vcm, ksl, vsl, kwn, vwn, ngl, cmp_pos, wk1, wk2, wv1, wv2, cos, sin)
    qs = apply_rope(sq.reshape(B, S, SWA_HEADS, HEAD_DIM), cos, sin)
    ksw = apply_rope(sk.reshape(B, S, SWA_KV, HEAD_DIM), cos, sin)
    o_swa = banded_attention(qs, ksw, sv.reshape(B, S, SWA_KV, HEAD_DIM), SWA_WINDOW, sinks).reshape(B, S, SWA_WIDTH)
    o_hgrn = hgrn2_mixer(hq, hf, hi, hg, lb, norm_g)
    return jnp.concatenate([o_nsa, o_swa, o_hgrn], axis=-1) @ w_out

def setup_inputs(seed: int = 0) -> dict:
    key = jax.random.key(seed)
    ks = jax.random.split(key, 20)
    f32 = jnp.float32
    beta = (8.0 * DEPTH) ** -0.25

    def nrm(k, shape, scale):
        return jax.random.normal(k, shape, f32) * scale

    return {
        'x': nrm(ks[0], (BATCH, SEQ, D_MODEL), 1.0),
        'p': nrm(ks[1], (DEPTH, BATCH, SEQ, PLE_DIM), 1.0),
        'ln_g': 1.0 + nrm(ks[2], (DEPTH, 3, D_MODEL), 0.02),
        'ln_b': nrm(ks[3], (DEPTH, 3, D_MODEL), 0.02),
        'ffn_w_gu': nrm(ks[4], (DEPTH, 2, D_MODEL, 2 * D_FF), D_MODEL ** -0.5),
        'ffn_w_down': nrm(ks[5], (DEPTH, 2, D_FF, D_MODEL), beta * D_FF ** -0.5),
        'w_in': nrm(ks[6], (DEPTH, D_MODEL, N_IN), D_MODEL ** -0.5),
        'w_out': nrm(ks[7], (DEPTH, D_MIX, D_MODEL), beta * D_MIX ** -0.5),
        'cmp_pos': nrm(ks[8], (DEPTH, CMP_LEN, HEAD_DIM), 0.1),
        'cmp_k_w1': nrm(ks[9], (DEPTH, CMP_LEN * HEAD_DIM, CMP_HID), (CMP_LEN * HEAD_DIM) ** -0.5),
        'cmp_k_w2': nrm(ks[10], (DEPTH, CMP_HID, HEAD_DIM), CMP_HID ** -0.5),
        'cmp_v_w1': nrm(ks[11], (DEPTH, CMP_LEN * HEAD_DIM, CMP_HID), (CMP_LEN * HEAD_DIM) ** -0.5),
        'cmp_v_w2': nrm(ks[12], (DEPTH, CMP_HID, HEAD_DIM), CMP_HID ** -0.5),
        'swa_sinks': nrm(ks[13], (DEPTH, SWA_HEADS), 0.5),
        'hgrn_lb_raw': nrm(ks[14], (DEPTH, HGRN_WIDTH), 0.1),
        'hgrn_norm_g': 1.0 + nrm(ks[15], (DEPTH, HGRN_WIDTH), 0.02),
        'ple_w': nrm(ks[16], (DEPTH, PLE_DIM, D_MODEL), beta * PLE_DIM ** -0.5),
        'ple_gate_w': nrm(ks[17], (DEPTH, D_MODEL, D_MODEL), D_MODEL ** -0.5),
        'ple_gate_b': nrm(ks[18], (DEPTH, D_MODEL), 0.02),
    }

def reference(x, p, ln_g, ln_b, ffn_w_gu, ffn_w_down, w_in, w_out, cmp_pos,
              cmp_k_w1, cmp_k_w2, cmp_v_w1, cmp_v_w2, swa_sinks, hgrn_lb_raw,
              hgrn_norm_g, ple_w, ple_gate_w, ple_gate_b):
    B, S, _ = x.shape
    cos, sin = rope_tables(S)
    alpha = (2.0 * DEPTH) ** 0.25
    sm = jax.nn.softmax(hgrn_lb_raw.astype(jnp.float32), axis=0)
    lower_bounds = jnp.cumsum(sm, axis=0) - sm[0]
    for i in range(DEPTH):
        x = layer_norm(alpha * x + 0.5 * swiglu(x, ffn_w_gu[i, 0], ffn_w_down[i, 0]), ln_g[i, 0], ln_b[i, 0])
        y = token_mix(x, w_in[i], w_out[i], cmp_pos[i], cmp_k_w1[i], cmp_k_w2[i], cmp_v_w1[i], cmp_v_w2[i],
                      swa_sinks[i], lower_bounds[i], hgrn_norm_g[i], cos, sin)
        x = layer_norm(alpha * x + y, ln_g[i, 1], ln_b[i, 1])
        x = layer_norm(alpha * x + 0.5 * swiglu(x, ffn_w_gu[i, 1], ffn_w_down[i, 1]), ln_g[i, 2], ln_b[i, 2])
        x = x + jax.nn.sigmoid(x @ ple_gate_w[i] + ple_gate_b[i]) * (p[i] @ ple_w[i])
    return x


_drawn_inputs = setup_inputs


def setup_inputs(seed=0):
    import zlib

    import numpy as np

    out = dict(_drawn_inputs(seed))
    spreads = {}
    factors = {'cmp_pos': 7.947,
     'cmp_k_w1': 4.628,
     'cmp_k_w2': 4.836,
     'swa_sinks': 8.0,
     'hgrn_lb_raw': 4.548,
     'hgrn_norm_g': 8.0,
     'ple_gate_b': 8.0}
    for name, (base, spread) in spreads.items():
        noise = np.random.default_rng([zlib.crc32(name.encode()), seed]).standard_normal(out[name].shape)
        drawn = base * np.exp(spread * noise) if base else spread * noise
        out[name] = __import__('jax').numpy.asarray(drawn.astype(out[name].dtype))
    for name, factor in factors.items():
        out[name] = (out[name] * factor).astype(out[name].dtype)
    return out
```

```python
from contextlib import ExitStack

import numpy as np

import concourse.bass as bass
from concourse import mybir

F32 = mybir.dt.float32
F32R = mybir.dt.float32r
ALU = mybir.AluOpType
ACT = mybir.ActivationFunctionType
AX = mybir.AxisListType

P = 128
D_MODEL, SEQ, DEPTH, D_FF, PLE_DIM = 1024, 512, 2, 2816, 256
HEAD_DIM, NSA_HEADS, SWA_HEADS, HGRN_HEADS = 64, 4, 4, 4
CMP_LEN, CMP_STRIDE, CMP_HID = 32, 16, 256
N_CMP = (SEQ - CMP_LEN) // CMP_STRIDE + 1
DT = D_MODEL // P
FT = D_FF // P
QT = SEQ // P
PT_ = PLE_DIM // P
KD = FT // 2
NSA_COLS = 256 + 6 * 64 + 12
N_PM = 26
ALPHA = (2.0 * DEPTH) ** 0.25
LN_EPS, RMS_EPS = 1e-5, 1e-6
SCALE = HEAD_DIM ** -0.5
LN_FLOOR = float(np.log(np.float32(1e-30)))
RAW, SPLIT = 4, 2
LEVELS = 7

T_Q, T_CMP, T_SLC, T_WIN, T_GATE, T_SQ, T_SK, T_SV, T_HQ, T_HF, T_HI, T_HG = 0, 2, 3, 4, 5, 6, 8, 9, 10, 14, 18, 22

C_ID, C_ROT, C_DUP, C_ROTDUP, C_CAUSAL, C_BAND, C_CMP = (P * k for k in range(7))
C_HG = C_CMP + QT * N_CMP
C_END = C_HG + (LEVELS + 1) * P


def shape_constants():
    c = np.zeros((P, C_END), np.float32)
    r = np.arange(P)
    c[:, C_ID:C_ID + P] = np.eye(P)
    for m in range(P):
        other = m + 32 if m % 64 < 32 else m - 32
        sign = -1.0 if m % 64 < 32 else 1.0
        c[other, C_ROT + m] = sign
        for half in (0, 64):
            c[half + m % 64, C_DUP + m] = 1.0
            c[half + other % 64, C_ROTDUP + m] = sign
    q, k = r[:, None], r[None, :]
    c[:, C_CAUSAL:C_CAUSAL + P] = np.where(k <= q, 0.0, -1e30)
    c[:, C_BAND:C_BAND + P] = np.where(k > q, 0.0, -1e30)
    ends = np.arange(N_CMP) * CMP_STRIDE + CMP_LEN - 1
    for i in range(QT):
        c[:, C_CMP + i * N_CMP:C_CMP + (i + 1) * N_CMP] = np.where(ends[None, :] <= i * P + q, 0.0, -1e30)
    s, t = r[:, None], r[None, :]
    for lv in range(LEVELS):
        m = 1 << lv
        same = (s // (2 * m)) == (t // (2 * m))
        c[:, C_HG + lv * P:C_HG + (lv + 1) * P] = same & (s // m % 2 == 0) & (t // m % 2 == 1)
    c[:, C_HG + LEVELS * P:] = s == t
    inv = (1.0 / (np.float32(10000.0) ** (np.arange(0, HEAD_DIM, 2, dtype=np.float32) / HEAD_DIM))).astype(np.float32)
    ang = np.arange(SEQ, dtype=np.float32)[:, None] * inv[None, :]
    rope = np.concatenate([np.tile(np.cos(ang).T, (4, 1)), np.tile(np.sin(ang).T, (4, 1))], axis=1)
    return c, rope.astype(np.float32)


def build(nc, x, p, ln_g, ln_b, ffn_w_gu, ffn_w_down, w_in, w_out, cmp_pos, cmp_k_w1, cmp_k_w2, cmp_v_w1,
          cmp_v_w2, swa_sinks, hgrn_lb_raw, hgrn_norm_g, ple_w, ple_gate_w, ple_gate_b, consts_d, rope_d, out):
    with ExitStack() as whole:
        def scope():
            return ExitStack()

        stage = ["start"]

        def sb(ctx, name, shape, dt=F32):
            return ctx.enter_context(nc.sbuf_tensor(f"{stage[0]}_{name}", shape, dt))

        ps = whole.enter_context(nc.psum_tensor("banks", [P, 8, 512], F32))

        xT = sb(whole, "xT", [P, DT, SEQ])
        xhi = sb(whole, "xhi", [P, DT, SEQ], F32R)
        xlo = sb(whole, "xlo", [P, DT, SEQ], F32R)
        ident = sb(whole, "ident", [P, P])
        mean_w = sb(whole, "mean_w", [P, P])
        par = sb(whole, "par", [P, P])
        hgp = sb(whole, "hgp", [P, DEPTH, 3, HGRN_HEADS])
        lng = sb(whole, "lng", [P, 3 * DT])
        lnb = sb(whole, "lnb", [P, 3 * DT])
        gbh = sb(whole, "gbh", [P, DT])
        epsc = sb(whole, "epsc", [P, 2])
        sinks = sb(whole, "sinks", [P, DEPTH * SWA_HEADS])
        PG, PB, PGB, PNG, PLB = 0, 24 * DEPTH, 48 * DEPTH, 56 * DEPTH, 60 * DEPTH

        def semaphores(names, slots=()):
            sems = {n: nc.alloc_semaphore(f"{stage[0]}_{n}") for n in names}
            for n, count in slots:
                sems[n] = [nc.alloc_semaphore(f"{stage[0]}_{n}{k}") for k in range(count)]
            return sems

        def clear(sems):
            for s in sems.values():
                for one in (s if isinstance(s, list) else [s]):
                    nc.sync.sem_clear(one)
            nc.all_engine_barrier()
            for s in sems.values():
                for one in (s if isinstance(s, list) else [s]):
                    nc.release_semaphore(one)

        STREAM = ["hi_done", "lo_done", "mm_done"]

        def load_chunk(sp, sems, raw, c, slot, src, kt):
            sp.wait_ge(sems["lo_done"], c + 1)
            sp.dma_start(raw[:, slot, 0:kt, :], src).then_inc(sems["raw_in"][slot], 16)

        def arrived(c, slot):
            return (c - slot) * (16 // RAW) + 16

        def split_hi(act, sems, w, c, slot, kt):
            act.wait_ge(sems["raw_in"][slot], arrived(c, slot))
            act.wait_ge(sems["mm_done"], c + 1)
            act.activation(w.hi[:, slot % SPLIT, 0:kt, :], w.raw[:, slot, 0:kt, :], ACT.Copy).then_inc(sems["hi_done"], 1)

        def split_lo(dve, sems, w, c, slot, kt):
            dve.wait_ge(sems["hi_done"], c + 1)
            dve.tensor_tensor(w.lo[:, slot % SPLIT, 0:kt, :], w.raw[:, slot, 0:kt, :], w.hi[:, slot % SPLIT, 0:kt, :],
                              ALU.subtract).then_inc(sems["lo_done"], 1)

        def multiply(pe, sems, w, c, slot, kt, bank, hi, lo, first=True, last=True, ready=None, n=SEQ):
            pe.wait_ge(sems["lo_done"], c + RAW + 1)
            for k in range(kt):
                if ready:
                    ready(k)
                wh, wl = w.hi[:, slot % SPLIT, k, :], w.lo[:, slot % SPLIT, k, :]
                pe.matmul(ps[:, bank, 0:n], wh, hi(k), start=(first and k == 0), stop=False)
                pe.matmul(ps[:, bank, 0:n], wh, lo(k), start=False, stop=False)
                mm = pe.matmul(ps[:, bank, 0:n], wl, hi(k), start=False, stop=(last and k == kt - 1))
            mm.then_inc(sems["mm_done"], 1)

        class Weights:
            def __init__(self, ctx, kt):
                self.raw = sb(ctx, "w_raw", [P, RAW, kt, P])
                self.hi = sb(ctx, "w_hi", [P, SPLIT, kt, P], F32R)
                self.lo = sb(ctx, "w_lo", [P, SPLIT, kt, P], F32R)

        def in_pairs(eng, n, split, consume, next_split=None, par0=0):
            loops = (n - 1) // 2
            with eng.Fori(0, loops) as i:
                for u in range(2):
                    split(2 * i + u + 1, (u + 1 + par0) % 2)
                    consume(2 * i + u, (u + par0) % 2)
            for q in range(2 * loops, n):
                if q + 1 < n:
                    split(q + 1, (q + 1 + par0) % 2)
                elif next_split:
                    next_split()
                consume(q, (q + par0) % 2)

        def by_pairs(eng, n, body, par0=0):
            with eng.Fori(0, n // 2) as i:
                for u in range(2):
                    body(2 * i + u, (u + par0) % 2)
            if n % 2:
                body(n - 1, (n - 1 + par0) % 2)

        def at(t, k):
            if isinstance(k, int):
                return t[:, k, :]
            return t[:, bass.ds(k, 1), :].rearrange("p a n -> p (a n)")

        def col(t, k):
            return t[:, k:k + 1] if isinstance(k, int) else t[:, bass.ds(k, 1)]

        def cols_of(w, layer, k0, kt, c0):
            v = w.rearrange("l (t p) n -> l p t n", p=P)
            return v[bass.ds(layer, 1), :, k0:k0 + kt, bass.ds(c0, P)].rearrange("a p t n -> (a p) t n")

        LN = ["y_done", "acc_done", "ln_pe", "centred", "squared", "rstd_act", "newton", "scaled", "affine",
              "x_hi", "x_lo"]

        def ln_acc(pool, sems, acc, seed=2):
            pool.memset(acc, 0.0).then_inc(sems["acc_done"], 1)
            with pool.Fori(0, DT) as j:
                pool.wait_ge(sems["y_done"], j + seed + 1)
                pool.wait_ge(sems["acc_done"], j + 1)
                pool.tensor_tensor(acc, acc, at(xT, j), ALU.add).then_inc(sems["acc_done"], 1)

        def ln_pe(pe, sems, acc, sq):
            pe.wait_ge(sems["acc_done"], DT + 1)
            pe.matmul(ps[:, 6, :], mean_w[:], acc, start=True, stop=True).then_inc(sems["ln_pe"], 1)
            for j in range(DT):
                pe.wait_ge(sems["squared"], j + 1)
                pe.matmul(ps[:, 7, :], mean_w[:], sq[j % 2], start=(j == 0), stop=(j == DT - 1)).then_inc(sems["ln_pe"], 1)

        def ln_act(act, sems, which, sq, r0, eps_col):
            for j in range(DT):
                act.wait_ge(sems["centred"], j + 1)
                if j >= 2:
                    act.wait_ge(sems["ln_pe"], j)
                act.activation(sq[j % 2], xT[:, j, :], ACT.Square).then_inc(sems["squared"], 1)
            act.wait_ge(sems["ln_pe"], DT + 1)
            act.activation(r0, ps[:, 7, :], ACT.Ln, bias=epsc[:, eps_col:eps_col + 1]).then_inc(sems["rstd_act"], 1)
            act.wait_ge(sems["rstd_act"], 1)
            act.activation(r0, r0, ACT.Exp, scale=-0.5).then_inc(sems["rstd_act"], 1)
            for j in range(DT):
                k = which * DT + j
                act.wait_ge(sems["scaled"], j + 1)
                act.activation(xT[:, j, :], xT[:, j, :], ACT.Identity, bias=lnb[:, k:k + 1],
                               scale=lng[:, k:k + 1]).then_inc(sems["affine"], 1)
                act.wait_ge(sems["affine"], j + 1)
                act.activation(xhi[:, j, :], xT[:, j, :], ACT.Copy).then_inc(sems["x_hi"], 1)

        def ln_dve(dve, sems, eps, r0, t):
            dve.wait_ge(sems["ln_pe"], 1)
            for j in range(DT):
                dve.tensor_tensor(xT[:, j, :], xT[:, j, :], ps[:, 6, :], ALU.subtract).then_inc(sems["centred"], 1)
            dve.wait_ge(sems["rstd_act"], 2)
            dve.scalar_tensor_tensor(out=t, in0=ps[:, 7, :], scalar=eps, in1=r0, op0=ALU.add,
                                     op1=ALU.mult).then_inc(sems["newton"], 1)
            dve.wait_ge(sems["newton"], 1)
            dve.tensor_tensor(t, t, r0, ALU.mult).then_inc(sems["newton"], 1)
            dve.wait_ge(sems["newton"], 2)
            dve.tensor_scalar(t, t, -0.5, 1.5, ALU.mult, ALU.add).then_inc(sems["newton"], 1)
            dve.wait_ge(sems["newton"], 3)
            dve.tensor_tensor(t, t, r0, ALU.mult).then_inc(sems["newton"], 1)
            dve.wait_ge(sems["newton"], 4)
            dve.wait_ge(sems["centred"], DT)
            for j in range(DT + 1):
                if j < DT:
                    dve.tensor_tensor(xT[:, j, :], xT[:, j, :], t, ALU.mult).then_inc(sems["scaled"], 1)
                if j >= 1:
                    x_low(dve, sems, j - 1)

        def x_low(dve, sems, j, before=0):
            dve.wait_ge(sems["x_hi"], before + j + 1)
            dve.tensor_tensor(xlo[:, j, :], xT[:, j, :], xhi[:, j, :], ALU.subtract).then_inc(sems["x_lo"], 1)

        with scope() as ctx:
            xin = sb(ctx, "xin", [P, QT, D_MODEL])
            rows = sb(ctx, "rows", [P, P])
            lbs = sb(ctx, "lbs", [P, 6, HGRN_HEADS])
            sems = semaphores(["loaded", "x_in", "made", "turned", "emptied", "x_hi", "x_lo", "par_in", "lbt", "lba"])

            with nc.Block() as block:
                @block.sync
                def _(sp):
                    sp.dma_start(ident[:], consts_d[:, C_ID:C_ID + P]).then_inc(sems["loaded"], 16)
                    for src, r0, n in ((ln_g.rearrange("l t (j q) -> (l t j) q", q=P), PG, 24 * DEPTH),
                                       (ln_b.rearrange("l t (j q) -> (l t j) q", q=P), PB, 24 * DEPTH),
                                       (ple_gate_b.rearrange("l (j q) -> (l j) q", q=P), PGB, 8 * DEPTH),
                                       (hgrn_norm_g.rearrange("l (j q) -> (l j) q", q=P), PNG, 4 * DEPTH),
                                       (hgrn_lb_raw.rearrange("l (j q) -> (l j) q", q=P), PLB, 4 * DEPTH)):
                        sp.dma_start(rows[r0:r0 + n, :], src).then_inc(sems["loaded"], 16)
                    sp.dma_start(sinks[:], swa_sinks.rearrange("l h -> (l h)").partition_broadcast(P)).then_inc(sems["loaded"], 16)
                    for t in range(QT):
                        sp.dma_start(xin[:, t, :], x[0, t * P:(t + 1) * P, :]).then_inc(sems["x_in"], 16)
                    sp.wait_ge(sems["loaded"], 16 * 7)

                @block.gpsimd
                def _(pool):
                    pool.memset(mean_w[:], 1.0 / D_MODEL)
                    pool.memset(epsc[:, 0:1], 4.0 * LN_EPS)
                    pool.memset(epsc[:, 1:2], LN_EPS)
                    pool.memset(hgp[:, 0, 1, :], 0.0).then_inc(sems["made"], 1)

                @block.tensor
                def _(pe):
                    pe.wait_ge(sems["loaded"], 16 * 7)
                    pe.transpose(ps[:, 7, 0:P], rows[:], ident[:]).then_inc(sems["par_in"], 1)
                    pe.wait_ge(sems["x_in"], 16 * QT)
                    for j in range(DT):
                        if j >= 4:
                            pe.wait_ge(sems["emptied"], j - 3)
                        for t in range(QT):
                            mm = pe.transpose(ps[:, j % 4, t * P:(t + 1) * P], xin[:, t, j * P:(j + 1) * P], ident[:])
                        mm.then_inc(sems["turned"], 1)

                @block.scalar
                def _(act):
                    for j in range(DT):
                        act.wait_ge(sems["emptied"], j + 1)
                        act.activation(xhi[:, j, :], xT[:, j, :], ACT.Copy).then_inc(sems["x_hi"], 1)
                    act.wait_ge(sems["lbt"], 3)
                    act.activation(lbs[:, 3, :], lbs[:, 1, :], ACT.Exp)
                    act.activation(lbs[:, 4, :], lbs[:, 2, :], ACT.Exp).then_inc(sems["lba"], 1)
                    act.wait_ge(sems["lbt"], 4)
                    act.activation(lbs[:, 5, :], lbs[:, 5, :], ACT.Ln).then_inc(sems["lba"], 1)

                @block.vector
                def _(dve):
                    dve.wait_ge(sems["par_in"], 1)
                    dve.tensor_copy(par[:], ps[:, 7, 0:P]).then_inc(sems["lbt"], 1)
                    dve.wait_ge(sems["lbt"], 1)
                    r0, r1 = par[:, PLB:PLB + 4], par[:, PLB + 4:PLB + 8]
                    dve.tensor_tensor(lbs[:, 0, :], r0, r1, ALU.max).then_inc(sems["lbt"], 1)
                    dve.wait_ge(sems["lbt"], 2)
                    dve.tensor_tensor(lbs[:, 1, :], r0, lbs[:, 0, :], ALU.subtract)
                    dve.tensor_tensor(lbs[:, 2, :], r1, lbs[:, 0, :], ALU.subtract).then_inc(sems["lbt"], 1)
                    for j in range(DT):
                        dve.wait_ge(sems["turned"], j + 1)
                        dve.tensor_copy(xT[:, j, :], ps[:, j % 4, :]).then_inc(sems["emptied"], 1)
                    for j in range(DT):
                        x_low(dve, sems, j)
                    dve.wait_ge(sems["lba"], 1)
                    dve.tensor_tensor(lbs[:, 5, :], lbs[:, 3, :], lbs[:, 4, :], ALU.add).then_inc(sems["lbt"], 1)
                    dve.wait_ge(sems["lba"], 2)
                    dve.tensor_tensor(hgp[:, 1, 1, :], lbs[:, 1, :], lbs[:, 5, :], ALU.subtract).then_inc(sems["lbt"], 1)
                    dve.tensor_tensor(hgp[:, 1, 0, :], lbs[:, 2, :], lbs[:, 5, :], ALU.subtract).then_inc(sems["lbt"], 1)
                    dve.wait_ge(sems["lbt"], 6)
                    dve.tensor_scalar(hgp[:, 1, 0, :], hgp[:, 1, 0, :], LN_FLOOR, None, ALU.max)
                    dve.memset(hgp[:, 0, 0, :], LN_FLOOR).then_inc(sems["lbt"], 1)
                    dve.wait_ge(sems["made"], 1)
                    dve.wait_ge(sems["lbt"], 7)
                    for l in range(DEPTH):
                        dve.tensor_tensor(hgp[:, l, 2, :], hgp[:, l, 1, :], hgp[:, l, 0, :], ALU.subtract)
            clear(sems)

        def ffn(layer, half):
            ple = half == 1
            which = 2 * half
            stage[0] = f"ffn{half + 1}"
            with scope() as ctx:
                w = Weights(ctx, KD)
                hhi = sb(ctx, "hhi", [P, FT, SEQ], F32R)
                hlo = sb(ctx, "hlo", [P, FT, SEQ], F32R)
                gate = sb(ctx, "gate", [P, 2, SEQ])
                prod = sb(ctx, "prod", [P, 2, SEQ])
                acc, r0 = gate[:, 0, :], gate[:, 1, :]
                sq = [prod[:, 0, :], prod[:, 1, :]]
                if ple:
                    phi = sb(ctx, "phi", [P, PT_, SEQ], F32R)
                    plo = sb(ctx, "plo", [P, PT_, SEQ], F32R)
                    pin = gate[:, :, :].rearrange("p a (b n) -> p (a b) n", n=PLE_DIM)
                sems = semaphores(STREAM + LN + ["gate_done", "h_done", "h_hi", "h_lo", "par_done", "p_in", "p_turned",
                                           "p_hi", "p_lo", "e_act", "e_mul", "e_done"], slots=[("raw_in", RAW)])
                C_DN, C_PLE = 2 * FT, 2 * FT + 2 * DT

                gu = ffn_w_gu.rearrange("l h k n -> (l h) k n")
                dn = ffn_w_down.rearrange("l h k n -> (l h) k n")
                which_w = layer * 2 + half

                with nc.Block() as block:
                    @block.sync
                    def _(sp):
                        if ple:
                            for t in range(QT):
                                src = p[bass.ds(layer, 1), 0, t * P:(t + 1) * P, :].rearrange("a q n -> (a q) n")
                                sp.dma_start(pin[:, t, :], src).then_inc(sems["p_in"], 16)

                        def up(q, par_):
                            for u in range(2):
                                load_chunk(sp, sems, w.raw, 2 * q + u, 2 * par_ + u,
                                           cols_of(gu, which_w, 0, DT, q * P + u * D_FF), DT)

                        def down(q, par_):
                            for u in range(2):
                                load_chunk(sp, sems, w.raw, C_DN + 2 * q + u, 2 * par_ + u,
                                           cols_of(dn, which_w, u * KD, KD, q * P), KD)

                        def embed(q, par_):
                            load_chunk(sp, sems, w.raw, C_PLE + 2 * q, 2 * par_,
                                       cols_of(ple_gate_w, layer, 0, DT, q * P), DT)
                            load_chunk(sp, sems, w.raw, C_PLE + 2 * q + 1, 2 * par_ + 1,
                                       cols_of(ple_w, layer, 0, PT_, q * P), PT_)
                        by_pairs(sp, FT, up)
                        by_pairs(sp, DT, down)
                        if ple:
                            by_pairs(sp, DT, embed)

                    def split_with(one, eng):
                        def up(q, par_):
                            for u in range(2):
                                one(eng, sems, w, 2 * q + u, 2 * par_ + u, DT)

                        def down(q, par_):
                            for u in range(2):
                                one(eng, sems, w, C_DN + 2 * q + u, 2 * par_ + u, KD)

                        def embed(q, par_):
                            one(eng, sems, w, C_PLE + 2 * q, 2 * par_, DT)
                            one(eng, sems, w, C_PLE + 2 * q + 1, 2 * par_ + 1, PT_)
                        return up, down, embed

                    @block.gpsimd
                    def _(pool):
                        pool.wait_ge(sems["h_lo"], FT)
                        ln_acc(pool, sems, acc)

                    @block.tensor
                    def _(pe):
                        pe.sem_inc(sems["mm_done"], SPLIT)
                        if ple:
                            pe.wait_ge(sems["p_in"], 16 * QT)
                            for k in range(PT_):
                                for t in range(QT):
                                    mm = pe.transpose(ps[:, 4 + k, t * P:(t + 1) * P], pin[:, t, k * P:(k + 1) * P], ident[:])
                                mm.then_inc(sems["p_turned"], 1)

                        def up(q, par_):
                            pe.wait_ge(sems["h_done"], q + 1)
                            for u in range(2):
                                multiply(pe, sems, w, 2 * q + u, 2 * par_ + u, DT, 2 * par_ + u,
                                         lambda k: xhi[:, k, :], lambda k: xlo[:, k, :])

                        def down(q, par_):
                            pe.wait_ge(sems["y_done"], q + 1)

                            def ready(k):
                                if k >= KD - 2:
                                    pe.wait_ge(sems["h_lo"], FT - (KD - 1 - k))
                            for u in range(2):
                                multiply(pe, sems, w, C_DN + 2 * q + u, 2 * par_ + u, KD, 4 + par_,
                                         lambda k: hhi[:, u * KD + k, :], lambda k: hlo[:, u * KD + k, :],
                                         first=(u == 0), last=(u == 1), ready=ready if u else None)

                        def embed(q, par_):
                            pe.wait_ge(sems["e_done"], q + 1)
                            multiply(pe, sems, w, C_PLE + 2 * q, 2 * par_, DT, 2 * par_,
                                     lambda k: xhi[:, k, :], lambda k: xlo[:, k, :])
                            multiply(pe, sems, w, C_PLE + 2 * q + 1, 2 * par_ + 1, PT_, 2 * par_ + 1,
                                     lambda k: phi[:, k, :], lambda k: plo[:, k, :])
                        by_pairs(pe, FT, up)
                        if ple:
                            pe.wait_ge(sems["p_lo"], PT_)
                        by_pairs(pe, DT, down)
                        ln_pe(pe, sems, acc, sq)
                        if ple:
                            pe.wait_ge(sems["x_lo"], DT)
                            by_pairs(pe, DT, embed)

                    @block.scalar
                    def _(act):
                        s_up, s_down, s_embed = split_with(split_hi, act)
                        if ple:
                            for k in range(PT_):
                                act.wait_ge(sems["p_turned"], k + 1)
                                act.activation(phi[:, k, :], ps[:, 4 + k, :], ACT.Copy).then_inc(sems["p_hi"], 1)
                        s_up(0, 0)

                        def gates(q, par_):
                            act.wait_ge(sems["mm_done"], 2 * q + SPLIT + 1)
                            act.wait_ge(sems["h_done"], q + 1)
                            act.activation(gate[:, par_, :], ps[:, 2 * par_, :], ACT.Silu).then_inc(sems["gate_done"], 1)
                            act.wait_ge(sems["h_done"], q + SPLIT + 1)
                            act.activation(at(hhi, q), prod[:, par_, :], ACT.Copy).then_inc(sems["h_hi"], 1)
                        if ple:
                            act.wait_ge(sems["p_lo"], PT_)
                        in_pairs(act, FT, s_up, gates, lambda: s_down(0, 0))
                        in_pairs(act, DT, s_down, lambda q, par_: None, (lambda: s_embed(0, 0)) if ple else None)
                        ln_act(act, sems, which, sq, r0, 0)

                        def sigm(q, par_):
                            act.wait_ge(sems["mm_done"], C_PLE + 2 * q + SPLIT + 1)
                            act.wait_ge(sems["e_done"], q + 1)
                            act.activation(gate[:, par_, :], ps[:, 2 * par_, :], ACT.Tanh, scale=0.5,
                                           bias=col(gbh, q)).then_inc(sems["e_act"], 1)
                        if ple:
                            act.wait_ge(sems["scaled"], DT)
                            in_pairs(act, DT, s_embed, sigm)
                            act.wait_ge(sems["e_done"], DT + SPLIT)
                            for j in range(DT):
                                act.activation(xhi[:, j, :], xT[:, j, :], ACT.Copy).then_inc(sems["x_hi"], 1)

                    @block.vector
                    def _(dve):
                        s_up, s_down, s_embed = split_with(split_lo, dve)
                        dve.sem_inc(sems["lo_done"], RAW)
                        dve.sem_inc(sems["h_done"], 2)
                        dve.sem_inc(sems["y_done"], 2)
                        dve.sem_inc(sems["e_done"], 2)
                        if not ple:
                            dve.tensor_copy(lng[:], par[:, bass.ds(layer * 24 + PG, 24)])
                            dve.tensor_copy(lnb[:], par[:, bass.ds(layer * 24 + PB, 24)])
                            dve.tensor_scalar(gbh[:], par[:, bass.ds(layer * 8 + PGB, 8)], 0.5, None,
                                              ALU.mult).then_inc(sems["par_done"], 1)
                        else:
                            for k in range(PT_):
                                dve.wait_ge(sems["p_hi"], k + 1)
                                dve.tensor_tensor(plo[:, k, :], ps[:, 4 + k, :], phi[:, k, :],
                                                  ALU.subtract).then_inc(sems["p_lo"], 1)
                        s_up(0, 0)

                        def hidden(q, par_):
                            dve.wait_ge(sems["gate_done"], q + 1)
                            dve.wait_ge(sems["mm_done"], 2 * q + SPLIT + 2)
                            dve.tensor_tensor(prod[:, par_, :], gate[:, par_, :], ps[:, 2 * par_ + 1, :],
                                              ALU.mult).then_inc(sems["h_done"], 1)
                            dve.wait_ge(sems["h_hi"], q + 1)
                            dve.tensor_tensor(at(hlo, q), prod[:, par_, :], at(hhi, q),
                                              ALU.subtract).then_inc(sems["h_lo"], 1)

                        def residual(q, par_):
                            dve.wait_ge(sems["mm_done"], C_DN + 2 * q + SPLIT + 2)
                            dve.scalar_tensor_tensor(out=at(xT, q), in0=at(xT, q), scalar=2.0 * ALPHA,
                                                     in1=ps[:, 4 + par_, :], op0=ALU.mult,
                                                     op1=ALU.add).then_inc(sems["y_done"], 1)
                        in_pairs(dve, FT, s_up, hidden, lambda: s_down(0, 0))
                        in_pairs(dve, DT, s_down, residual, (lambda: s_embed(0, 0)) if ple else None)
                        ln_dve(dve, sems, 4.0 * LN_EPS, r0, acc)

                        def embed(q, par_):
                            dve.wait_ge(sems["e_act"], q + 1)
                            dve.wait_ge(sems["mm_done"], C_PLE + 2 * q + SPLIT + 2)
                            dve.scalar_tensor_tensor(out=prod[:, par_, :], in0=gate[:, par_, :], scalar=1.0,
                                                     in1=ps[:, 2 * par_ + 1, :], op0=ALU.add,
                                                     op1=ALU.mult).then_inc(sems["e_mul"], 1)
                            dve.wait_ge(sems["e_mul"], q + 1)
                            dve.scalar_tensor_tensor(out=at(xT, q), in0=prod[:, par_, :], scalar=0.5,
                                                     in1=at(xT, q), op0=ALU.mult, op1=ALU.add).then_inc(sems["e_done"], 1)
                        if ple:
                            in_pairs(dve, DT, s_embed, embed)
                            for j in range(DT):
                                x_low(dve, sems, j, before=DT)
                clear(sems)

        def attention(layer, proj):
            stage[0] = "attn"
            NSA_N, UNITS = NSA_HEADS * QT, (NSA_HEADS + SWA_HEADS) * QT
            with scope() as ctx:
                w = Weights(ctx, DT)
                cst = sb(ctx, "masks", [P, C_HG])
                rope = sb(ctx, "rope", [P, 2, SEQ])
                roped = sb(ctx, "roped", [P, 6, SEQ])
                v_tok = sb(ctx, "v_tok", [P, 2, QT, HEAD_DIM])
                v_swa = sb(ctx, "v_swa", [P, QT, P])
                gates = sb(ctx, "gates", [P, QT, 3 * NSA_HEADS])
                anyv = sb(ctx, "anyv", [P, 1])
                prob = sb(ctx, "prob", [P, 2, 2, SEQ])
                prob_t = sb(ctx, "prob_t", [P, 2, 2, SEQ])
                blk_hi = sb(ctx, "blk_hi", [P, 2, 16, 32], F32R)
                blk_lo = sb(ctx, "blk_lo", [P, 2, 16, 32], F32R)
                pos2 = sb(ctx, "pos2", [CMP_LEN, P])
                pos_t = sb(ctx, "pos_t", [P, CMP_LEN])
                hid = sb(ctx, "hid", [P, 4, 32])
                w2k = sb(ctx, "w2k", [P, 2, P])
                w2v = sb(ctx, "w2v", [P, 2, HEAD_DIM])
                kc = sb(ctx, "kc", [P, 32])
                vc = sb(ctx, "vc", [N_CMP, HEAD_DIM])
                p_cmp = sb(ctx, "p_cmp", [P, NSA_N, N_CMP])
                pt_cmp = sb(ctx, "pt_cmp", [N_CMP, NSA_N, P])
                st_cmp = sb(ctx, "st_cmp", [P, 3, NSA_N])
                mx = sb(ctx, "mx", [P, 2, 2])
                nb = sb(ctx, "nb", [P, 2, 2])
                sums = sb(ctx, "sums", [P, 2, 2])
                rec = sb(ctx, "rec", [P, 2, 2])
                e_sink = sb(ctx, "e_sink", [P, 2])
                blk = prob[:, 0, :, :].rearrange("p a (l n) -> p a l n", n=32)
                sin_part = prob_t[:, 0, :, :]
                sems = semaphores(STREAM + ["even_out", "odd_out", "aux_in", "pos_turned", "pos_out", "blk_done", "blk_hi",
                                      "blk_lo", "hid_done", "rope_mm", "rope_cos", "rope_out", "rope_step", "v_turned",
                                      "v_out", "gate_out", "kc_mm", "kc_out", "vc_out", "sc_ready", "sc_step",
                                      "sc_sub", "sc_exp", "pc_done", "pct_ready", "pct_act", "pct_dve", "s_ready",
                                      "nb_ready", "exp_done", "step", "act_step", "p_norm", "pt_ready", "ev_act",
                                      "ev_dve", "pv_done", "o_hi", "o_lo"], slots=[("raw_in", RAW)])
                PAIRS, C_W1 = N_PM // 2, N_PM
                win = w_in

                def c_mat(c):
                    return cst[:, c:c + P]

                def proj_pairs(eng, split, consume):
                    for q in range(3):
                        if split:
                            split(q + 1, (q + 1) % 2)
                        consume(q, q % 2, False)
                    with eng.Fori(0, 4) as i:
                        for u in range(2):
                            if split:
                                split(2 * i + 4 + u, u)
                            consume(2 * i + 3 + u, 1 - u, False)
                    for q in (11, 12):
                        if split and q + 1 < PAIRS:
                            split(q + 1, (q + 1) % 2)
                        consume(q, q % 2, True)

                def w_cols(tile):
                    return tile * P if isinstance(tile, int) and tile < T_SQ else NSA_COLS + (tile - T_SQ) * P

                units = [(True, 2 * hp + hh, i, 0) for hp in range(2) for i in range(QT) for hh in range(2)]
                units += [(False, 2 * hp + hh, i, max(i - 1, 0)) for hp in range(2) for i in range(QT) for hh in range(2)]
                ev_a, ev_d, na, nd = [], [], 0, 0
                for n, (nsa, *_r) in enumerate(units):
                    na, nd = na + (nsa or n % 2 == 0), nd + (nsa or n % 2 == 1)
                    ev_a.append(na)
                    ev_d.append(nd)

                def halves(h):
                    return slice(64 * (h % 2), 64 * (h % 2) + 64)

                def rope_dst(r):
                    return proj[:, ROPE[r][1], :] if r in (4, 5) else roped[:, r if r < 4 else r - 2, :]

                with nc.Block() as block:
                    @block.sync
                    def _(sp):
                        def aux(dst, src):
                            sp.dma_start(dst, src).then_inc(sems["aux_in"], 16)

                        def tiles(q, par_, _gate=False):
                            for u in range(2):
                                t = 2 * q + u
                                src = win.rearrange("l (t p) n -> l p t n", p=P)[bass.ds(layer, 1), :, :, bass.ds(w_cols(t), P)]
                                load_chunk(sp, sems, w.raw, t, (2 * par_ + u) % RAW, src.rearrange("a p t n -> (a p) t n"), DT)
                        tiles(0, 0)
                        one = bass.ds(layer, 1)
                        aux(pos2[:, 0:64], cmp_pos[one, :, :].rearrange("a l d -> (a l) d"))
                        aux(pos2[:, 64:128], cmp_pos[one, :, :].rearrange("a l d -> (a l) d"))
                        aux(cst[:], consts_d[:, 0:C_HG])
                        aux(rope[:], rope_d.rearrange("p (a n) -> p a n", a=2))
                        w2 = cmp_k_w2.rearrange("l (t p) n -> l p t n", p=P)[one, :, :, :].rearrange("a p t n -> (a p) t n")
                        aux(w2k[:, :, 0:64], w2)
                        aux(w2k[:, :, 64:128], w2)
                        aux(w2v[:], cmp_v_w2.rearrange("l (t p) n -> l p t n", p=P)[one, :, :, :].rearrange("a p t n -> (a p) t n"))
                        for q in (1, 2):
                            tiles(q, q % 2)
                        with sp.Fori(0, 4) as i:
                            for u in range(2):
                                tiles(2 * i + 3 + u, 1 - u)
                        for q in (11, 12):
                            tiles(q, q % 2)
                        for q in range(4):
                            for u in range(2):
                                c = C_W1 + 2 * q + u
                                load_chunk(sp, sems, w.raw, c, c % RAW,
                                           cols_of((cmp_k_w1, cmp_v_w1)[q // 2], layer, u * DT, DT, (q % 2) * P), DT)

                    def splits(one, eng):
                        def go(q, par_):
                            for u in range(2):
                                one(eng, sems, w, 2 * q + u, 2 * par_ + u, DT)
                        return go

                    @block.tensor
                    def _(pe):
                        pe.sem_inc(sems["mm_done"], SPLIT)

                        def project(q, par_, _gate):
                            pe.wait_ge(sems["even_out"], q + 1)
                            pe.wait_ge(sems["odd_out"], q + 1)
                            for u in range(2):
                                multiply(pe, sems, w, 2 * q + u, 2 * par_ + u, DT, 2 * par_ + u,
                                         lambda k: xhi[:, k, :], lambda k: xlo[:, k, :])
                        for q in range(3):
                            project(q, q % 2, False)
                        pe.wait_ge(sems["aux_in"], 16 * 7)
                        pe.transpose(ps[:, 4, 0:CMP_LEN], pos2[:], ident[0:CMP_LEN, 0:CMP_LEN]).then_inc(sems["pos_turned"], 1)
                        with pe.Fori(0, 4) as i:
                            for u in range(2):
                                project(2 * i + 3 + u, 1 - u, False)
                        for q in (11, 12):
                            project(q, q % 2, True)

                        pe.wait_ge(sems["even_out"], PAIRS + 2)
                        pe.wait_ge(sems["odd_out"], PAIRS + 2)
                        pe.wait_ge(sems["blk_lo"], 2)
                        for q in range(4):
                            for u in range(2):
                                c = C_W1 + 2 * q + u
                                multiply(pe, sems, w, c, c % RAW, DT, q,
                                         lambda k: blk_hi[:, q // 2, u * DT + k, :], lambda k: blk_lo[:, q // 2, u * DT + k, :],
                                         first=(u == 0), last=(u == 1), n=32)

                        pe.wait_ge(sems["pos_out"], 1)
                        for r in range(8):
                            pe.wait_ge(sems["rope_out"], r + 1)
                            a, b = 4 + 2 * (r % 2), 5 + 2 * (r % 2)
                            kind, src, half = ROPE[r]
                            if kind == "q":
                                pe.matmul(ps[:, a, :], c_mat(C_ROT), proj[:, src, :], start=True, stop=True).then_inc(sems["rope_mm"], 1)
                            else:
                                rows_ = slice(half, half + 64)
                                pe.matmul(ps[:, a, :], cst[rows_, C_ROTDUP:C_ROTDUP + P], proj[rows_, src, :], start=True, stop=True)
                                pe.matmul(ps[:, b, :], cst[rows_, C_DUP:C_DUP + P], proj[rows_, src, :], start=True,
                                          stop=True).then_inc(sems["rope_mm"], 1)

                        pe.wait_ge(sems["hid_done"], 4)
                        pe.wait_ge(sems["rope_out"], 8 + 2)
                        for m in range(2):
                            mm = pe.matmul(ps[:, 4, 0:32], w2k[:, m, :], hid[:, m, :], start=(m == 0), stop=(m == 1))
                        mm.then_inc(sems["kc_mm"], 1)
                        for m in range(2):
                            mm = pe.matmul(ps[0:N_CMP, 5, 0:HEAD_DIM], hid[:, 2 + m, 0:N_CMP], w2v[:, m, :], start=(m == 0), stop=(m == 1))
                        mm.then_inc(sems["kc_mm"], 1)

                        for n, t in enumerate((T_SLC, T_WIN, T_SV, T_GATE)):
                            for c in range(QT):
                                mm = pe.transpose(ps[:, n, c * P:(c + 1) * P], proj[:, t, c * P:(c + 1) * P], ident[:])
                            mm.then_inc(sems["v_turned"], 1)

                        pe.wait_ge(sems["kc_out"], 1)
                        for n in range(NSA_N):
                            h, i = 2 * (n % 8 // QT) + n // 8, n % QT
                            o = ps[:, 6 + h % 2, n % 8 * N_CMP:(n % 8 + 1) * N_CMP]
                            pe.matmul(o, proj[halves(h), T_Q + h // 2, i * P:(i + 1) * P], kc[halves(h), 0:N_CMP], start=True, stop=False)
                            mm = pe.matmul(o, ident[:], cst[:, C_CMP + i * N_CMP:C_CMP + (i + 1) * N_CMP], start=False, stop=True)
                        mm.then_inc(sems["sc_ready"], 1)
                        pe.wait_ge(sems["vc_out"], 1)
                        pe.wait_ge(sems["pc_done"], 1)
                        for n in range(NSA_N):
                            mm = pe.transpose(ps[0:N_CMP, 4 + n // 4, (n % 4) * P:(n % 4 + 1) * P], p_cmp[:, n, :], ident[:])
                            if n % 4 == 3:
                                mm.then_inc(sems["pct_ready"], 1)
                        pe.wait_ge(sems["v_out"], 3)
                        pe.wait_ge(sems["gate_out"], 1)

                        def scores(n):
                            nsa, h, i, k0 = units[n]
                            pe.wait_ge(sems["exp_done"], n + 1)
                            a = 2 * (n % 2)
                            qs = (roped[halves(h), h // 2, i * P:(i + 1) * P] if nsa
                                  else proj[halves(h), T_SQ + h // 2, i * P:(i + 1) * P])
                            for br in range(2 if nsa else 1):
                                ks = 2 + br if nsa else 4 + h // 2
                                w_ = (i + 1 - k0) * P
                                pe.matmul(ps[:, a + br, 0:w_], qs, roped[halves(h), ks, k0 * P:(i + 1) * P], start=True, stop=False)
                                if not nsa and i > 0:
                                    pe.matmul(ps[:, a, 0:P], ident[:], c_mat(C_BAND), start=False, stop=False)
                                mm = pe.matmul(ps[:, a + br, w_ - P:w_], ident[:], c_mat(C_CAUSAL), start=False, stop=True)
                            mm.then_inc(sems["s_ready"], 1)

                        def turn(n):
                            nsa, h, i, k0 = units[n]
                            pe.wait_ge(sems["p_norm"], n + 1)
                            if n == 0:
                                pe.wait_ge(sems["pct_act"], 2)
                                pe.wait_ge(sems["pct_dve"], 2)
                            else:
                                pe.wait_ge(sems["ev_act"], ev_a[n - 1] if nsa or n == NSA_N else ev_a[n - 2])
                                pe.wait_ge(sems["ev_dve"], ev_d[n - 1] if nsa or n == NSA_N else ev_d[n - 2])
                            for br in range(2 if nsa else 1):
                                b = 4 + (br if nsa else n % 2)
                                for c in range(i + 1 - k0):
                                    mm = pe.transpose(ps[:, b, c * P:(c + 1) * P], prob[:, n % 2, br, c * P:(c + 1) * P], ident[:])
                            mm.then_inc(sems["pt_ready"], 1)

                        def values(n):
                            nsa, h, i, k0 = units[n]
                            pe.wait_ge(sems["ev_act"], ev_a[n])
                            if ev_d[n]:
                                pe.wait_ge(sems["ev_dve"], ev_d[n])
                            if n % 8 == 0 and n >= NSA_N:
                                pe.wait_ge(sems["o_lo"], n // 8 - 1)
                            o = ps[halves(h), 6 + n // 8 % 2, i * P:(i + 1) * P]
                            todo = [(v_tok[:, br, c, :] if nsa else v_swa[:, k0 + c, (h // 2) * 64:(h // 2) * 64 + 64],
                                     prob_t[:, n % 2, br, c * P:(c + 1) * P])
                                    for br in range(2 if nsa else 1) for c in range(i + 1 - k0)]
                            if nsa:
                                todo.append((vc[:], pt_cmp[:, (h % 2) * 8 + (h // 2) * QT + i, :]))
                            for k, (v, pr) in enumerate(todo):
                                mm = pe.matmul(o, v, pr, start=(k == 0), stop=(k == len(todo) - 1))
                            mm.then_inc(sems["pv_done"], 1)

                        scores(0)
                        for n in range(UNITS + 2):
                            if n + 1 < UNITS:
                                scores(n + 1)
                            if n >= 2:
                                values(n - 2)
                            if 1 <= n <= UNITS:
                                turn(n - 1)

                    def out_hi(act, g):
                        act.wait_ge(sems["pv_done"], 8 * g + 8)
                        act.activation(xhi[:, g, :], ps[:, 6 + g % 2, :], ACT.Copy).then_inc(sems["o_hi"], 1)

                    @block.scalar
                    def _(act):
                        split = splits(split_hi, act)
                        act.sem_inc(sems["even_out"], 2)
                        act.sem_inc(sems["exp_done"], 2)

                        def out_even(q, par_, gate):
                            act.wait_ge(sems["mm_done"], 2 * q + SPLIT + 1)
                            act.activation(at(proj, 2 * q), ps[:, 2 * par_, :], ACT.Silu if gate else ACT.Copy).then_inc(sems["even_out"], 1)
                            if gate:
                                act.wait_ge(sems["mm_done"], 2 * q + SPLIT + 2)
                                act.activation(at(proj, 2 * q + 1), ps[:, 2 * par_ + 1, :], ACT.Silu).then_inc(sems["odd_out"], 1)
                        split(0, 0)
                        proj_pairs(act, split, out_even)
                        for kv in range(2):
                            act.wait_ge(sems["blk_done"], 2)
                            act.activation(blk_hi[:, kv], blk[:, kv], ACT.Copy).then_inc(sems["blk_hi"], 1)
                        for q in range(4):
                            split(PAIRS + q, (PAIRS + q) % 2)
                        for q in range(4):
                            act.wait_ge(sems["mm_done"], C_W1 + 2 * q + SPLIT + 2)
                            act.activation(hid[:, q, :], ps[:, q, 0:32], ACT.Silu).then_inc(sems["hid_done"], 1)
                        act.wait_ge(sems["kc_mm"], 1)
                        act.activation(kc[:], ps[:, 4, 0:32], ACT.Copy).then_inc(sems["kc_out"], 1)
                        for n in range(2):
                            act.wait_ge(sems["v_turned"], n + 1)
                            src = ps[:, n, :].rearrange("p (c d) -> p c d", d=P)[:, :, 64:128]
                            act.activation(v_tok[:, n], src, ACT.Copy).then_inc(sems["v_out"], 1)
                        act.wait_ge(sems["v_turned"], 3)
                        act.activation(v_swa[:, :, :].rearrange("p c d -> p (c d)"), ps[:, 2, :], ACT.Copy).then_inc(sems["v_out"], 1)
                        act.wait_ge(sems["v_turned"], 4)
                        src = ps[:, 3, :].rearrange("p (c d) -> p c d", d=P)[:, :, 0:3 * NSA_HEADS]
                        act.activation(gates[:], src, ACT.Tanh, scale=0.5).then_inc(sems["gate_out"], 1)
                        act.wait_ge(sems["sc_sub"], 2)
                        act.activation(p_cmp[:], p_cmp[:], ACT.Exp, scale=SCALE).then_inc(sems["sc_exp"], 1)
                        for b in (0, 2):
                            act.wait_ge(sems["pct_ready"], b + 1)
                            act.activation(pt_cmp[:, 4 * b:4 * b + 4, :].rearrange("p a n -> p (a n)"), ps[0:N_CMP, 4 + b, :],
                                           ACT.Copy).then_inc(sems["pct_act"], 1)

                        steps = 0
                        for n in range(UNITS + 2):
                            if n < UNITS:
                                nsa, h, i, k0 = units[n]
                                w_ = (i + 1 - k0) * P
                                act.wait_ge(sems["nb_ready"], n + 1)
                                if n >= 2:
                                    act.wait_ge(sems["pt_ready"], n - 1)
                                if not nsa:
                                    steps += 1
                                    act.activation(e_sink[:, n % 2:n % 2 + 1], sinks[:, bass.ds(layer * SWA_HEADS + h, 1)], ACT.Exp,
                                                   bias=nb[:, n % 2, 0:1]).then_inc(sems["act_step"], 1)
                                for br in range(2 if nsa else 1):
                                    e = act.activation(prob[:, n % 2, br, 0:w_], ps[:, 2 * (n % 2) + br, 0:w_], ACT.Exp, scale=SCALE,
                                                       bias=nb[:, n % 2, br:br + 1], accum_out=sums[:, n % 2, br:br + 1])
                                e.then_inc(sems["exp_done"], 1)
                            if n >= 2 and (units[n - 2][0] or n % 2 == 0):
                                m = n - 2
                                nsa, h, i, k0 = units[m]
                                w_ = (i + 1 - k0) * P
                                act.wait_ge(sems["pt_ready"], m + 1)
                                if m >= 2:
                                    act.wait_ge(sems["pv_done"], m - 1)
                                act.activation(prob_t[:, m % 2, 0, 0:w_], ps[:, 4 + (0 if nsa else m % 2), 0:w_], ACT.Copy).then_inc(sems["ev_act"], 1)
                            if n >= 3 and (n - 3) % 8 == 7:
                                out_hi(act, (n - 3) // 8)
                        out_hi(act, UNITS // 8 - 1)

                    @block.vector
                    def _(dve):
                        split = splits(split_lo, dve)
                        dve.sem_inc(sems["lo_done"], RAW)
                        dve.sem_inc(sems["odd_out"], 2)
                        dve.sem_inc(sems["rope_out"], 2)
                        dve.memset(blk[:], 0.0).then_inc(sems["step"], 1)

                        def out_odd(q, par_, gate):
                            if not gate:
                                dve.wait_ge(sems["mm_done"], 2 * q + SPLIT + 2)
                                dve.tensor_copy(at(proj, 2 * q + 1), ps[:, 2 * par_ + 1, :]).then_inc(sems["odd_out"], 1)
                        split(0, 0)
                        proj_pairs(dve, split, out_odd)

                        dve.wait_ge(sems["pos_turned"], 1)
                        dve.tensor_copy(pos_t[:], ps[:, 4, 0:CMP_LEN]).then_inc(sems["pos_out"], 1)
                        dve.wait_ge(sems["pos_out"], 1)
                        dve.wait_ge(sems["step"], 1)
                        for kv in range(2):
                            for s in range(2):
                                rows_ = slice(64 * kv, 64 * kv + 64)
                                full = proj[rows_, T_CMP, :]
                                for hi_l in range(2):
                                    src = (full[:, 16 * hi_l:16 * hi_l + 16 * N_CMP].rearrange("p (n l s) -> p s l n", l=8, s=2)[:, s])
                                    pos = pos_t[rows_, 16 * hi_l:16 * hi_l + 16].rearrange("p (l s) -> p s l", s=2)[:, s]
                                    d = dve.tensor_tensor(blk[64 * s:64 * s + 64, kv, 8 * hi_l:8 * hi_l + 8, 0:N_CMP], src,
                                                          pos[:, :, None].broadcast_to([64, 8, N_CMP]), ALU.add)
                            d.then_inc(sems["blk_done"], 1)
                        for kv in range(2):
                            dve.wait_ge(sems["blk_hi"], kv + 1)
                            dve.tensor_tensor(blk_lo[:, kv], blk[:, kv], blk_hi[:, kv], ALU.subtract).then_inc(sems["blk_lo"], 1)
                        for q in range(4):
                            split(PAIRS + q, (PAIRS + q) % 2)

                        cos, sin = rope[:, 0, :], rope[:, 1, :]
                        for r in range(8):
                            kind, src, half = ROPE[r]
                            a, b = 4 + 2 * (r % 2), 5 + 2 * (r % 2)
                            dst = rope_dst(r)
                            dve.wait_ge(sems["rope_mm"], r + 1)
                            if kind == "q":
                                dve.tensor_tensor(sin_part[:, r % 2, :], ps[:, a, :], sin, ALU.mult).then_inc(sems["rope_step"], 1)
                                dve.wait_ge(sems["rope_cos"], rope_pool[r])
                            else:
                                dve.tensor_tensor(dst, ps[:, b, :], cos, ALU.mult)
                                dve.tensor_tensor(sin_part[:, r % 2, :], ps[:, a, :], sin, ALU.mult).then_inc(sems["rope_step"], 1)
                            dve.wait_ge(sems["rope_step"], r + 1)
                            dve.tensor_tensor(dst, dst, sin_part[:, r % 2, :], ALU.add).then_inc(sems["rope_out"], 1)

                        dve.wait_ge(sems["kc_mm"], 2)
                        dve.tensor_copy(vc[:], ps[0:N_CMP, 5, 0:HEAD_DIM]).then_inc(sems["vc_out"], 1)
                        st = [1]

                        def then(ins):
                            ins.then_inc(sems["step"], 1)
                            st[0] += 1
                            dve.wait_ge(sems["step"], st[0])
                        dve.wait_ge(sems["gate_out"], 1)
                        then(dve.tensor_scalar(gates[:], gates[:], 0.5, 0.5, ALU.mult, ALU.add))
                        then(dve.tensor_scalar(anyv[:], cst[:, C_CMP:C_CMP + 1], -1.0, None, ALU.is_ge))
                        g0 = gates[:, 0, :].rearrange("p (h b) -> p b h", b=3)[:, 0]
                        then(dve.tensor_scalar(g0, g0, anyv[:, 0:1], None, ALU.mult))
                        dve.wait_ge(sems["sc_ready"], 1)
                        wide = [P, 8, N_CMP]
                        for b in range(2):
                            sc = ps[:, 6 + b, 0:8 * N_CMP].rearrange("p (u n) -> p u n", n=N_CMP)
                            m8 = st_cmp[:, 0, 8 * b:8 * b + 8]
                            then(dve.tensor_reduce(m8, sc, AX.X, ALU.max))
                            dve.tensor_tensor(p_cmp[:, 8 * b:8 * b + 8, :], sc, m8[:, :, None].broadcast_to(wide),
                                              ALU.subtract).then_inc(sems["sc_sub"], 1)
                        dve.wait_ge(sems["sc_exp"], 1)
                        then(dve.tensor_reduce(st_cmp[:, 1, :], p_cmp[:], AX.X, ALU.add))
                        then(dve.reciprocal(st_cmp[:, 2, :], st_cmp[:, 1, :]))
                        for b in range(2):
                            gc = gates[:, :, :].rearrange("p i (g s b) -> p s b g i", s=2, b=3)[:, b, 0]
                            rc = st_cmp[:, 2, 8 * b:8 * b + 8].rearrange("p (g i) -> p g i", i=QT)
                            then(dve.tensor_tensor(rc, rc, gc, ALU.mult))
                        dve.tensor_tensor(p_cmp[:], p_cmp[:], st_cmp[:, 2, :, None].broadcast_to([P, NSA_N, N_CMP]),
                                          ALU.mult).then_inc(sems["pc_done"], 1)
                        for b in (1, 3):
                            dve.wait_ge(sems["pct_ready"], b + 1)
                            dve.tensor_copy(pt_cmp[:, 4 * b:4 * b + 4, :].rearrange("p a n -> p (a n)"), ps[0:N_CMP, 4 + b, :]).then_inc(sems["pct_dve"], 1)

                        def row_max(n):
                            nsa, h, i, k0 = units[n]
                            w_ = (i + 1 - k0) * P
                            br = 2 if nsa else 1
                            dve.wait_ge(sems["s_ready"], n + 1)
                            then(dve.tensor_reduce(mx[:, n % 2, 0:br], ps[:, 2 * (n % 2):2 * (n % 2) + br, 0:w_], AX.X, ALU.max))
                            if nsa:
                                dve.tensor_scalar(nb[:, n % 2, 0:br], mx[:, n % 2, 0:br], -SCALE, None, ALU.mult).then_inc(sems["nb_ready"], 1)
                            else:
                                then(dve.tensor_scalar(mx[:, n % 2, 0:1], mx[:, n % 2, 0:1], SCALE,
                                                       sinks[:, bass.ds(layer * SWA_HEADS + h, 1)], ALU.mult, ALU.max))
                                dve.tensor_scalar(nb[:, n % 2, 0:1], mx[:, n % 2, 0:1], -1.0, None, ALU.mult).then_inc(sems["nb_ready"], 1)

                        def normalise(n):
                            nsa, h, i, k0 = units[n]
                            w_ = (i + 1 - k0) * P
                            br = 2 if nsa else 1
                            dve.wait_ge(sems["exp_done"], n + 3)
                            if not nsa:
                                then(dve.tensor_tensor(sums[:, n % 2, 0:1], sums[:, n % 2, 0:1], e_sink[:, n % 2:n % 2 + 1], ALU.add))
                            then(dve.reciprocal(rec[:, n % 2, 0:br], sums[:, n % 2, 0:br]))
                            if nsa:
                                then(dve.tensor_tensor(rec[:, n % 2, :], rec[:, n % 2, :], gates[:, i, 3 * h + 1:3 * h + 3], ALU.mult))
                            for b in range(br):
                                d = dve.tensor_scalar(prob[:, n % 2, b, 0:w_], prob[:, n % 2, b, 0:w_], rec[:, n % 2, b:b + 1], None, ALU.mult)
                            d.then_inc(sems["p_norm"], 1)

                        def out_lo(g):
                            dve.wait_ge(sems["o_hi"], g + 1)
                            dve.tensor_tensor(xlo[:, g, :], ps[:, 6 + g % 2, :], xhi[:, g, :], ALU.subtract).then_inc(sems["o_lo"], 1)

                        for n in range(UNITS + 2):
                            if n < UNITS:
                                row_max(n)
                            if n >= 2 and (units[n - 2][0] or (n - 2) % 2 == 1):
                                m = n - 2
                                nsa, h, i, k0 = units[m]
                                w_ = (i + 1 - k0) * P
                                dve.wait_ge(sems["pt_ready"], m + 1)
                                if m >= 2:
                                    dve.wait_ge(sems["pv_done"], m - 1)
                                dve.tensor_copy(prob_t[:, m % 2, 1 if nsa else 0, 0:w_], ps[:, 5, 0:w_]).then_inc(sems["ev_dve"], 1)
                            if 1 <= n <= UNITS:
                                normalise(n - 1)
                            if n >= 3 and (n - 3) % 8 == 7:
                                out_lo((n - 3) // 8)
                        out_lo(UNITS // 8 - 1)

                    @block.gpsimd
                    def _(pool):
                        for r in range(8):
                            kind, src, half = ROPE[r]
                            if kind == "q":
                                pool.wait_ge(sems["rope_mm"], r + 1)
                                pool.tensor_tensor(rope_dst(r), proj[:, src, :], rope[:, 0, :], ALU.mult).then_inc(sems["rope_cos"], 1)
                clear(sems)

        def hgrn2(layer, proj):
            stage[0] = "hgrn"
            H = HGRN_HEADS
            with scope() as ctx:
                hmask = sb(ctx, "hmask", [P, (LEVELS + 1) * P])
                reset = sb(ctx, "reset", [P, SEQ])
                lsp = sb(ctx, "lsp", [P, SEQ])
                lsg = sb(ctx, "lsg", [P, SEQ])
                karg = sb(ctx, "karg", [P, SEQ])
                logf = sb(ctx, "logf", [P, SEQ])
                cum = sb(ctx, "cum", [P, 2, SEQ])
                lev = sb(ctx, "lev", [P, 2, LEVELS, SEQ])
                ebs = sb(ctx, "ebs", [P, 2, SEQ])
                qd = sb(ctx, "qd", [P, 2, SEQ])
                kd = sb(ctx, "kd", [P, 2, SEQ])
                v_tok = sb(ctx, "v_tok", [P, 2, QT, P])
                att = sb(ctx, "att", [P, 2, (LEVELS + 1) * P])
                kd_t = sb(ctx, "kd_t", [P, 2, P])
                state = sb(ctx, "state", [P, 2, P])
                osq = sb(ctx, "osq", [P, SEQ])
                var = sb(ctx, "var", [P, SEQ])
                rms = sb(ctx, "rms", [P, SEQ])
                tmp = sb(ctx, "tmp", [P, SEQ])
                ngc = sb(ctx, "ngc", [P, HGRN_HEADS])
                hgc = sb(ctx, "hgc", [P, 3, HGRN_HEADS])
                sems = semaphores(["aux_in", "reset_done", "step", "act_step", "pool_step", "a0", "d0", "a1", "d1", "d2", "p2", "a2",
                             "d3", "p3", "c_mm", "att_done", "b4_mm", "b4_out", "st_mm", "st_out", "pv_done",
                             "sq_done", "ms_mm", "ms_out", "rs_act", "o_done", "o_hi", "o_lo"])

                def pairs(t, lv, side):
                    m = 1 << lv
                    return t.rearrange("p (b s m) -> p s b m", s=2, m=m)[:, side]

                def last_of(t, lv):
                    m = 1 << lv
                    v = t.rearrange("p (b s m) -> p s b m", s=2, m=m)[:, 0, :, m - 1:m]
                    return v.broadcast_to([P, SEQ // (2 * m), m])

                def b4_before_v(h):
                    return 4 * h

                def b4_before_k(h, c):
                    return 4 * h + 1 + c

                with nc.Block() as block:
                    @block.sync
                    def _(sp):
                        sp.dma_start(hmask[:], consts_d[:, C_HG:C_END]).then_inc(sems["aux_in"], 16)
                        sp.wait_ge(sems["aux_in"], 16)

                    @block.tensor
                    def _(pe):
                        def values_turned(h):
                            if b4_before_v(h):
                                pe.wait_ge(sems["b4_out"], b4_before_v(h))
                            for c in range(QT):
                                mm = pe.transpose(ps[:, 4, c * P:(c + 1) * P], proj[:, T_HI + h, c * P:(c + 1) * P], ident[:])
                            mm.then_inc(sems["b4_mm"], 1)

                        def mean_square(h):
                            pe.wait_ge(sems["sq_done"], h + 1)
                            pe.wait_ge(sems["st_out"], 3 * h + 3)
                            pe.matmul(ps[:, 5, :], mean_w[:], osq[:], start=True, stop=True).then_inc(sems["ms_mm"], 1)

                        for h in range(H):
                            values_turned(h)
                            pe.wait_ge(sems["d3"], h + 1)
                            pe.wait_ge(sems["p3"], h + 1)
                            for c in range(QT):
                                n, tok = QT * h + c, slice(c * P, (c + 1) * P)
                                if n >= 2:
                                    pe.wait_ge(sems["att_done"], n - 1)
                                a = 2 * (n % 2)
                                for lv in range(LEVELS + 1):
                                    o = ps[:, a + lv // 4, (lv % 4) * P:(lv % 4 + 1) * P]
                                    if lv < LEVELS:
                                        both = lev[:, h % 2, lv, tok]
                                        mm = pe.matmul(o, both, both, start=True, stop=True)
                                    else:
                                        mm = pe.matmul(o, proj[:, T_HF + h, tok], proj[:, T_HQ + h, tok], start=True, stop=True)
                                mm.then_inc(sems["c_mm"], 1)
                                if c < QT - 1:
                                    pe.wait_ge(sems["b4_out"], b4_before_k(h, c))
                                    pe.transpose(ps[:, 4, 0:P], kd[:, h % 2, tok], ident[:]).then_inc(sems["b4_mm"], 1)
                                    pe.wait_ge(sems["b4_out"], b4_before_k(h, c) + 1)
                                    if 3 * h + c:
                                        pe.wait_ge(sems["st_out"], 3 * h + c)
                                    if h and c == 0:
                                        pe.wait_ge(sems["ms_out"], h)
                                    pe.matmul(ps[:, 5, 0:P], kd_t[:, n % 2, :], v_tok[:, h % 2, c, :], start=True,
                                              stop=True).then_inc(sems["st_mm"], 1)
                                o = ps[:, 6 + h % 2, tok]
                                if c == 0 and h >= 2:
                                    pe.wait_ge(sems["o_done"], h - 1)
                                if c > 0:
                                    pe.wait_ge(sems["st_out"], 3 * h + c)
                                    pe.matmul(o, state[:, (c - 1) % 2, :], qd[:, h % 2, tok], start=True, stop=False)
                                pe.wait_ge(sems["att_done"], n + 1)
                                for lv in range(LEVELS + 1):
                                    mm = pe.matmul(o, v_tok[:, h % 2, c, :], att[:, n % 2, lv * P:(lv + 1) * P],
                                                   start=(c == 0 and lv == 0), stop=(lv == LEVELS))
                                mm.then_inc(sems["pv_done"], 1)
                            mean_square(h)

                    @block.scalar
                    def _(act):
                        st = [0]

                        def then(ins):
                            ins.then_inc(sems["act_step"], 1)
                            st[0] += 1
                            act.wait_ge(sems["act_step"], st[0])

                        def part(h, k):
                            if k == 0:
                                if h:
                                    act.wait_ge(sems["d0"], h)
                                then(act.activation(lsp[:], proj[:, T_HF + h, :], ACT.Abs))
                                then(act.activation(lsp[:], lsp[:], ACT.Exp, scale=-1.0))
                                act.activation(lsp[:], lsp[:], ACT.Ln, bias=1.0).then_inc(sems["a0"], 1)
                            if k == 1:
                                act.wait_ge(sems["d0"], h + 1)
                                act.activation(proj[:, T_HF + h, :], karg[:], ACT.Exp, scale=-1.0, bias=hgc[:, 1, h:h + 1])
                                then(act.activation(lsg[:], lsg[:], ACT.Abs))
                                then(act.activation(lsg[:], lsg[:], ACT.Exp, scale=-1.0))
                                act.activation(lsg[:], lsg[:], ACT.Ln, bias=1.0).then_inc(sems["a1"], 1)
                            if k == 2:
                                act.wait_ge(sems["d2"], h + 1)
                                act.wait_ge(sems["p2"], h + 1)
                                l2 = lev[:, h % 2].rearrange("p l n -> p (l n)")
                                act.activation(l2, l2, ACT.Exp)
                                act.activation(kd[:, h % 2, :], kd[:, h % 2, :], ACT.Exp)
                                act.activation(ebs[:, h % 2, :], cum[:, h % 2, :], ACT.Exp).then_inc(sems["a2"], 1)

                        def values_out(h):
                            act.wait_ge(sems["b4_mm"], b4_before_v(h) + 1)
                            if h >= 2:
                                act.wait_ge(sems["pv_done"], QT * (h - 1))
                            act.activation(v_tok[:, h % 2].rearrange("p c d -> p (c d)"), ps[:, 4, :], ACT.Copy).then_inc(sems["b4_out"], 1)

                        for k in range(3):
                            part(0, k)
                        for h in range(H):
                            values_out(h)
                            for c in range(QT):
                                n = QT * h + c
                                if c < QT - 1:
                                    act.wait_ge(sems["b4_mm"], b4_before_k(h, c) + 1)
                                    if 3 * h + c >= 2:
                                        act.wait_ge(sems["st_mm"], 3 * h + c - 1)
                                    act.activation(kd_t[:, n % 2, :], ps[:, 4, 0:P], ACT.Copy).then_inc(sems["b4_out"], 1)
                                if h + 1 < H:
                                    part(h + 1, c)
                            act.wait_ge(sems["pv_done"], QT * h + QT)
                            if h:
                                act.wait_ge(sems["ms_mm"], h)
                            act.activation(osq[:], ps[:, 6 + h % 2, :], ACT.Square).then_inc(sems["sq_done"], 1)
                            act.wait_ge(sems["ms_out"], h + 1)
                            then(act.activation(rms[:], var[:], ACT.Ln))
                            act.activation(rms[:], rms[:], ACT.Exp, scale=-0.5).then_inc(sems["rs_act"], 1)
                            act.wait_ge(sems["o_done"], h + 1)
                            act.activation(xhi[:, 4 + h, :], tmp[:], ACT.Copy).then_inc(sems["o_hi"], 1)

                    @block.vector
                    def _(dve):
                        st = [0]

                        def then(ins):
                            ins.then_inc(sems["step"], 1)
                            st[0] += 1
                            dve.wait_ge(sems["step"], st[0])

                        def part(h, k):
                            z, hp = proj[:, T_HF + h, :], h % 2
                            if k == 0:
                                dve.wait_ge(sems["a0"], h + 1)
                                if h == 0:
                                    dve.tensor_copy(ngc[:], par[:, bass.ds(layer * HGRN_HEADS + PNG, HGRN_HEADS)])
                                    src = hgp[:, bass.ds(layer, 1), :, :].rearrange("p a k h -> p (a k h)")
                                    then(dve.tensor_copy(hgc[:, :, :].rearrange("p k h -> p (k h)"), src))
                                dve.scalar_tensor_tensor(out=karg[:], in0=z, scalar=0.0, in1=lsp[:], op0=ALU.max, op1=ALU.add)
                                then(dve.scalar_tensor_tensor(out=lsg[:], in0=z, scalar=0.0, in1=lsp[:], op0=ALU.min, op1=ALU.subtract))
                                dve.tensor_scalar(logf[:], lsg[:], hgc[:, 1, h:h + 1], hgc[:, 0, h:h + 1], ALU.add, ALU.max)
                                dve.tensor_scalar(lsg[:], lsg[:], hgc[:, 2, h:h + 1], None, ALU.add).then_inc(sems["d0"], 1)
                            if k == 1:
                                dve.wait_ge(sems["a1"], h + 1)
                                dve.wait_ge(sems["reset_done"], 2)
                                then(dve.tensor_tensor(logf[:], logf[:], lsg[:], ALU.add))
                                if h >= 2:
                                    dve.wait_ge(sems["a2"], h - 1)
                                dve.tensor_tensor_scan(cum[:, hp, :], reset[:], logf[:], 0.0, ALU.mult, ALU.add).then_inc(sems["d1"], 1)
                            if k == 2:
                                dve.wait_ge(sems["d1"], h + 1)
                                if h >= 2:
                                    dve.wait_ge(sems["pv_done"], QT * (h - 1))
                                for lv in range(LEVELS):
                                    dve.tensor_tensor(pairs(lev[:, hp, lv, :], lv, 1), pairs(cum[:, hp, :], lv, 1),
                                                      last_of(cum[:, hp, :], lv), ALU.subtract)
                                cv = cum[:, hp, :].rearrange("p (c n) -> p c n", n=P)
                                dve.tensor_tensor(kd[:, hp, :].rearrange("p (c n) -> p c n", n=P), cv[:, :, P - 1:P].broadcast_to([P, QT, P]),
                                                  cv, ALU.subtract).then_inc(sems["d2"], 1)
                            if k == 3:
                                dve.wait_ge(sems["a2"], h + 1)
                                for lv in range(LEVELS):
                                    r = pairs(lev[:, hp, lv, :], lv, 1)
                                    d = dve.tensor_tensor(r, r, pairs(proj[:, T_HQ + h, :], lv, 1), ALU.mult)
                                d.then_inc(sems["d3"], 1)

                        for k in range(4):
                            part(0, k)
                        dve.wait_ge(sems["aux_in"], 16)
                        for h in range(H):
                            for c in range(QT):
                                n = QT * h + c
                                dve.wait_ge(sems["c_mm"], n + 1)
                                if n >= 2:
                                    dve.wait_ge(sems["pv_done"], n - 1)
                                both = ps[:, 2 * (n % 2):2 * (n % 2) + 2, :].rearrange("p a n -> p (a n)")
                                dve.tensor_tensor(att[:, n % 2, :], both, hmask[:], ALU.mult).then_inc(sems["att_done"], 1)
                                if c < QT - 1:
                                    dve.wait_ge(sems["st_mm"], 3 * h + c + 1)
                                    if c == 0:
                                        if h:
                                            dve.wait_ge(sems["pv_done"], QT * h)
                                        dve.tensor_copy(state[:, 0, :], ps[:, 5, 0:P]).then_inc(sems["st_out"], 1)
                                    else:
                                        dve.wait_ge(sems["pv_done"], n)
                                        dve.wait_ge(sems["st_out"], 3 * h + c)
                                        dve.scalar_tensor_tensor(out=state[:, c % 2, :], in0=state[:, (c - 1) % 2, :],
                                                                 scalar=ebs[:, h % 2, c * P + P - 1:c * P + P], in1=ps[:, 5, 0:P],
                                                                 op0=ALU.mult, op1=ALU.add).then_inc(sems["st_out"], 1)
                                if h + 1 < H:
                                    part(h + 1, c)
                            dve.wait_ge(sems["ms_mm"], h + 1)
                            dve.tensor_scalar(var[:], ps[:, 5, :], float(D_MODEL // P), RMS_EPS, ALU.mult, ALU.add).then_inc(sems["ms_out"], 1)
                            dve.wait_ge(sems["rs_act"], h + 1)
                            if h:
                                dve.wait_ge(sems["o_hi"], h)
                            then(dve.tensor_tensor(tmp[:], var[:], rms[:], ALU.mult))
                            then(dve.tensor_tensor(tmp[:], tmp[:], rms[:], ALU.mult))
                            then(dve.tensor_scalar(tmp[:], tmp[:], -0.5, 1.5, ALU.mult, ALU.add))
                            then(dve.tensor_tensor(tmp[:], tmp[:], rms[:], ALU.mult))
                            then(dve.tensor_tensor(tmp[:], tmp[:], ps[:, 6 + h % 2, :], ALU.mult))
                            dve.scalar_tensor_tensor(out=tmp[:], in0=tmp[:], scalar=ngc[:, h:h + 1], in1=proj[:, T_HG + h, :],
                                                     op0=ALU.mult, op1=ALU.mult).then_inc(sems["o_done"], 1)
                            dve.wait_ge(sems["o_hi"], h + 1)
                            dve.tensor_tensor(xlo[:, 4 + h, :], tmp[:], xhi[:, 4 + h, :], ALU.subtract).then_inc(sems["o_lo"], 1)

                    @block.gpsimd
                    def _(pool):
                        pool.memset(reset[:], 1.0).then_inc(sems["reset_done"], 1)
                        pool.wait_ge(sems["reset_done"], 1)
                        pool.memset(reset[:, :].rearrange("p (c n) -> p c n", n=P)[:, :, 0:1], 0.0).then_inc(sems["reset_done"], 1)
                        for h in range(H):
                            hp = h % 2
                            pool.wait_ge(sems["d1"], h + 1)
                            if h >= 2:
                                pool.wait_ge(sems["pv_done"], QT * (h - 1))
                            for lv in range(LEVELS):
                                d = pool.tensor_tensor(pairs(lev[:, hp, lv, :], lv, 0), last_of(cum[:, hp, :], lv),
                                                       pairs(cum[:, hp, :], lv, 0), ALU.subtract)
                            d.then_inc(sems["p2"], 1)
                            pool.wait_ge(sems["a2"], h + 1)
                            for lv in range(LEVELS):
                                left = pairs(lev[:, hp, lv, :], lv, 0)
                                pool.tensor_tensor(left, left, pairs(proj[:, T_HF + h, :], lv, 0), ALU.mult)
                            pool.tensor_tensor(kd[:, hp, :], kd[:, hp, :], proj[:, T_HF + h, :], ALU.mult)
                            pool.tensor_tensor(qd[:, hp, :], ebs[:, hp, :], proj[:, T_HQ + h, :], ALU.mult).then_inc(sems["p3"], 1)
                clear(sems)

        def mix_out(layer):
            stage[0] = "mixout"
            with scope() as ctx:
                w = Weights(ctx, DT)
                acc = sb(ctx, "acc", [P, SEQ])
                r0 = sb(ctx, "r0", [P, SEQ])
                sq = [sb(ctx, f"sq{k}", [P, SEQ])[:] for k in range(2)]
                sems = semaphores(STREAM + LN, slots=[("raw_in", RAW)])
                N = DT // 2
                with nc.Block() as block:
                    def chunks(one):
                        def go(q, par_):
                            for u in range(2):
                                one(2 * q + u, 2 * par_ + u)
                        return go

                    @block.sync
                    def _(sp):
                        by_pairs(sp, N, chunks(lambda c, s: load_chunk(sp, sems, w.raw, c, s, cols_of(w_out, layer, 0, DT, c * P), DT)))

                    @block.gpsimd
                    def _(pool):
                        ln_acc(pool, sems, acc[:], seed=4)

                    @block.tensor
                    def _(pe):
                        pe.sem_inc(sems["mm_done"], SPLIT)

                        def two(q, par_):
                            pe.wait_ge(sems["y_done"], 2 * q + 2)
                            for u in range(2):
                                multiply(pe, sems, w, 2 * q + u, 2 * par_ + u, DT, 2 * par_ + u,
                                         lambda k: xhi[:, k, :], lambda k: xlo[:, k, :])
                        by_pairs(pe, N, two)
                        ln_pe(pe, sems, acc[:], sq)

                    @block.scalar
                    def _(act):
                        split = chunks(lambda c, s: split_hi(act, sems, w, c, s, DT))
                        split(0, 0)
                        in_pairs(act, N, split, lambda q, par_: None)
                        ln_act(act, sems, 1, sq, r0[:], 1)

                    @block.vector
                    def _(dve):
                        dve.sem_inc(sems["lo_done"], RAW)
                        dve.sem_inc(sems["y_done"], 4)
                        split = chunks(lambda c, s: split_lo(dve, sems, w, c, s, DT))
                        split(0, 0)

                        def residual(q, par_):
                            for u in range(2):
                                dve.wait_ge(sems["mm_done"], 2 * q + u + SPLIT + 1)
                                dve.scalar_tensor_tensor(out=at(xT, 2 * q + u), in0=at(xT, 2 * q + u), scalar=ALPHA,
                                                         in1=ps[:, 2 * par_ + u, :], op0=ALU.mult, op1=ALU.add).then_inc(sems["y_done"], 1)
                        in_pairs(dve, N, split, residual)
                        ln_dve(dve, sems, LN_EPS, r0[:], acc[:])
                clear(sems)

        ROPE = [("q", T_Q, 0), ("q", T_Q + 1, 0), ("k", T_SLC, 0), ("k", T_WIN, 0),
                ("q", T_SQ, 0), ("q", T_SQ + 1, 0), ("k", T_SK, 0), ("k", T_SK, 64)]
        rope_pool = [1, 2, 2, 2, 3, 4, 4, 4]

        def mixer(layer):
            stage[0] = "mix"
            with scope() as ctx:
                proj = sb(ctx, "proj", [P, N_PM, SEQ])
                attention(layer, proj)
                hgrn2(layer, proj)
            mix_out(layer)

        with nc.Fori(0, DEPTH) as layer:
            ffn(layer, 0)
            mixer(layer)
            ffn(layer, 1)

        stage[0] = "end"
        with scope() as ctx:
            xo = sb(ctx, "xo", [P, QT, D_MODEL])
            sems = semaphores(["turned", "emptied", "stored"])
            with nc.Block() as block:
                @block.tensor
                def _(pe):
                    n = 0
                    for t in range(QT):
                        for h in range(2):
                            if n >= 4:
                                pe.wait_ge(sems["emptied"], n - 3)
                            for j in range(4):
                                mm = pe.transpose(ps[:, n % 4, j * P:(j + 1) * P],
                                                  xT[:, 4 * h + j, t * P:(t + 1) * P], ident[:])
                            mm.then_inc(sems["turned"], 1)
                            n += 1

                @block.vector
                def _(dve):
                    for n in range(2 * QT):
                        dve.wait_ge(sems["turned"], n + 1)
                        dve.tensor_copy(xo[:, n // 2, (n % 2) * 512:(n % 2 + 1) * 512], ps[:, n % 4, :]).then_inc(sems["emptied"], 1)

                @block.sync
                def _(sp):
                    for t in range(QT):
                        sp.wait_ge(sems["emptied"], 2 * t + 2)
                        sp.dma_start(out[0, t * P:(t + 1) * P, :], xo[:, t, :]).then_inc(sems["stored"], 16)
                    sp.wait_ge(sems["stored"], 16 * QT)


_INS = ['x', 'p', 'ln_g', 'ln_b', 'ffn_w_gu', 'ffn_w_down', 'w_in', 'w_out', 'cmp_pos', 'cmp_k_w1', 'cmp_k_w2',
        'cmp_v_w1', 'cmp_v_w2', 'swa_sinks', 'hgrn_lb_raw', 'hgrn_norm_g', 'ple_w', 'ple_gate_w', 'ple_gate_b']


def kernel(**inputs):
    import concourse.bacc as bacc
    from concourse.bass_utils import run_bass_kernel_spmd

    nc = bacc.Bacc("TRN2", target_bir_lowering=False, num_devices=1)
    consts, rope = shape_constants()
    named = {f"in_{name}_dram": np.ascontiguousarray(inputs[name]) for name in _INS}
    named["in_consts_dram"] = consts
    named["in_rope_dram"] = rope
    args = [nc.dram_tensor(name, a.shape, mybir.dt.from_np(a.dtype), kind="ExternalInput").ap()
            for name, a in named.items()]
    out = nc.dram_tensor("out_0_dram", (1, SEQ, D_MODEL), F32, kind="ExternalOutput").ap()
    build(nc, *args, out)
    r = run_bass_kernel_spmd(nc, [named], core_ids=[0])
    return r.results[0]["out_0_dram"]
```

```python
from contextlib import ExitStack

import numpy as np

import concourse.bass as bass
from concourse import mybir

F32 = mybir.dt.float32
F32R = mybir.dt.float32r
ALU = mybir.AluOpType
ACT = mybir.ActivationFunctionType
AX = mybir.AxisListType

P = 128
D_MODEL, SEQ, DEPTH, D_FF, PLE_DIM = 1024, 512, 2, 2816, 256
HEAD_DIM, NSA_HEADS, SWA_HEADS, HGRN_HEADS = 64, 4, 4, 4
CMP_LEN, CMP_STRIDE, CMP_HID = 32, 16, 256
N_CMP = (SEQ - CMP_LEN) // CMP_STRIDE + 1
DT = D_MODEL // P
FT = D_FF // P
QT = SEQ // P
PT_ = PLE_DIM // P
KD = FT // 2
NSA_COLS = 256 + 6 * 64 + 12
N_PM = 26
ALPHA = (2.0 * DEPTH) ** 0.25
LN_EPS, RMS_EPS = 1e-5, 1e-6
SCALE = HEAD_DIM ** -0.5
LN_FLOOR = float(np.log(np.float32(1e-30)))
RAW, SPLIT = 4, 2
LEVELS = 7

T_Q, T_CMP, T_SLC, T_WIN, T_GATE, T_SQ, T_SK, T_SV, T_HQ, T_HF, T_HI, T_HG = 0, 2, 3, 4, 5, 6, 8, 9, 10, 14, 18, 22

C_ID, C_ROT, C_DUP, C_ROTDUP, C_CAUSAL, C_BAND, C_CMP = (P * k for k in range(7))
C_HG = C_CMP + QT * N_CMP
C_END = C_HG + (LEVELS + 1) * P


def shape_constants():
    c = np.zeros((P, C_END), np.float32)
    r = np.arange(P)
    c[:, C_ID:C_ID + P] = np.eye(P)
    for m in range(P):
        other = m + 32 if m % 64 < 32 else m - 32
        sign = -1.0 if m % 64 < 32 else 1.0
        c[other, C_ROT + m] = sign
        for half in (0, 64):
            c[half + m % 64, C_DUP + m] = 1.0
            c[half + other % 64, C_ROTDUP + m] = sign
    q, k = r[:, None], r[None, :]
    c[:, C_CAUSAL:C_CAUSAL + P] = np.where(k <= q, 0.0, -1e30)
    c[:, C_BAND:C_BAND + P] = np.where(k > q, 0.0, -1e30)
    ends = np.arange(N_CMP) * CMP_STRIDE + CMP_LEN - 1
    for i in range(QT):
        c[:, C_CMP + i * N_CMP:C_CMP + (i + 1) * N_CMP] = np.where(ends[None, :] <= i * P + q, 0.0, -1e30)
    s, t = r[:, None], r[None, :]
    for lv in range(LEVELS):
        m = 1 << lv
        same = (s // (2 * m)) == (t // (2 * m))
        c[:, C_HG + lv * P:C_HG + (lv + 1) * P] = same & (s // m % 2 == 0) & (t // m % 2 == 1)
    c[:, C_HG + LEVELS * P:] = s == t
    inv = (1.0 / (np.float32(10000.0) ** (np.arange(0, HEAD_DIM, 2, dtype=np.float32) / HEAD_DIM))).astype(np.float32)
    ang = np.arange(SEQ, dtype=np.float32)[:, None] * inv[None, :]
    rope = np.concatenate([np.tile(np.cos(ang).T, (4, 1)), np.tile(np.sin(ang).T, (4, 1))], axis=1)
    return c, rope.astype(np.float32)


def build(nc, x, p, ln_g, ln_b, ffn_w_gu, ffn_w_down, w_in, w_out, cmp_pos, cmp_k_w1, cmp_k_w2, cmp_v_w1,
          cmp_v_w2, swa_sinks, hgrn_lb_raw, hgrn_norm_g, ple_w, ple_gate_w, ple_gate_b, consts_d, rope_d, out):
    with ExitStack() as whole:
        def scope():
            return ExitStack()

        stage = ["start"]

        def sb(ctx, name, shape, dt=F32):
            return ctx.enter_context(nc.sbuf_tensor(f"{stage[0]}_{name}", shape, dt))

        ps = whole.enter_context(nc.psum_tensor("banks", [P, 8, 512], F32))

        xT = sb(whole, "xT", [P, DT, SEQ])
        xhi = sb(whole, "xhi", [P, DT, SEQ], F32R)
        xlo = sb(whole, "xlo", [P, DT, SEQ], F32R)
        ident = sb(whole, "ident", [P, P])
        mean_w = sb(whole, "mean_w", [P, P])
        par = sb(whole, "par", [P, P])
        hgp = sb(whole, "hgp", [P, DEPTH, 3, HGRN_HEADS])
        lng = sb(whole, "lng", [P, 3 * DT])
        lnb = sb(whole, "lnb", [P, 3 * DT])
        gbh = sb(whole, "gbh", [P, DT])
        epsc = sb(whole, "epsc", [P, 2])
        sinks = sb(whole, "sinks", [P, DEPTH * SWA_HEADS])
        PG, PB, PGB, PNG, PLB = 0, 24 * DEPTH, 48 * DEPTH, 56 * DEPTH, 60 * DEPTH

        def semaphores(names, slots=()):
            sems = {n: nc.alloc_semaphore(f"{stage[0]}_{n}") for n in names}
            for n, count in slots:
                sems[n] = [nc.alloc_semaphore(f"{stage[0]}_{n}{k}") for k in range(count)]
            return sems

        def clear(sems):
            for s in sems.values():
                for one in (s if isinstance(s, list) else [s]):
                    nc.sync.sem_clear(one)
            nc.all_engine_barrier()
            for s in sems.values():
                for one in (s if isinstance(s, list) else [s]):
                    nc.release_semaphore(one)

        STREAM = ["hi_done", "lo_done", "mm_done"]

        def load_chunk(sp, sems, raw, c, slot, src, kt):
            sp.wait_ge(sems["lo_done"], c + 1)
            sp.dma_start(raw[:, slot, 0:kt, :], src).then_inc(sems["raw_in"][slot], 16)

        def arrived(c, slot):
            return (c - slot) * (16 // RAW) + 16

        def split_hi(act, sems, w, c, slot, kt):
            act.wait_ge(sems["raw_in"][slot], arrived(c, slot))
            act.wait_ge(sems["mm_done"], c + 1)
            act.activation(w.hi[:, slot % SPLIT, 0:kt, :], w.raw[:, slot, 0:kt, :], ACT.Copy).then_inc(sems["hi_done"], 1)

        def split_lo(dve, sems, w, c, slot, kt):
            dve.wait_ge(sems["hi_done"], c + 1)
            dve.tensor_tensor(w.lo[:, slot % SPLIT, 0:kt, :], w.raw[:, slot, 0:kt, :], w.hi[:, slot % SPLIT, 0:kt, :],
                              ALU.subtract).then_inc(sems["lo_done"], 1)

        def multiply(pe, sems, w, c, slot, kt, bank, hi, lo, first=True, last=True, ready=None, n=SEQ):
            pe.wait_ge(sems["lo_done"], c + RAW + 1)
            for k in range(kt):
                if ready:
                    ready(k)
                wh, wl = w.hi[:, slot % SPLIT, k, :], w.lo[:, slot % SPLIT, k, :]
                pe.matmul(ps[:, bank, 0:n], wh, hi(k), start=(first and k == 0), stop=False)
                pe.matmul(ps[:, bank, 0:n], wh, lo(k), start=False, stop=False)
                mm = pe.matmul(ps[:, bank, 0:n], wl, hi(k), start=False, stop=(last and k == kt - 1))
            mm.then_inc(sems["mm_done"], 1)

        class Weights:
            def __init__(self, ctx, kt):
                self.raw = sb(ctx, "w_raw", [P, RAW, kt, P])
                self.hi = sb(ctx, "w_hi", [P, SPLIT, kt, P], F32R)
                self.lo = sb(ctx, "w_lo", [P, SPLIT, kt, P], F32R)

        def in_pairs(eng, n, split, consume, next_split=None, par0=0):
            loops = (n - 1) // 2
            with eng.Fori(0, loops) as i:
                for u in range(2):
                    split(2 * i + u + 1, (u + 1 + par0) % 2)
                    consume(2 * i + u, (u + par0) % 2)
            for q in range(2 * loops, n):
                if q + 1 < n:
                    split(q + 1, (q + 1 + par0) % 2)
                elif next_split:
                    next_split()
                consume(q, (q + par0) % 2)

        def by_pairs(eng, n, body, par0=0):
            with eng.Fori(0, n // 2) as i:
                for u in range(2):
                    body(2 * i + u, (u + par0) % 2)
            if n % 2:
                body(n - 1, (n - 1 + par0) % 2)

        def at(t, k):
            if isinstance(k, int):
                return t[:, k, :]
            return t[:, bass.ds(k, 1), :].rearrange("p a n -> p (a n)")

        def col(t, k):
            return t[:, k:k + 1] if isinstance(k, int) else t[:, bass.ds(k, 1)]

        def cols_of(w, layer, k0, kt, c0):
            v = w.rearrange("l (t p) n -> l p t n", p=P)
            return v[bass.ds(layer, 1), :, k0:k0 + kt, bass.ds(c0, P)].rearrange("a p t n -> (a p) t n")

        LN = ["y_done", "acc_done", "ln_pe", "centred", "squared", "rstd_act", "newton", "scaled", "affine",
              "x_hi", "x_lo"]

        def ln_acc(pool, sems, acc, seed=2):
            pool.memset(acc, 0.0).then_inc(sems["acc_done"], 1)
            with pool.Fori(0, DT) as j:
                pool.wait_ge(sems["y_done"], j + seed + 1)
                pool.wait_ge(sems["acc_done"], j + 1)
                pool.tensor_tensor(acc, acc, at(xT, j), ALU.add).then_inc(sems["acc_done"], 1)

        def ln_pe(pe, sems, acc, sq):
            pe.wait_ge(sems["acc_done"], DT + 1)
            pe.matmul(ps[:, 6, :], mean_w[:], acc, start=True, stop=True).then_inc(sems["ln_pe"], 1)
            for j in range(DT):
                pe.wait_ge(sems["squared"], j + 1)
                pe.matmul(ps[:, 7, :], mean_w[:], sq[j % 2], start=(j == 0), stop=(j == DT - 1)).then_inc(sems["ln_pe"], 1)

        def ln_act(act, sems, which, sq, r0, eps_col):
            act.preload_act_table_set("natural_log_exp_and_others")
            for j in range(DT):
                act.wait_ge(sems["centred"], j + 1)
                if j >= 2:
                    act.wait_ge(sems["ln_pe"], j)
                act.activation(sq[j % 2], xT[:, j, :], ACT.Square).then_inc(sems["squared"], 1)
            act.wait_ge(sems["ln_pe"], DT + 1)
            act.activation(r0, ps[:, 7, :], ACT.Ln, bias=epsc[:, eps_col:eps_col + 1]).then_inc(sems["rstd_act"], 1)
            act.wait_ge(sems["rstd_act"], 1)
            act.activation(r0, r0, ACT.Exp, scale=-0.5).then_inc(sems["rstd_act"], 1)
            for j in range(DT):
                k = which * DT + j
                act.wait_ge(sems["scaled"], j + 1)
                act.activation(xT[:, j, :], xT[:, j, :], ACT.Identity, bias=lnb[:, k:k + 1],
                               scale=lng[:, k:k + 1]).then_inc(sems["affine"], 1)
                act.wait_ge(sems["affine"], j + 1)
                act.activation(xhi[:, j, :], xT[:, j, :], ACT.Copy).then_inc(sems["x_hi"], 1)

        def ln_dve(dve, sems, eps, r0, t):
            dve.wait_ge(sems["ln_pe"], 1)
            for j in range(DT):
                dve.tensor_tensor(xT[:, j, :], xT[:, j, :], ps[:, 6, :], ALU.subtract).then_inc(sems["centred"], 1)
            dve.wait_ge(sems["rstd_act"], 2)
            dve.scalar_tensor_tensor(out=t, in0=ps[:, 7, :], scalar=eps, in1=r0, op0=ALU.add,
                                     op1=ALU.mult).then_inc(sems["newton"], 1)
            dve.wait_ge(sems["newton"], 1)
            dve.tensor_tensor(t, t, r0, ALU.mult).then_inc(sems["newton"], 1)
            dve.wait_ge(sems["newton"], 2)
            dve.tensor_scalar(t, t, -0.5, 1.5, ALU.mult, ALU.add).then_inc(sems["newton"], 1)
            dve.wait_ge(sems["newton"], 3)
            dve.tensor_tensor(t, t, r0, ALU.mult).then_inc(sems["newton"], 1)
            dve.wait_ge(sems["newton"], 4)
            dve.wait_ge(sems["centred"], DT)
            for j in range(DT + 1):
                if j < DT:
                    dve.tensor_tensor(xT[:, j, :], xT[:, j, :], t, ALU.mult).then_inc(sems["scaled"], 1)
                if j >= 1:
                    x_low(dve, sems, j - 1)

        def x_low(dve, sems, j, before=0):
            dve.wait_ge(sems["x_hi"], before + j + 1)
            dve.tensor_tensor(xlo[:, j, :], xT[:, j, :], xhi[:, j, :], ALU.subtract).then_inc(sems["x_lo"], 1)

        with scope() as ctx:
            xin = sb(ctx, "xin", [P, QT, D_MODEL])
            rows = sb(ctx, "rows", [P, P])
            lbs = sb(ctx, "lbs", [P, 6, HGRN_HEADS])
            sems = semaphores(["loaded", "x_in", "made", "turned", "emptied", "x_hi", "x_lo", "par_in", "lbt", "lba"])

            with nc.Block() as block:
                @block.sync
                def _(sp):
                    sp.dma_start(ident[:], consts_d[:, C_ID:C_ID + P]).then_inc(sems["loaded"], 16)
                    for src, r0, n in ((ln_g.rearrange("l t (j q) -> (l t j) q", q=P), PG, 24 * DEPTH),
                                       (ln_b.rearrange("l t (j q) -> (l t j) q", q=P), PB, 24 * DEPTH),
                                       (ple_gate_b.rearrange("l (j q) -> (l j) q", q=P), PGB, 8 * DEPTH),
                                       (hgrn_norm_g.rearrange("l (j q) -> (l j) q", q=P), PNG, 4 * DEPTH),
                                       (hgrn_lb_raw.rearrange("l (j q) -> (l j) q", q=P), PLB, 4 * DEPTH)):
                        sp.dma_start(rows[r0:r0 + n, :], src).then_inc(sems["loaded"], 16)
                    sp.dma_start(sinks[:], swa_sinks.rearrange("l h -> (l h)").partition_broadcast(P)).then_inc(sems["loaded"], 16)
                    for t in range(QT):
                        sp.dma_start(xin[:, t, :], x[0, t * P:(t + 1) * P, :]).then_inc(sems["x_in"], 16)
                    sp.wait_ge(sems["loaded"], 16 * 7)

                @block.gpsimd
                def _(pool):
                    pool.memset(mean_w[:], 1.0 / D_MODEL)
                    pool.memset(epsc[:, 0:1], 4.0 * LN_EPS)
                    pool.memset(epsc[:, 1:2], LN_EPS)
                    pool.memset(hgp[:, 0, 1, :], 0.0).then_inc(sems["made"], 1)

                @block.tensor
                def _(pe):
                    pe.wait_ge(sems["loaded"], 16 * 7)
                    pe.transpose(ps[:, 7, 0:P], rows[:], ident[:]).then_inc(sems["par_in"], 1)
                    pe.wait_ge(sems["x_in"], 16 * QT)
                    for j in range(DT):
                        if j >= 4:
                            pe.wait_ge(sems["emptied"], j - 3)
                        for t in range(QT):
                            mm = pe.transpose(ps[:, j % 4, t * P:(t + 1) * P], xin[:, t, j * P:(j + 1) * P], ident[:])
                        mm.then_inc(sems["turned"], 1)

                @block.scalar
                def _(act):
                    for j in range(DT):
                        act.wait_ge(sems["emptied"], j + 1)
                        act.activation(xhi[:, j, :], xT[:, j, :], ACT.Copy).then_inc(sems["x_hi"], 1)
                    act.wait_ge(sems["lbt"], 3)
                    act.activation(lbs[:, 3, :], lbs[:, 1, :], ACT.Exp)
                    act.activation(lbs[:, 4, :], lbs[:, 2, :], ACT.Exp).then_inc(sems["lba"], 1)
                    act.wait_ge(sems["lbt"], 4)
                    act.activation(lbs[:, 5, :], lbs[:, 5, :], ACT.Ln).then_inc(sems["lba"], 1)

                @block.vector
                def _(dve):
                    dve.wait_ge(sems["par_in"], 1)
                    dve.tensor_copy(par[:], ps[:, 7, 0:P]).then_inc(sems["lbt"], 1)
                    dve.wait_ge(sems["lbt"], 1)
                    r0, r1 = par[:, PLB:PLB + 4], par[:, PLB + 4:PLB + 8]
                    dve.tensor_tensor(lbs[:, 0, :], r0, r1, ALU.max).then_inc(sems["lbt"], 1)
                    dve.wait_ge(sems["lbt"], 2)
                    dve.tensor_tensor(lbs[:, 1, :], r0, lbs[:, 0, :], ALU.subtract)
                    dve.tensor_tensor(lbs[:, 2, :], r1, lbs[:, 0, :], ALU.subtract).then_inc(sems["lbt"], 1)
                    for j in range(DT):
                        dve.wait_ge(sems["turned"], j + 1)
                        dve.tensor_copy(xT[:, j, :], ps[:, j % 4, :]).then_inc(sems["emptied"], 1)
                    for j in range(DT):
                        x_low(dve, sems, j)
                    dve.wait_ge(sems["lba"], 1)
                    dve.tensor_tensor(lbs[:, 5, :], lbs[:, 3, :], lbs[:, 4, :], ALU.add).then_inc(sems["lbt"], 1)
                    dve.wait_ge(sems["lba"], 2)
                    dve.tensor_tensor(hgp[:, 1, 1, :], lbs[:, 1, :], lbs[:, 5, :], ALU.subtract).then_inc(sems["lbt"], 1)
                    dve.tensor_tensor(hgp[:, 1, 0, :], lbs[:, 2, :], lbs[:, 5, :], ALU.subtract).then_inc(sems["lbt"], 1)
                    dve.wait_ge(sems["lbt"], 6)
                    dve.tensor_scalar(hgp[:, 1, 0, :], hgp[:, 1, 0, :], LN_FLOOR, None, ALU.max)
                    dve.memset(hgp[:, 0, 0, :], LN_FLOOR).then_inc(sems["lbt"], 1)
                    dve.wait_ge(sems["made"], 1)
                    dve.wait_ge(sems["lbt"], 7)
                    for l in range(DEPTH):
                        dve.tensor_tensor(hgp[:, l, 2, :], hgp[:, l, 1, :], hgp[:, l, 0, :], ALU.subtract)
            clear(sems)

        def ffn(layer, half):
            ple = half == 1
            which = 2 * half
            stage[0] = f"ffn{half + 1}"
            with scope() as ctx:
                w = Weights(ctx, KD)
                hhi = sb(ctx, "hhi", [P, FT, SEQ], F32R)
                hlo = sb(ctx, "hlo", [P, FT, SEQ], F32R)
                gate = sb(ctx, "gate", [P, 2, SEQ])
                prod = sb(ctx, "prod", [P, 2, SEQ])
                acc, r0 = gate[:, 0, :], gate[:, 1, :]
                sq = [prod[:, 0, :], prod[:, 1, :]]
                if ple:
                    phi = sb(ctx, "phi", [P, PT_, SEQ], F32R)
                    plo = sb(ctx, "plo", [P, PT_, SEQ], F32R)
                    pin = gate[:, :, :].rearrange("p a (b n) -> p (a b) n", n=PLE_DIM)
                sems = semaphores(STREAM + LN + ["gate_done", "h_done", "h_hi", "h_lo", "par_done", "p_in", "p_turned",
                                           "p_hi", "p_lo", "e_act", "e_mul", "e_done"], slots=[("raw_in", RAW)])
                C_DN, C_PLE = 2 * FT, 2 * FT + 2 * DT

                gu = ffn_w_gu.rearrange("l h k n -> (l h) k n")
                dn = ffn_w_down.rearrange("l h k n -> (l h) k n")
                which_w = layer * 2 + half

                with nc.Block() as block:
                    @block.sync
                    def _(sp):
                        if ple:
                            for t in range(QT):
                                src = p[bass.ds(layer, 1), 0, t * P:(t + 1) * P, :].rearrange("a q n -> (a q) n")
                                sp.dma_start(pin[:, t, :], src).then_inc(sems["p_in"], 16)

                        def up(q, par_):
                            for u in range(2):
                                load_chunk(sp, sems, w.raw, 2 * q + u, 2 * par_ + u,
                                           cols_of(gu, which_w, 0, DT, q * P + u * D_FF), DT)

                        def down(q, par_):
                            for u in range(2):
                                load_chunk(sp, sems, w.raw, C_DN + 2 * q + u, 2 * par_ + u,
                                           cols_of(dn, which_w, u * KD, KD, q * P), KD)

                        def embed(q, par_):
                            load_chunk(sp, sems, w.raw, C_PLE + 2 * q, 2 * par_,
                                       cols_of(ple_gate_w, layer, 0, DT, q * P), DT)
                            load_chunk(sp, sems, w.raw, C_PLE + 2 * q + 1, 2 * par_ + 1,
                                       cols_of(ple_w, layer, 0, PT_, q * P), PT_)
                        by_pairs(sp, FT, up)
                        by_pairs(sp, DT, down)
                        if ple:
                            by_pairs(sp, DT, embed)

                    def split_with(one, eng):
                        def up(q, par_):
                            for u in range(2):
                                one(eng, sems, w, 2 * q + u, 2 * par_ + u, DT)

                        def down(q, par_):
                            for u in range(2):
                                one(eng, sems, w, C_DN + 2 * q + u, 2 * par_ + u, KD)

                        def embed(q, par_):
                            one(eng, sems, w, C_PLE + 2 * q, 2 * par_, DT)
                            one(eng, sems, w, C_PLE + 2 * q + 1, 2 * par_ + 1, PT_)
                        return up, down, embed

                    @block.gpsimd
                    def _(pool):
                        pool.wait_ge(sems["h_lo"], FT)
                        ln_acc(pool, sems, acc)

                    @block.tensor
                    def _(pe):
                        pe.sem_inc(sems["mm_done"], SPLIT)
                        if ple:
                            pe.wait_ge(sems["p_in"], 16 * QT)
                            for k in range(PT_):
                                for t in range(QT):
                                    mm = pe.transpose(ps[:, 4 + k, t * P:(t + 1) * P], pin[:, t, k * P:(k + 1) * P], ident[:])
                                mm.then_inc(sems["p_turned"], 1)

                        def up(q, par_):
                            pe.wait_ge(sems["h_done"], q + 1)
                            for u in range(2):
                                multiply(pe, sems, w, 2 * q + u, 2 * par_ + u, DT, 2 * par_ + u,
                                         lambda k: xhi[:, k, :], lambda k: xlo[:, k, :])

                        def down(q, par_):
                            pe.wait_ge(sems["y_done"], q + 1)

                            def ready(k):
                                if k >= KD - 2:
                                    pe.wait_ge(sems["h_lo"], FT - (KD - 1 - k))
                            for u in range(2):
                                multiply(pe, sems, w, C_DN + 2 * q + u, 2 * par_ + u, KD, 4 + par_,
                                         lambda k: hhi[:, u * KD + k, :], lambda k: hlo[:, u * KD + k, :],
                                         first=(u == 0), last=(u == 1), ready=ready if u else None)

                        def embed(q, par_):
                            pe.wait_ge(sems["e_done"], q + 1)
                            multiply(pe, sems, w, C_PLE + 2 * q, 2 * par_, DT, 2 * par_,
                                     lambda k: xhi[:, k, :], lambda k: xlo[:, k, :])
                            multiply(pe, sems, w, C_PLE + 2 * q + 1, 2 * par_ + 1, PT_, 2 * par_ + 1,
                                     lambda k: phi[:, k, :], lambda k: plo[:, k, :])
                        by_pairs(pe, FT, up)
                        if ple:
                            pe.wait_ge(sems["p_lo"], PT_)
                        by_pairs(pe, DT, down)
                        ln_pe(pe, sems, acc, sq)
                        if ple:
                            pe.wait_ge(sems["x_lo"], DT)
                            by_pairs(pe, DT, embed)

                    @block.scalar
                    def _(act):
                        s_up, s_down, s_embed = split_with(split_hi, act)
                        if ple:
                            for k in range(PT_):
                                act.wait_ge(sems["p_turned"], k + 1)
                                act.activation(phi[:, k, :], ps[:, 4 + k, :], ACT.Copy).then_inc(sems["p_hi"], 1)
                        s_up(0, 0)

                        def gates(q, par_):
                            act.wait_ge(sems["mm_done"], 2 * q + SPLIT + 1)
                            act.wait_ge(sems["h_done"], q + 1)
                            act.activation(gate[:, par_, :], ps[:, 2 * par_, :], ACT.Silu).then_inc(sems["gate_done"], 1)
                            act.wait_ge(sems["h_done"], q + SPLIT + 1)
                            act.activation(at(hhi, q), prod[:, par_, :], ACT.Copy).then_inc(sems["h_hi"], 1)
                        if ple:
                            act.wait_ge(sems["p_lo"], PT_)
                        act.preload_act_table_set("silu_and_others")
                        in_pairs(act, FT, s_up, gates, lambda: s_down(0, 0))
                        in_pairs(act, DT, s_down, lambda q, par_: None, (lambda: s_embed(0, 0)) if ple else None)
                        ln_act(act, sems, which, sq, r0, 0)

                        def sigm(q, par_):
                            act.wait_ge(sems["mm_done"], C_PLE + 2 * q + SPLIT + 1)
                            act.wait_ge(sems["e_done"], q + 1)
                            act.activation(gate[:, par_, :], ps[:, 2 * par_, :], ACT.Tanh, scale=0.5,
                                           bias=col(gbh, q)).then_inc(sems["e_act"], 1)
                        if ple:
                            act.preload_act_table_set("silu_and_others")
                            act.wait_ge(sems["scaled"], DT)
                            in_pairs(act, DT, s_embed, sigm)
                            act.wait_ge(sems["e_done"], DT + SPLIT)
                            for j in range(DT):
                                act.activation(xhi[:, j, :], xT[:, j, :], ACT.Copy).then_inc(sems["x_hi"], 1)

                    @block.vector
                    def _(dve):
                        s_up, s_down, s_embed = split_with(split_lo, dve)
                        dve.sem_inc(sems["lo_done"], RAW)
                        dve.sem_inc(sems["h_done"], 2)
                        dve.sem_inc(sems["y_done"], 2)
                        dve.sem_inc(sems["e_done"], 2)
                        if not ple:
                            dve.tensor_copy(lng[:], par[:, bass.ds(layer * 24 + PG, 24)])
                            dve.tensor_copy(lnb[:], par[:, bass.ds(layer * 24 + PB, 24)])
                            dve.tensor_scalar(gbh[:], par[:, bass.ds(layer * 8 + PGB, 8)], 0.5, None,
                                              ALU.mult).then_inc(sems["par_done"], 1)
                        else:
                            for k in range(PT_):
                                dve.wait_ge(sems["p_hi"], k + 1)
                                dve.tensor_tensor(plo[:, k, :], ps[:, 4 + k, :], phi[:, k, :],
                                                  ALU.subtract).then_inc(sems["p_lo"], 1)
                        s_up(0, 0)

                        def hidden(q, par_):
                            dve.wait_ge(sems["gate_done"], q + 1)
                            dve.wait_ge(sems["mm_done"], 2 * q + SPLIT + 2)
                            dve.tensor_tensor(prod[:, par_, :], gate[:, par_, :], ps[:, 2 * par_ + 1, :],
                                              ALU.mult).then_inc(sems["h_done"], 1)
                            dve.wait_ge(sems["h_hi"], q + 1)
                            dve.tensor_tensor(at(hlo, q), prod[:, par_, :], at(hhi, q),
                                              ALU.subtract).then_inc(sems["h_lo"], 1)

                        def residual(q, par_):
                            dve.wait_ge(sems["mm_done"], C_DN + 2 * q + SPLIT + 2)
                            dve.scalar_tensor_tensor(out=at(xT, q), in0=at(xT, q), scalar=2.0 * ALPHA,
                                                     in1=ps[:, 4 + par_, :], op0=ALU.mult,
                                                     op1=ALU.add).then_inc(sems["y_done"], 1)
                        in_pairs(dve, FT, s_up, hidden, lambda: s_down(0, 0))
                        in_pairs(dve, DT, s_down, residual, (lambda: s_embed(0, 0)) if ple else None)
                        ln_dve(dve, sems, 4.0 * LN_EPS, r0, acc)

                        def embed(q, par_):
                            dve.wait_ge(sems["e_act"], q + 1)
                            dve.wait_ge(sems["mm_done"], C_PLE + 2 * q + SPLIT + 2)
                            dve.scalar_tensor_tensor(out=prod[:, par_, :], in0=gate[:, par_, :], scalar=1.0,
                                                     in1=ps[:, 2 * par_ + 1, :], op0=ALU.add,
                                                     op1=ALU.mult).then_inc(sems["e_mul"], 1)
                            dve.wait_ge(sems["e_mul"], q + 1)
                            dve.scalar_tensor_tensor(out=at(xT, q), in0=prod[:, par_, :], scalar=0.5,
                                                     in1=at(xT, q), op0=ALU.mult, op1=ALU.add).then_inc(sems["e_done"], 1)
                        if ple:
                            in_pairs(dve, DT, s_embed, embed)
                            for j in range(DT):
                                x_low(dve, sems, j, before=DT)
                clear(sems)

        def attention(layer, proj, v_tok, v_swa, gates):
            stage[0] = "attn"
            NSA_N, UNITS = NSA_HEADS * QT, (NSA_HEADS + SWA_HEADS) * QT
            with scope() as ctx:
                cst = sb(ctx, "masks", [P, C_HG])
                anyv = sb(ctx, "anyv", [P, 1])
                prob = sb(ctx, "prob", [P, 2, 2, SEQ])
                prob_t = sb(ctx, "prob_t", [P, 2, 2, SEQ])
                hid_t = sb(ctx, "hid_t", [N_CMP, 2 * CMP_HID])
                hid = sb(ctx, "hid", [P, 4, 32])
                w2k = sb(ctx, "w2k", [P, 2, P])
                w2v = sb(ctx, "w2v", [P, 2, HEAD_DIM])
                kc = sb(ctx, "kc", [P, 32])
                vc = sb(ctx, "vc", [N_CMP, HEAD_DIM])
                p_cmp = sb(ctx, "p_cmp", [P, NSA_N, N_CMP])
                pt_cmp = sb(ctx, "pt_cmp", [N_CMP, NSA_N, P])
                st_cmp = sb(ctx, "st_cmp", [P, 3, NSA_N])
                mx = sb(ctx, "mx", [P, 2, 2])
                nb = sb(ctx, "nb", [P, 2, 2])
                sums = sb(ctx, "sums", [P, 2, 2])
                rec = sb(ctx, "rec", [P, 2, 2])
                e_sink = sb(ctx, "e_sink", [P, 2])
                sems = semaphores(["hg_silu", "hg_gated", "hg_hi", "hg_lo", "aux_in", "hid_done", "hid_turned", "hid_out", "gate_out", "kc_mm", "kc_out", "vc_out", "sc_ready", "sc_step",
                                      "sc_sub", "sc_exp", "pc_done", "pct_ready", "pct_act", "pct_dve", "s_ready",
                                      "nb_ready", "exp_done", "step", "act_step", "p_norm", "pt_ready", "ev_act",
                                      "ev_dve", "pv_done", "o_hi", "o_lo"])

                def c_mat(c):
                    return cst[:, c:c + P]

                units = [(True, 2 * hp + hh, i, 0) for hp in range(2) for i in range(QT) for hh in range(2)]
                units += [(False, 2 * hp + hh, i, max(i - 1, 0)) for hp in range(2) for i in range(QT) for hh in range(2)]
                ev_a, ev_d, na, nd = [], [], 0, 0
                for n, (nsa, *_r) in enumerate(units):
                    na, nd = na + (nsa or n % 2 == 0), nd + (nsa or n % 2 == 1)
                    ev_a.append(na)
                    ev_d.append(nd)

                def halves(h):
                    return slice(64 * (h % 2), 64 * (h % 2) + 64)

                with nc.Block() as block:
                    @block.sync
                    def _(sp):
                        def aux(dst, src):
                            sp.dma_start(dst, src).then_inc(sems["aux_in"], 16)

                        one = bass.ds(layer, 1)
                        aux(cst[:], consts_d[:, 0:C_HG])
                        w2 = cmp_k_w2.rearrange("l (t p) n -> l p t n", p=P)[one, :, :, :].rearrange("a p t n -> (a p) t n")
                        aux(w2k[:, :, 0:64], w2)
                        aux(w2k[:, :, 64:128], w2)
                        aux(w2v[:], cmp_v_w2.rearrange("l (t p) n -> l p t n", p=P)[one, :, :, :].rearrange("a p t n -> (a p) t n"))

                    @block.tensor
                    def _(pe):
                        pe.wait_ge(sems["hid_done"], 1)
                        for q in range(4):
                            mm = pe.transpose(ps[:, 3, 32 * q:32 * q + N_CMP], hid_t[:, q * P:(q + 1) * P], ident[0:N_CMP, 0:N_CMP])
                        mm.then_inc(sems["hid_turned"], 1)
                        pe.wait_ge(sems["aux_in"], 16 * 4)

                        pe.wait_ge(sems["hid_out"], 1)
                        for m in range(2):
                            mm = pe.matmul(ps[:, 4, 0:N_CMP], w2k[:, m, :], hid[:, m, 0:N_CMP], start=(m == 0), stop=(m == 1))
                        mm.then_inc(sems["kc_mm"], 1)
                        for m in range(2):
                            mm = pe.matmul(ps[0:N_CMP, 5, 0:HEAD_DIM], hid[:, 2 + m, 0:N_CMP], w2v[:, m, :], start=(m == 0), stop=(m == 1))
                        mm.then_inc(sems["kc_mm"], 1)

                        pe.wait_ge(sems["kc_out"], 1)
                        for n in range(NSA_N):
                            h, i = 2 * (n % 8 // QT) + n // 8, n % QT
                            o = ps[:, 6 + h % 2, n % 8 * N_CMP:(n % 8 + 1) * N_CMP]
                            pe.matmul(o, proj[halves(h), T_Q + h // 2, i * P:(i + 1) * P], kc[halves(h), 0:N_CMP], start=True, stop=False)
                            mm = pe.matmul(o, ident[:], cst[:, C_CMP + i * N_CMP:C_CMP + (i + 1) * N_CMP], start=False, stop=True)
                        mm.then_inc(sems["sc_ready"], 1)
                        pe.wait_ge(sems["vc_out"], 1)
                        pe.wait_ge(sems["pc_done"], 1)
                        for n in range(NSA_N):
                            mm = pe.transpose(ps[0:N_CMP, 4 + n // 4, (n % 4) * P:(n % 4 + 1) * P], p_cmp[:, n, :], ident[:])
                            if n % 4 == 3:
                                mm.then_inc(sems["pct_ready"], 1)

                        def scores(n):
                            nsa, h, i, k0 = units[n]
                            pe.wait_ge(sems["exp_done"], n + 1)
                            a = 2 * (n % 2)
                            qs = proj[halves(h), (T_HQ if nsa else T_SQ) + h // 2, i * P:(i + 1) * P]
                            for br in range(2 if nsa else 1):
                                ks = T_HF + br if nsa else (T_HQ + 2, T_HF + 2)[h // 2]
                                w_ = (i + 1 - k0) * P
                                pe.matmul(ps[:, a + br, 0:w_], qs, proj[halves(h), ks, k0 * P:(i + 1) * P], start=True, stop=False)
                                if not nsa and i > 0:
                                    pe.matmul(ps[:, a, 0:P], ident[:], c_mat(C_BAND), start=False, stop=False)
                                mm = pe.matmul(ps[:, a + br, w_ - P:w_], ident[:], c_mat(C_CAUSAL), start=False, stop=True)
                            mm.then_inc(sems["s_ready"], 1)

                        def turn(n):
                            nsa, h, i, k0 = units[n]
                            pe.wait_ge(sems["p_norm"], n + 1)
                            if n == 0:
                                pe.wait_ge(sems["pct_act"], 2)
                                pe.wait_ge(sems["pct_dve"], 2)
                            else:
                                pe.wait_ge(sems["ev_act"], ev_a[n - 1] if nsa or n == NSA_N else ev_a[n - 2])
                                pe.wait_ge(sems["ev_dve"], ev_d[n - 1] if nsa or n == NSA_N else ev_d[n - 2])
                            for br in range(2 if nsa else 1):
                                b = 4 + (br if nsa else n % 2)
                                for c in range(i + 1 - k0):
                                    mm = pe.transpose(ps[:, b, c * P:(c + 1) * P], prob[:, n % 2, br, c * P:(c + 1) * P], ident[:])
                            mm.then_inc(sems["pt_ready"], 1)

                        def values(n):
                            nsa, h, i, k0 = units[n]
                            pe.wait_ge(sems["ev_act"], ev_a[n])
                            if ev_d[n]:
                                pe.wait_ge(sems["ev_dve"], ev_d[n])
                            if n % 8 == 0 and n >= NSA_N:
                                pe.wait_ge(sems["o_lo"], n // 8 - 1)
                            o = ps[halves(h), 6 + n // 8 % 2, i * P:(i + 1) * P]
                            todo = [(v_tok[:, br, c, :] if nsa else v_swa[:, k0 + c, (h // 2) * 64:(h // 2) * 64 + 64],
                                     prob_t[:, n % 2, br, c * P:(c + 1) * P])
                                    for br in range(2 if nsa else 1) for c in range(i + 1 - k0)]
                            if nsa:
                                todo.append((vc[:], pt_cmp[:, (h % 2) * 8 + (h // 2) * QT + i, :]))
                            for k, (v, pr) in enumerate(todo):
                                mm = pe.matmul(o, v, pr, start=(k == 0), stop=(k == len(todo) - 1))
                            mm.then_inc(sems["pv_done"], 1)

                        scores(0)
                        for n in range(UNITS + 2):
                            if n + 1 < UNITS:
                                scores(n + 1)
                            if n >= 2:
                                values(n - 2)
                            if 1 <= n <= UNITS:
                                turn(n - 1)

                    def out_hi(act, g):
                        act.wait_ge(sems["pv_done"], 8 * g + 8)
                        act.activation(xhi[:, g, :], ps[:, 6 + g % 2, :], ACT.Copy).then_inc(sems["o_hi"], 1)

                    @block.scalar
                    def _(act):
                        act.sem_inc(sems["exp_done"], 2)
                        act.preload_act_table_set("silu_and_others")
                        act.activation(hid_t[:], ps[0:N_CMP, 7, :], ACT.Silu).then_inc(sems["hid_done"], 1)
                        act.activation(gates[:], gates[:], ACT.Tanh, scale=0.5).then_inc(sems["gate_out"], 1)
                        act.wait_ge(sems["hid_turned"], 1)
                        src = ps[:, 3, 0:P].rearrange("p (q n) -> p q n", n=32)[:, :, 0:N_CMP]
                        act.activation(hid[:, :, 0:N_CMP], src, ACT.Copy).then_inc(sems["hid_out"], 1)
                        for h in range(HGRN_HEADS):
                            act.activation(proj[:, T_HG + h, :], proj[:, T_HG + h, :], ACT.Silu).then_inc(sems["hg_silu"], 1)
                        act.wait_ge(sems["kc_mm"], 1)
                        act.activation(kc[:, 0:N_CMP], ps[:, 4, 0:N_CMP], ACT.Copy).then_inc(sems["kc_out"], 1)
                        for h in range(HGRN_HEADS):
                            act.wait_ge(sems["hg_gated"], h + 1)
                            act.activation(xhi[:, 4 + h, :], proj[:, T_HI + h, :], ACT.Copy).then_inc(sems["hg_hi"], 1)
                        act.preload_act_table_set("natural_log_exp_and_others")
                        act.wait_ge(sems["sc_sub"], 2)
                        act.activation(p_cmp[:], p_cmp[:], ACT.Exp, scale=SCALE).then_inc(sems["sc_exp"], 1)
                        for b in (0, 2):
                            act.wait_ge(sems["pct_ready"], b + 1)
                            act.activation(pt_cmp[:, 4 * b:4 * b + 4, :].rearrange("p a n -> p (a n)"), ps[0:N_CMP, 4 + b, :],
                                           ACT.Copy).then_inc(sems["pct_act"], 1)

                        steps = 0
                        for n in range(UNITS + 2):
                            if n < UNITS:
                                nsa, h, i, k0 = units[n]
                                w_ = (i + 1 - k0) * P
                                act.wait_ge(sems["nb_ready"], n + 1)
                                if n >= 2:
                                    act.wait_ge(sems["pt_ready"], n - 1)
                                if not nsa:
                                    steps += 1
                                    act.activation(e_sink[:, n % 2:n % 2 + 1], sinks[:, bass.ds(layer * SWA_HEADS + h, 1)], ACT.Exp,
                                                   bias=nb[:, n % 2, 0:1]).then_inc(sems["act_step"], 1)
                                for br in range(2 if nsa else 1):
                                    e = act.activation(prob[:, n % 2, br, 0:w_], ps[:, 2 * (n % 2) + br, 0:w_], ACT.Exp, scale=SCALE,
                                                       bias=nb[:, n % 2, br:br + 1], accum_out=sums[:, n % 2, br:br + 1])
                                e.then_inc(sems["exp_done"], 1)
                            if n >= 2 and (units[n - 2][0] or n % 2 == 0):
                                m = n - 2
                                nsa, h, i, k0 = units[m]
                                w_ = (i + 1 - k0) * P
                                act.wait_ge(sems["pt_ready"], m + 1)
                                if m >= 2:
                                    act.wait_ge(sems["pv_done"], m - 1)
                                act.activation(prob_t[:, m % 2, 0, 0:w_], ps[:, 4 + (0 if nsa else m % 2), 0:w_], ACT.Copy).then_inc(sems["ev_act"], 1)
                            if n >= 3 and (n - 3) % 8 == 7:
                                out_hi(act, (n - 3) // 8)
                        out_hi(act, UNITS // 8 - 1)

                    @block.vector
                    def _(dve):
                        for h in range(HGRN_HEADS):
                            dve.wait_ge(sems["hg_silu"], h + 1)
                            o = proj[:, T_HI + h, :]
                            dve.tensor_tensor(o, o, proj[:, T_HG + h, :], ALU.mult).then_inc(sems["hg_gated"], 1)
                        for h in range(HGRN_HEADS):
                            dve.wait_ge(sems["hg_hi"], h + 1)
                            dve.tensor_tensor(xlo[:, 4 + h, :], proj[:, T_HI + h, :], xhi[:, 4 + h, :],
                                              ALU.subtract).then_inc(sems["hg_lo"], 1)

                        dve.wait_ge(sems["kc_mm"], 2)
                        dve.tensor_copy(vc[:], ps[0:N_CMP, 5, 0:HEAD_DIM]).then_inc(sems["vc_out"], 1)
                        st = [0]

                        def then(ins):
                            ins.then_inc(sems["step"], 1)
                            st[0] += 1
                            dve.wait_ge(sems["step"], st[0])
                        dve.wait_ge(sems["gate_out"], 1)
                        then(dve.tensor_scalar(gates[:], gates[:], 0.5, 0.5, ALU.mult, ALU.add))
                        dve.wait_ge(sems["aux_in"], 16 * 4)
                        then(dve.tensor_scalar(anyv[:], cst[:, C_CMP:C_CMP + 1], -1.0, None, ALU.is_ge))
                        g0 = gates[:, 0, :].rearrange("p (h b) -> p b h", b=3)[:, 0]
                        then(dve.tensor_scalar(g0, g0, anyv[:, 0:1], None, ALU.mult))
                        dve.wait_ge(sems["sc_ready"], 1)
                        wide = [P, 8, N_CMP]
                        for b in range(2):
                            sc = ps[:, 6 + b, 0:8 * N_CMP].rearrange("p (u n) -> p u n", n=N_CMP)
                            m8 = st_cmp[:, 0, 8 * b:8 * b + 8]
                            then(dve.tensor_reduce(m8, sc, AX.X, ALU.max))
                            dve.tensor_tensor(p_cmp[:, 8 * b:8 * b + 8, :], sc, m8[:, :, None].broadcast_to(wide),
                                              ALU.subtract).then_inc(sems["sc_sub"], 1)
                        dve.wait_ge(sems["sc_exp"], 1)
                        then(dve.tensor_reduce(st_cmp[:, 1, :], p_cmp[:], AX.X, ALU.add))
                        then(dve.reciprocal(st_cmp[:, 2, :], st_cmp[:, 1, :]))
                        for b in range(2):
                            gc = gates[:, :, :].rearrange("p i (g s b) -> p s b g i", s=2, b=3)[:, b, 0]
                            rc = st_cmp[:, 2, 8 * b:8 * b + 8].rearrange("p (g i) -> p g i", i=QT)
                            then(dve.tensor_tensor(rc, rc, gc, ALU.mult))
                        dve.tensor_tensor(p_cmp[:], p_cmp[:], st_cmp[:, 2, :, None].broadcast_to([P, NSA_N, N_CMP]),
                                          ALU.mult).then_inc(sems["pc_done"], 1)
                        for b in (1, 3):
                            dve.wait_ge(sems["pct_ready"], b + 1)
                            dve.tensor_copy(pt_cmp[:, 4 * b:4 * b + 4, :].rearrange("p a n -> p (a n)"), ps[0:N_CMP, 4 + b, :]).then_inc(sems["pct_dve"], 1)

                        def row_max(n):
                            nsa, h, i, k0 = units[n]
                            w_ = (i + 1 - k0) * P
                            br = 2 if nsa else 1
                            dve.wait_ge(sems["s_ready"], n + 1)
                            then(dve.tensor_reduce(mx[:, n % 2, 0:br], ps[:, 2 * (n % 2):2 * (n % 2) + br, 0:w_], AX.X, ALU.max))
                            if nsa:
                                dve.tensor_scalar(nb[:, n % 2, 0:br], mx[:, n % 2, 0:br], -SCALE, None, ALU.mult).then_inc(sems["nb_ready"], 1)
                            else:
                                then(dve.tensor_scalar(mx[:, n % 2, 0:1], mx[:, n % 2, 0:1], SCALE,
                                                       sinks[:, bass.ds(layer * SWA_HEADS + h, 1)], ALU.mult, ALU.max))
                                dve.tensor_scalar(nb[:, n % 2, 0:1], mx[:, n % 2, 0:1], -1.0, None, ALU.mult).then_inc(sems["nb_ready"], 1)

                        def normalise(n):
                            nsa, h, i, k0 = units[n]
                            w_ = (i + 1 - k0) * P
                            br = 2 if nsa else 1
                            dve.wait_ge(sems["exp_done"], n + 3)
                            if not nsa:
                                then(dve.tensor_tensor(sums[:, n % 2, 0:1], sums[:, n % 2, 0:1], e_sink[:, n % 2:n % 2 + 1], ALU.add))
                            then(dve.reciprocal(rec[:, n % 2, 0:br], sums[:, n % 2, 0:br]))
                            if nsa:
                                then(dve.tensor_tensor(rec[:, n % 2, :], rec[:, n % 2, :], gates[:, i, 3 * h + 1:3 * h + 3], ALU.mult))
                            for b in range(br):
                                d = dve.tensor_scalar(prob[:, n % 2, b, 0:w_], prob[:, n % 2, b, 0:w_], rec[:, n % 2, b:b + 1], None, ALU.mult)
                            d.then_inc(sems["p_norm"], 1)

                        def out_lo(g):
                            dve.wait_ge(sems["o_hi"], g + 1)
                            dve.tensor_tensor(xlo[:, g, :], ps[:, 6 + g % 2, :], xhi[:, g, :], ALU.subtract).then_inc(sems["o_lo"], 1)

                        for n in range(UNITS + 2):
                            if n < UNITS:
                                row_max(n)
                            if n >= 2 and (units[n - 2][0] or (n - 2) % 2 == 1):
                                m = n - 2
                                nsa, h, i, k0 = units[m]
                                w_ = (i + 1 - k0) * P
                                dve.wait_ge(sems["pt_ready"], m + 1)
                                if m >= 2:
                                    dve.wait_ge(sems["pv_done"], m - 1)
                                dve.tensor_copy(prob_t[:, m % 2, 1 if nsa else 0, 0:w_], ps[:, 5, 0:w_]).then_inc(sems["ev_dve"], 1)
                            if 1 <= n <= UNITS:
                                normalise(n - 1)
                            if n >= 3 and (n - 3) % 8 == 7:
                                out_lo((n - 3) // 8)
                        out_lo(UNITS // 8 - 1)
                clear(sems)

        ORDER = [T_HF, T_HQ, T_HI, T_HF + 1, T_HQ + 1, T_HI + 1, T_HF + 2, T_HQ + 2, T_HI + 2, T_HF + 3, T_HQ + 3,
                 T_HI + 3, T_CMP, T_Q, T_Q + 1, T_SLC, T_WIN, T_SQ, T_SQ + 1, T_SK, T_SV, T_GATE, T_HG, T_HG + 1,
                 T_HG + 2, T_HG + 3]
        FIRST_STEP = 6
        FIRST_ROPE = FIRST_STEP + HGRN_HEADS * QT
        CMP_CHUNKS = 4
        ROPE = [("q", T_Q, 0, T_HQ), ("q", T_Q + 1, 0, T_HQ + 1), ("k", T_SLC, 0, T_HF), ("k", T_WIN, 0, T_HF + 1),
                ("q", T_SQ, 0, T_SQ), ("q", T_SQ + 1, 0, T_SQ + 1), ("k", T_SK, 0, T_HQ + 2), ("k", T_SK, 64, T_HF + 2)]
        rope_pool = [1, 2, 2, 2, 3, 4, 4, 4]
        BLK = (T_HQ + 3, T_HF + 3)

        def project_hgrn2(layer, proj, v_sel, v_swa, gates):
            stage[0] = "hgrn"
            H, STEPS = HGRN_HEADS, HGRN_HEADS * QT
            with scope() as ctx:
                w = Weights(ctx, DT)
                hmask = sb(ctx, "hmask", [P, (LEVELS + 1) * P])
                reset = sb(ctx, "reset", [P, SEQ])
                lsp = sb(ctx, "lsp", [P, SEQ])
                lsg = sb(ctx, "lsg", [P, SEQ])
                karg = sb(ctx, "karg", [P, SEQ])
                logf = sb(ctx, "logf", [P, SEQ])
                cum = sb(ctx, "cum", [P, SEQ])
                lev = sb(ctx, "lev", [P, 2, LEVELS, SEQ])
                qd = sb(ctx, "qd", [P, 2, SEQ])
                kd = sb(ctx, "kd", [P, 2, SEQ])
                dec = sb(ctx, "dec", [P, 2, QT])
                v_tok = sb(ctx, "v_tok", [P, 2, QT, P])
                att = sb(ctx, "att", [P, (LEVELS + 1) * P])
                kd_t = sb(ctx, "kd_t", [P, 2, P])
                state = sb(ctx, "state", [P, 2, P])
                var = sb(ctx, "var", [P, SEQ])
                rms = sb(ctx, "rms", [P, SEQ])
                tmp = sb(ctx, "tmp", [P, SEQ])
                rotm = sb(ctx, "rotm", [P, 3 * P])
                pos2 = tmp[0:CMP_LEN, 0:P]
                pos_t = sb(ctx, "pos_t", [P, CMP_LEN])
                cos, sin, sin_part = lsp, lsg, (karg, logf)
                ngc = sb(ctx, "ngc", [P, HGRN_HEADS])
                hgc = sb(ctx, "hgc", [P, 3, HGRN_HEADS])
                sems = semaphores(STREAM + ["out_act", "out_dve", "aux_in", "reset_done", "step", "act_step", "a0", "d0",
                                            "a1", "d1", "d2", "p2", "a2", "d3", "p3", "c_mm", "att_done", "b4_mm",
                                            "b4_out", "st_mm", "st_out", "pv_done", "o_raw", "sq_done", "ms_mm",
                                            "ms_out", "rs_act", "o_done", "mask_in", "rope_in", "pos_turned", "pos_out",
                                            "blk_done", "rope_mm", "rope_cos", "rope_step", "rope_out", "cmp_mm",
                                            "v_turned", "v_out"], slots=[("raw_in", RAW)])

                def projected(eng, tile):
                    s = ORDER.index(tile)
                    eng.wait_ge(sems["out_dve" if s % 2 else "out_act"], s // 2 + 1)

                def pairs(t, lv, side):
                    m = 1 << lv
                    return t.rearrange("p (b s m) -> p s b m", s=2, m=m)[:, side]

                def last_of(t, lv):
                    m = 1 << lv
                    v = t.rearrange("p (b s m) -> p s b m", s=2, m=m)[:, 0, :, m - 1:m]
                    return v.broadcast_to([P, SEQ // (2 * m), m])

                def b4_before_v(h):
                    return 4 * h

                def b4_before_k(h, c):
                    return 4 * h + 1 + c

                def blocks_of(kv):
                    return proj[:, BLK[kv], :].rearrange("p (l n) -> p l n", n=32)

                def squares_step(h):
                    return min(QT * h + 5, STEPS + 1)

                def w_cmp(c):
                    return w.raw[:, c % RAW].rearrange("p k n -> p (k n)").rearrange("p (a m) -> p a m", m=CMP_HID)

                with nc.Block() as block:
                    @block.sync
                    def _(sp):
                        for s, tile in enumerate(ORDER):
                            c0 = tile * P if tile < T_SQ else NSA_COLS + (tile - T_SQ) * P
                            load_chunk(sp, sems, w.raw, s, s % RAW, cols_of(w_in, layer, 0, DT, c0), DT)
                            if s == 3:
                                sp.dma_start(hmask[:], consts_d[:, C_HG:C_END]).then_inc(sems["mask_in"], 16)
                                for half in (0, 64):
                                    sp.dma_start(pos2[:, half:half + 64], cmp_pos[bass.ds(layer, 1), :, :].rearrange(
                                        "a l d -> (a l) d")).then_inc(sems["aux_in"], 16)
                                sp.dma_start(rotm[:], consts_d[:, C_ROT:C_ROT + 3 * P]).then_inc(sems["aux_in"], 16)
                            if s == 20:
                                sp.wait_ge(sems["d1"], H)
                                sp.wait_ge(sems["a1"], H)
                                sp.dma_start(cos[:], rope_d[:, 0:SEQ]).then_inc(sems["rope_in"], 16)
                                sp.dma_start(sin[:], rope_d[:, SEQ:2 * SEQ]).then_inc(sems["rope_in"], 16)
                        for j in range(2 * CMP_CHUNKS):
                            c = N_PM + j
                            sp.wait_ge(sems["lo_done"], min(c, N_PM + RAW - 1) + 1)
                            if j >= RAW:
                                sp.wait_ge(sems["cmp_mm"], j - RAW + 1)
                            src = (cmp_k_w1, cmp_v_w1)[j // CMP_CHUNKS].rearrange("l (t p) n -> l p t n", p=P)
                            t = j % CMP_CHUNKS * 4
                            sp.dma_start(w_cmp(c), src[bass.ds(layer, 1), :, t:t + 4, :].rearrange("a p t n -> (a p) t n")
                                         ).then_inc(sems["raw_in"][c % RAW], 16)

                    @block.tensor
                    def _(pe):
                        pe.sem_inc(sems["mm_done"], SPLIT)

                        def values_turned(h):
                            if b4_before_v(h):
                                pe.wait_ge(sems["b4_out"], b4_before_v(h))
                            projected(pe, T_HI + h)
                            for c in range(QT):
                                mm = pe.transpose(ps[:, 4, c * P:(c + 1) * P], proj[:, T_HI + h, c * P:(c + 1) * P], ident[:])
                            mm.then_inc(sems["b4_mm"], 1)

                        def products(n):
                            h, c, tok = n // QT, n % QT, slice(n % QT * P, n % QT * P + P)
                            if c == 0:
                                pe.wait_ge(sems["d3"], h + 1)
                                pe.wait_ge(sems["p3"], h + 1)
                            if n:
                                pe.wait_ge(sems["att_done"], n)
                            for lv in range(LEVELS + 1):
                                o = ps[:, 2 + lv // 4, (lv % 4) * P:(lv % 4 + 1) * P]
                                if lv < LEVELS:
                                    both = lev[:, h % 2, lv, tok]
                                    mm = pe.matmul(o, both, both, start=True, stop=True)
                                else:
                                    mm = pe.matmul(o, proj[:, T_HF + h, tok], proj[:, T_HQ + h, tok], start=True, stop=True)
                            mm.then_inc(sems["c_mm"], 1)
                            if c < QT - 1:
                                pe.wait_ge(sems["b4_out"], b4_before_k(h, c))
                                pe.transpose(ps[:, 4, 0:P], kd[:, h % 2, tok], ident[:]).then_inc(sems["b4_mm"], 1)
                            elif h + 1 < H:
                                values_turned(h + 1)

                        def outputs(n):
                            h, c, tok = n // QT, n % QT, slice(n % QT * P, n % QT * P + P)
                            if c < QT - 1:
                                pe.wait_ge(sems["b4_out"], b4_before_k(h, c) + 1)
                                if 3 * h + c:
                                    pe.wait_ge(sems["st_out"], 3 * h + c)
                                pe.matmul(ps[:, 5, 0:P], kd_t[:, n % 2, :], v_tok[:, h % 2, c, :], start=True,
                                          stop=True).then_inc(sems["st_mm"], 1)
                            if c == 0 and h:
                                pe.wait_ge(sems["o_raw"], h)
                            if c > 0:
                                pe.wait_ge(sems["st_out"], 3 * h + c)
                                pe.matmul(ps[:, 6, tok], state[:, (c - 1) % 2, :], qd[:, h % 2, tok], start=True, stop=False)
                            pe.wait_ge(sems["att_done"], n + 1)
                            for lv in range(LEVELS + 1):
                                mm = pe.matmul(ps[:, 6, tok], v_tok[:, h % 2, c, :], att[:, lv * P:(lv + 1) * P],
                                               start=(c == 0 and lv == 0), stop=(lv == LEVELS))
                            mm.then_inc(sems["pv_done"], 1)

                        def rotate(r):
                            a, b = 2 + 2 * (r % 2), 3 + 2 * (r % 2)
                            kind, src, half, _dst = ROPE[r]
                            if r == 0:
                                pe.wait_ge(sems["att_done"], STEPS)
                            if r == 1:
                                pe.wait_ge(sems["b4_out"], 4 * H)
                                pe.wait_ge(sems["st_out"], 3 * H)
                            if r >= 2:
                                pe.wait_ge(sems["rope_out"], r - 1)
                            projected(pe, src)
                            if kind == "q":
                                pe.matmul(ps[:, a, :], rotm[:, 0:P], proj[:, src, :], start=True, stop=True).then_inc(sems["rope_mm"], 1)
                            else:
                                rows_ = slice(half, half + 64)
                                pe.matmul(ps[:, a, :], rotm[rows_, 2 * P:3 * P], proj[rows_, src, :], start=True, stop=True)
                                pe.matmul(ps[:, b, :], rotm[rows_, P:2 * P], proj[rows_, src, :], start=True,
                                          stop=True).then_inc(sems["rope_mm"], 1)

                        for s in range(N_PM):
                            if s >= 2:
                                pe.wait_ge(sems["out_dve" if s % 2 else "out_act"], s // 2)
                            multiply(pe, sems, w, s, s % RAW, DT, s % 2, lambda k: xhi[:, k, :], lambda k: xlo[:, k, :])
                            n = s - FIRST_STEP
                            if s == 4:
                                pe.wait_ge(sems["aux_in"], 16 * 3)
                                pe.transpose(ps[:, 7, 0:CMP_LEN], pos2, ident[0:CMP_LEN, 0:CMP_LEN]).then_inc(sems["pos_turned"], 1)
                            if n == -1:
                                values_turned(0)
                            if 1 <= n <= STEPS:
                                outputs(n - 1)
                            for h in range(H):
                                if n == squares_step(h) + 1:
                                    pe.wait_ge(sems["sq_done"], h + 1)
                                    pe.wait_ge(sems["pos_out"], 1)
                                    if h:
                                        pe.wait_ge(sems["ms_out"], h)
                                    pe.matmul(ps[:, 7, :], mean_w[:], rms[:], start=True, stop=True).then_inc(sems["ms_mm"], 1)
                            if 0 <= n < STEPS:
                                products(n)
                            if s >= FIRST_ROPE:
                                rotate(2 * (s - FIRST_ROPE))
                                rotate(2 * (s - FIRST_ROPE) + 1)

                        pe.wait_ge(sems["blk_done"], 2)
                        pe.wait_ge(sems["ms_out"], H)
                        for j in range(2 * CMP_CHUNKS):
                            kv, c = j // CMP_CHUNKS, N_PM + j
                            pe.wait_ge(sems["raw_in"][c % RAW], 16 * (c // RAW + 1))
                            for k in range(4):
                                l = j % CMP_CHUNKS * 4 + k
                                mm = pe.matmul(ps[0:N_CMP, 7, kv * CMP_HID:(kv + 1) * CMP_HID], blocks_of(kv)[:, l, 0:N_CMP],
                                               w_cmp(c)[:, k, :], start=(l == 0), stop=(l == 4 * CMP_CHUNKS - 1))
                            mm.then_inc(sems["cmp_mm"], 1)

                        pe.wait_ge(sems["rope_out"], 8)
                        for n, t in enumerate((T_SLC, T_WIN, T_SV, T_GATE)):
                            projected(pe, t)
                            for c in range(QT):
                                mm = pe.transpose(ps[:, 2 + n, c * P:(c + 1) * P], proj[:, t, c * P:(c + 1) * P], ident[:])
                            mm.then_inc(sems["v_turned"], 1)

                    @block.scalar
                    def _(act):
                        st = [0]
                        act.preload_act_table_set("natural_log_exp_and_others")

                        def then(ins):
                            ins.then_inc(sems["act_step"], 1)
                            st[0] += 1
                            act.wait_ge(sems["act_step"], st[0])

                        def part(h, k):
                            if k == 0:
                                projected(act, T_HF + h)
                                if h:
                                    act.wait_ge(sems["d0"], h)
                                then(act.activation(lsp[:], proj[:, T_HF + h, :], ACT.Abs))
                                then(act.activation(lsp[:], lsp[:], ACT.Exp, scale=-1.0))
                                act.activation(lsp[:], lsp[:], ACT.Ln, bias=1.0).then_inc(sems["a0"], 1)
                            if k == 1:
                                act.wait_ge(sems["d0"], h + 1)
                                act.activation(proj[:, T_HF + h, :], karg[:], ACT.Exp, scale=-1.0, bias=hgc[:, 1, h:h + 1])
                                then(act.activation(lsg[:], lsg[:], ACT.Abs))
                                then(act.activation(lsg[:], lsg[:], ACT.Exp, scale=-1.0))
                                act.activation(lsg[:], lsg[:], ACT.Ln, bias=1.0).then_inc(sems["a1"], 1)
                            if k == 2:
                                act.wait_ge(sems["d2"], h + 1)
                                act.wait_ge(sems["p2"], h + 1)
                                l2 = lev[:, h % 2].rearrange("p l n -> p (l n)")
                                act.activation(l2, l2, ACT.Exp)
                                act.activation(kd[:, h % 2, :], kd[:, h % 2, :], ACT.Exp)
                                act.activation(dec[:, h % 2, :], cum[:, :].rearrange("p (c n) -> p c n", n=P)[:, :, P - 1], ACT.Exp)
                                act.activation(qd[:, h % 2, :], cum[:], ACT.Exp).then_inc(sems["a2"], 1)

                        def values_out(h):
                            act.wait_ge(sems["b4_mm"], b4_before_v(h) + 1)
                            if h >= 2:
                                act.wait_ge(sems["pv_done"], QT * (h - 1))
                            act.activation(v_tok[:, h % 2].rearrange("p c d -> p (c d)"), ps[:, 4, :], ACT.Copy).then_inc(sems["b4_out"], 1)

                        split_hi(act, sems, w, 0, 0, DT)
                        for s in range(N_PM + 1):
                            n, h, c = s - FIRST_STEP, (s - FIRST_STEP) // QT, (s - FIRST_STEP) % QT
                            if s + 1 < N_PM:
                                split_hi(act, sems, w, s + 1, (s + 1) % RAW, DT)
                            if s % 2 and s <= N_PM:
                                act.wait_ge(sems["mm_done"], s - 1 + SPLIT + 1)
                                act.activation(proj[:, ORDER[s - 1], :], ps[:, 0, :], ACT.Copy).then_inc(sems["out_act"], 1)
                            if -4 <= n < STEPS and c < 3 and h + 1 < H:
                                part(h + 1, c)
                            if n == -1:
                                values_out(0)
                            if 0 <= n < STEPS and c < QT - 1:
                                act.wait_ge(sems["b4_mm"], b4_before_k(h, c) + 1)
                                if 3 * h + c >= 2:
                                    act.wait_ge(sems["st_mm"], 3 * h + c - 1)
                                act.activation(kd_t[:, n % 2, :], ps[:, 4, 0:P], ACT.Copy).then_inc(sems["b4_out"], 1)
                            elif 0 <= n < STEPS - 1:
                                values_out(h + 1)
                            for g in range(H):
                                if n == squares_step(g):
                                    act.wait_ge(sems["o_raw"], g + 1)
                                    if g:
                                        act.wait_ge(sems["o_done"], g)
                                    act.activation(rms[:], proj[:, T_HI + g, :], ACT.Square).then_inc(sems["sq_done"], 1)
                                if n == squares_step(g) + 1:
                                    act.wait_ge(sems["ms_out"], g + 1)
                                    then(act.activation(rms[:], var[:], ACT.Ln))
                                    act.activation(rms[:], rms[:], ACT.Exp, scale=-0.5).then_inc(sems["rs_act"], 1)
                        for n in range(2):
                            act.wait_ge(sems["v_turned"], n + 1)
                            src = ps[:, 2 + n, :].rearrange("p (c d) -> p c d", d=P)[:, :, HEAD_DIM:2 * HEAD_DIM]
                            act.activation(v_sel[:, n], src, ACT.Copy)
                        act.wait_ge(sems["v_turned"], 4)
                        src = ps[:, 5, :].rearrange("p (c d) -> p c d", d=P)[:, :, 0:3 * NSA_HEADS]
                        act.activation(gates[:], src, ACT.Copy)

                    @block.vector
                    def _(dve):
                        dve.sem_inc(sems["lo_done"], RAW)
                        st = [0]

                        def then(ins):
                            ins.then_inc(sems["step"], 1)
                            st[0] += 1
                            dve.wait_ge(sems["step"], st[0])

                        def part(h, k):
                            z, hp = proj[:, T_HF + h, :], h % 2
                            if k == 0:
                                dve.wait_ge(sems["a0"], h + 1)
                                dve.scalar_tensor_tensor(out=karg[:], in0=z, scalar=0.0, in1=lsp[:], op0=ALU.max, op1=ALU.add)
                                then(dve.scalar_tensor_tensor(out=lsg[:], in0=z, scalar=0.0, in1=lsp[:], op0=ALU.min, op1=ALU.subtract))
                                dve.tensor_scalar(logf[:], lsg[:], hgc[:, 1, h:h + 1], hgc[:, 0, h:h + 1], ALU.add, ALU.max)
                                dve.tensor_scalar(lsg[:], lsg[:], hgc[:, 2, h:h + 1], None, ALU.add).then_inc(sems["d0"], 1)
                            if k == 1:
                                dve.wait_ge(sems["a1"], h + 1)
                                dve.wait_ge(sems["reset_done"], 2)
                                then(dve.tensor_tensor(logf[:], logf[:], lsg[:], ALU.add))
                                if h:
                                    dve.wait_ge(sems["a2"], h)
                                    dve.wait_ge(sems["p2"], h)
                                dve.tensor_tensor_scan(cum[:], reset[:], logf[:], 0.0, ALU.mult, ALU.add).then_inc(sems["d1"], 1)
                            if k == 2:
                                dve.wait_ge(sems["d1"], h + 1)
                                if h >= 2:
                                    dve.wait_ge(sems["pv_done"], QT * (h - 1))
                                for lv in range(LEVELS):
                                    dve.tensor_tensor(pairs(lev[:, hp, lv, :], lv, 1), pairs(cum[:], lv, 1),
                                                      last_of(cum[:], lv), ALU.subtract)
                                cv = cum[:, :].rearrange("p (c n) -> p c n", n=P)
                                dve.tensor_tensor(kd[:, hp, :].rearrange("p (c n) -> p c n", n=P), cv[:, :, P - 1:P].broadcast_to([P, QT, P]),
                                                  cv, ALU.subtract).then_inc(sems["d2"], 1)
                            if k == 3:
                                dve.wait_ge(sems["a2"], h + 1)
                                projected(dve, T_HQ + h)
                                for lv in range(LEVELS):
                                    r = pairs(lev[:, hp, lv, :], lv, 1)
                                    d = dve.tensor_tensor(r, r, pairs(proj[:, T_HQ + h, :], lv, 1), ALU.mult)
                                d.then_inc(sems["d3"], 1)

                        def rotate(r):
                            kind, src, half, dst = ROPE[r]
                            a, b = 2 + 2 * (r % 2), 3 + 2 * (r % 2)
                            dst, part_ = proj[:, dst, :], sin_part[r % 2][:]
                            if r == 0:
                                dve.wait_ge(sems["rope_in"], 32)
                            dve.wait_ge(sems["rope_mm"], r + 1)
                            if kind == "q":
                                dve.tensor_tensor(part_, ps[:, a, :], sin[:], ALU.mult).then_inc(sems["rope_step"], 1)
                                dve.wait_ge(sems["rope_cos"], rope_pool[r])
                            else:
                                dve.tensor_tensor(dst, ps[:, b, :], cos[:], ALU.mult)
                                dve.tensor_tensor(part_, ps[:, a, :], sin[:], ALU.mult).then_inc(sems["rope_step"], 1)
                            dve.wait_ge(sems["rope_step"], r + 1)
                            dve.tensor_tensor(dst, dst, part_, ALU.add).then_inc(sems["rope_out"], 1)

                        def cut_blocks(kv):
                            if kv == 0:
                                dve.wait_ge(sems["pos_out"], 1)
                                dve.wait_ge(sems["c_mm"], STEPS)
                                projected(dve, T_CMP)
                            rows_ = slice(64 * kv, 64 * kv + 64)
                            full = proj[rows_, T_CMP, :]
                            for s_ in range(2):
                                for hi_l in range(2):
                                    src = (full[:, 16 * hi_l:16 * hi_l + 16 * N_CMP].rearrange("p (n l s) -> p s l n", l=8, s=2)[:, s_])
                                    pos = pos_t[rows_, 16 * hi_l:16 * hi_l + 16].rearrange("p (l s) -> p s l", s=2)[:, s_]
                                    d = dve.tensor_tensor(blocks_of(kv)[64 * s_:64 * s_ + 64, 8 * hi_l:8 * hi_l + 8, 0:N_CMP], src,
                                                          pos[:, :, None].broadcast_to([64, 8, N_CMP]), ALU.add)
                            d.then_inc(sems["blk_done"], 1)

                        dve.tensor_copy(ngc[:], par[:, bass.ds(layer * HGRN_HEADS + PNG, HGRN_HEADS)])
                        src = hgp[:, bass.ds(layer, 1), :, :].rearrange("p a k h -> p (a k h)")
                        then(dve.tensor_copy(hgc[:, :, :].rearrange("p k h -> p (k h)"), src))
                        split_lo(dve, sems, w, 0, 0, DT)
                        for s in range(N_PM + 1):
                            n, h, c = s - FIRST_STEP, (s - FIRST_STEP) // QT, (s - FIRST_STEP) % QT
                            if s + 1 < N_PM:
                                split_lo(dve, sems, w, s + 1, (s + 1) % RAW, DT)
                            if s % 2 == 0 and s >= 2:
                                dve.wait_ge(sems["mm_done"], s - 1 + SPLIT + 1)
                                dve.tensor_copy(proj[:, ORDER[s - 1], :], ps[:, 1, :]).then_inc(sems["out_dve"], 1)
                            if n >= 1 and (n - 1) % QT < QT - 1 and n <= STEPS:
                                g, b = (n - 1) // QT, (n - 1) % QT
                                dve.wait_ge(sems["st_mm"], 3 * g + b + 1)
                                if b == 0:
                                    if g:
                                        dve.wait_ge(sems["pv_done"], n - 1)
                                    dve.tensor_copy(state[:, 0, :], ps[:, 5, 0:P]).then_inc(sems["st_out"], 1)
                                else:
                                    dve.wait_ge(sems["pv_done"], n - 1)
                                    dve.wait_ge(sems["st_out"], 3 * g + b)
                                    dve.scalar_tensor_tensor(out=state[:, b % 2, :], in0=state[:, (b - 1) % 2, :],
                                                             scalar=dec[:, g % 2, b:b + 1], in1=ps[:, 5, 0:P],
                                                             op0=ALU.mult, op1=ALU.add).then_inc(sems["st_out"], 1)
                            if -4 <= n < STEPS and h + 1 < H:
                                part(h + 1, c)
                            if n == 0:
                                dve.wait_ge(sems["mask_in"], 16)
                            if 0 <= n < STEPS:
                                dve.wait_ge(sems["c_mm"], n + 1)
                                if n:
                                    dve.wait_ge(sems["pv_done"], n)
                                both = ps[:, 2:4, :].rearrange("p a n -> p (a n)")
                                dve.tensor_tensor(att[:], both, hmask[:], ALU.mult).then_inc(sems["att_done"], 1)
                            for g in range(H):
                                if n == QT * g + QT:
                                    dve.wait_ge(sems["pv_done"], n)
                                    dve.tensor_copy(proj[:, T_HI + g, :], ps[:, 6, :]).then_inc(sems["o_raw"], 1)
                                if n == squares_step(g) + 1:
                                    dve.wait_ge(sems["ms_mm"], g + 1)
                                    dve.tensor_scalar(var[:], ps[:, 7, :], float(D_MODEL // P), RMS_EPS, ALU.mult, ALU.add).then_inc(sems["ms_out"], 1)
                                if n == squares_step(g) + 2:
                                    o = proj[:, T_HI + g, :]
                                    dve.wait_ge(sems["rs_act"], g + 1)
                                    then(dve.tensor_tensor(tmp[:], var[:], rms[:], ALU.mult))
                                    then(dve.tensor_tensor(tmp[:], tmp[:], rms[:], ALU.mult))
                                    then(dve.tensor_scalar(tmp[:], tmp[:], -0.5, 1.5, ALU.mult, ALU.add))
                                    then(dve.tensor_tensor(tmp[:], tmp[:], rms[:], ALU.mult))
                                    dve.scalar_tensor_tensor(out=o, in0=tmp[:], scalar=ngc[:, g:g + 1], in1=o,
                                                             op0=ALU.mult, op1=ALU.mult).then_inc(sems["o_done"], 1)
                            if s == 5:
                                dve.wait_ge(sems["pos_turned"], 1)
                                dve.tensor_copy(pos_t[:], ps[:, 7, 0:CMP_LEN]).then_inc(sems["pos_out"], 1)
                            if FIRST_ROPE <= s < N_PM:
                                rotate(2 * (s - FIRST_ROPE))
                                rotate(2 * (s - FIRST_ROPE) + 1)
                            if s in (FIRST_ROPE + 1, FIRST_ROPE + 2):
                                cut_blocks(s - FIRST_ROPE - 1)
                        dve.wait_ge(sems["v_turned"], 3)
                        dve.tensor_copy(v_swa[:, :, :].rearrange("p c d -> p (c d)"), ps[:, 4, :])

                    @block.gpsimd
                    def _(pool):
                        pool.memset(reset[:], 1.0).then_inc(sems["reset_done"], 1)
                        pool.wait_ge(sems["reset_done"], 1)
                        pool.memset(reset[:, :].rearrange("p (c n) -> p c n", n=P)[:, :, 0:1], 0.0).then_inc(sems["reset_done"], 1)
                        for h in range(H):
                            hp = h % 2
                            pool.wait_ge(sems["d1"], h + 1)
                            if h >= 2:
                                pool.wait_ge(sems["pv_done"], QT * (h - 1))
                            for lv in range(LEVELS):
                                d = pool.tensor_tensor(pairs(lev[:, hp, lv, :], lv, 0), last_of(cum[:], lv),
                                                       pairs(cum[:], lv, 0), ALU.subtract)
                            d.then_inc(sems["p2"], 1)
                            pool.wait_ge(sems["a2"], h + 1)
                            for lv in range(LEVELS):
                                left = pairs(lev[:, hp, lv, :], lv, 0)
                                pool.tensor_tensor(left, left, pairs(proj[:, T_HF + h, :], lv, 0), ALU.mult)
                            pool.tensor_tensor(kd[:, hp, :], kd[:, hp, :], proj[:, T_HF + h, :], ALU.mult)
                            projected(pool, T_HQ + h)
                            pool.tensor_tensor(qd[:, hp, :], qd[:, hp, :], proj[:, T_HQ + h, :], ALU.mult).then_inc(sems["p3"], 1)
                        pool.wait_ge(sems["rope_in"], 32)
                        for r in range(8):
                            kind, src, half, dst = ROPE[r]
                            if kind == "q":
                                pool.wait_ge(sems["rope_mm"], r + 1)
                                pool.tensor_tensor(proj[:, dst, :], proj[:, src, :], cos[:], ALU.mult).then_inc(sems["rope_cos"], 1)
                clear(sems)

        def mix_out(layer):
            stage[0] = "mixout"
            with scope() as ctx:
                w = Weights(ctx, DT)
                acc = sb(ctx, "acc", [P, SEQ])
                r0 = sb(ctx, "r0", [P, SEQ])
                sq = [sb(ctx, f"sq{k}", [P, SEQ])[:] for k in range(2)]
                sems = semaphores(STREAM + LN, slots=[("raw_in", RAW)])
                N = DT // 2
                with nc.Block() as block:
                    def chunks(one):
                        def go(q, par_):
                            for u in range(2):
                                one(2 * q + u, 2 * par_ + u)
                        return go

                    @block.sync
                    def _(sp):
                        by_pairs(sp, N, chunks(lambda c, s: load_chunk(sp, sems, w.raw, c, s, cols_of(w_out, layer, 0, DT, c * P), DT)))

                    @block.gpsimd
                    def _(pool):
                        ln_acc(pool, sems, acc[:], seed=4)

                    @block.tensor
                    def _(pe):
                        pe.sem_inc(sems["mm_done"], SPLIT)

                        def two(q, par_):
                            pe.wait_ge(sems["y_done"], 2 * q + 2)
                            for u in range(2):
                                multiply(pe, sems, w, 2 * q + u, 2 * par_ + u, DT, 2 * par_ + u,
                                         lambda k: xhi[:, k, :], lambda k: xlo[:, k, :])
                        by_pairs(pe, N, two)
                        ln_pe(pe, sems, acc[:], sq)

                    @block.scalar
                    def _(act):
                        split = chunks(lambda c, s: split_hi(act, sems, w, c, s, DT))
                        split(0, 0)
                        in_pairs(act, N, split, lambda q, par_: None)
                        ln_act(act, sems, 1, sq, r0[:], 1)

                    @block.vector
                    def _(dve):
                        dve.sem_inc(sems["lo_done"], RAW)
                        dve.sem_inc(sems["y_done"], 4)
                        split = chunks(lambda c, s: split_lo(dve, sems, w, c, s, DT))
                        split(0, 0)

                        def residual(q, par_):
                            for u in range(2):
                                dve.wait_ge(sems["mm_done"], 2 * q + u + SPLIT + 1)
                                dve.scalar_tensor_tensor(out=at(xT, 2 * q + u), in0=at(xT, 2 * q + u), scalar=ALPHA,
                                                         in1=ps[:, 2 * par_ + u, :], op0=ALU.mult, op1=ALU.add).then_inc(sems["y_done"], 1)
                        in_pairs(dve, N, split, residual)
                        ln_dve(dve, sems, LN_EPS, r0[:], acc[:])
                clear(sems)

        def mixer(layer):
            stage[0] = "mix"
            with scope() as ctx:
                proj = sb(ctx, "proj", [P, N_PM, SEQ])
                v_sel = sb(ctx, "v_sel", [P, 2, QT, HEAD_DIM])
                v_swa = sb(ctx, "v_swa", [P, QT, P])
                gates = sb(ctx, "gates", [P, QT, 3 * NSA_HEADS])
                project_hgrn2(layer, proj, v_sel, v_swa, gates)
                attention(layer, proj, v_sel, v_swa, gates)
            mix_out(layer)

        with nc.Fori(0, DEPTH) as layer:
            ffn(layer, 0)
            mixer(layer)
            ffn(layer, 1)

        stage[0] = "end"
        with scope() as ctx:
            xo = sb(ctx, "xo", [P, QT, D_MODEL])
            sems = semaphores(["turned", "emptied", "stored"])
            with nc.Block() as block:
                @block.tensor
                def _(pe):
                    n = 0
                    for t in range(QT):
                        for h in range(2):
                            if n >= 4:
                                pe.wait_ge(sems["emptied"], n - 3)
                            for j in range(4):
                                mm = pe.transpose(ps[:, n % 4, j * P:(j + 1) * P],
                                                  xT[:, 4 * h + j, t * P:(t + 1) * P], ident[:])
                            mm.then_inc(sems["turned"], 1)
                            n += 1

                @block.vector
                def _(dve):
                    for n in range(2 * QT):
                        dve.wait_ge(sems["turned"], n + 1)
                        dve.tensor_copy(xo[:, n // 2, (n % 2) * 512:(n % 2 + 1) * 512], ps[:, n % 4, :]).then_inc(sems["emptied"], 1)

                @block.sync
                def _(sp):
                    for t in range(QT):
                        sp.wait_ge(sems["emptied"], 2 * t + 2)
                        sp.dma_start(out[0, t * P:(t + 1) * P, :], xo[:, t, :]).then_inc(sems["stored"], 16)
                    sp.wait_ge(sems["stored"], 16 * QT)


_INS = ['x', 'p', 'ln_g', 'ln_b', 'ffn_w_gu', 'ffn_w_down', 'w_in', 'w_out', 'cmp_pos', 'cmp_k_w1', 'cmp_k_w2',
        'cmp_v_w1', 'cmp_v_w2', 'swa_sinks', 'hgrn_lb_raw', 'hgrn_norm_g', 'ple_w', 'ple_gate_w', 'ple_gate_b']


def kernel(**inputs):
    import concourse.bacc as bacc
    from concourse.bass_utils import run_bass_kernel_spmd

    nc = bacc.Bacc("TRN2", target_bir_lowering=False, num_devices=1)
    consts, rope = shape_constants()
    named = {f"in_{name}_dram": np.ascontiguousarray(inputs[name]) for name in _INS}
    named["in_consts_dram"] = consts
    named["in_rope_dram"] = rope
    args = [nc.dram_tensor(name, a.shape, mybir.dt.from_np(a.dtype), kind="ExternalInput").ap()
            for name, a in named.items()]
    out = nc.dram_tensor("out_0_dram", (1, SEQ, D_MODEL), F32, kind="ExternalOutput").ap()
    build(nc, *args, out)
    r = run_bass_kernel_spmd(nc, [named], core_ids=[0])
    return r.results[0]["out_0_dram"]
```

```python
from contextlib import ExitStack

import numpy as np

import concourse.bass as bass
from concourse import mybir

F32 = mybir.dt.float32
F32R = mybir.dt.float32r
ALU = mybir.AluOpType
ACT = mybir.ActivationFunctionType
AX = mybir.AxisListType

P = 128
D_MODEL, SEQ, DEPTH, D_FF, PLE_DIM = 1024, 512, 2, 2816, 256
HEAD_DIM, NSA_HEADS, SWA_HEADS, HGRN_HEADS = 64, 4, 4, 4
CMP_LEN, CMP_STRIDE, CMP_HID = 32, 16, 256
N_CMP = (SEQ - CMP_LEN) // CMP_STRIDE + 1
DT = D_MODEL // P
FT = D_FF // P
QT = SEQ // P
PT_ = PLE_DIM // P
KD = FT // 2
NSA_COLS = 256 + 6 * 64 + 12
N_PM = 26
ALPHA = (2.0 * DEPTH) ** 0.25
LN_EPS, RMS_EPS = 1e-5, 1e-6
SCALE = HEAD_DIM ** -0.5
LN_FLOOR = float(np.log(np.float32(1e-30)))
RAW, SPLIT = 4, 2
LEVELS = 7

T_Q, T_CMP, T_SLC, T_WIN, T_GATE, T_SQ, T_SK, T_SV, T_HQ, T_HF, T_HI, T_HG = 0, 2, 3, 4, 5, 6, 8, 9, 10, 14, 18, 22

C_ID, C_ROT, C_DUP, C_ROTDUP, C_CAUSAL, C_BAND, C_CMP = (P * k for k in range(7))
C_HG = C_CMP + QT * N_CMP
C_END = C_HG + (LEVELS + 1) * P


def shape_constants():
    c = np.zeros((P, C_END), np.float32)
    r = np.arange(P)
    c[:, C_ID:C_ID + P] = np.eye(P)
    for m in range(P):
        other = m + 32 if m % 64 < 32 else m - 32
        sign = -1.0 if m % 64 < 32 else 1.0
        c[other, C_ROT + m] = sign
        for half in (0, 64):
            c[half + m % 64, C_DUP + m] = 1.0
            c[half + other % 64, C_ROTDUP + m] = sign
    q, k = r[:, None], r[None, :]
    c[:, C_CAUSAL:C_CAUSAL + P] = np.where(k <= q, 0.0, -1e30)
    c[:, C_BAND:C_BAND + P] = np.where(k > q, 0.0, -1e30)
    ends = np.arange(N_CMP) * CMP_STRIDE + CMP_LEN - 1
    for i in range(QT):
        c[:, C_CMP + i * N_CMP:C_CMP + (i + 1) * N_CMP] = np.where(ends[None, :] <= i * P + q, 0.0, -1e30)
    s, t = r[:, None], r[None, :]
    for lv in range(LEVELS):
        m = 1 << lv
        same = (s // (2 * m)) == (t // (2 * m))
        c[:, C_HG + lv * P:C_HG + (lv + 1) * P] = same & (s // m % 2 == 0) & (t // m % 2 == 1)
    c[:, C_HG + LEVELS * P:] = s == t
    inv = (1.0 / (np.float32(10000.0) ** (np.arange(0, HEAD_DIM, 2, dtype=np.float32) / HEAD_DIM))).astype(np.float32)
    ang = np.arange(SEQ, dtype=np.float32)[:, None] * inv[None, :]
    rope = np.concatenate([np.tile(np.cos(ang).T, (4, 1)), np.tile(np.sin(ang).T, (4, 1))], axis=1)
    return c, rope.astype(np.float32)


def build(nc, x, p, ln_g, ln_b, ffn_w_gu, ffn_w_down, w_in, w_out, cmp_pos, cmp_k_w1, cmp_k_w2, cmp_v_w1,
          cmp_v_w2, swa_sinks, hgrn_lb_raw, hgrn_norm_g, ple_w, ple_gate_w, ple_gate_b, consts_d, rope_d, out):
    with ExitStack() as whole:
        def scope():
            return ExitStack()

        stage = ["start"]

        def sb(ctx, name, shape, dt=F32):
            return ctx.enter_context(nc.sbuf_tensor(f"{stage[0]}_{name}", shape, dt))

        ps = whole.enter_context(nc.psum_tensor("banks", [P, 8, 512], F32))

        xT = sb(whole, "xT", [P, DT, SEQ])
        xhi = sb(whole, "xhi", [P, DT, SEQ], F32R)
        xlo = sb(whole, "xlo", [P, DT, SEQ], F32R)
        ident = sb(whole, "ident", [P, P])
        mean_w = sb(whole, "mean_w", [P, P])
        mask_r = sb(whole, "mask_r", [P, C_HG - C_CAUSAL], F32R)
        ident_r = sb(whole, "ident_r", [P, P], F32R)
        par = sb(whole, "par", [P, P])
        hgp = sb(whole, "hgp", [P, DEPTH, 3, HGRN_HEADS])
        lng = sb(whole, "lng", [P, 3 * DT])
        lnb = sb(whole, "lnb", [P, 3 * DT])
        gbh = sb(whole, "gbh", [P, DT])
        xsum = sb(whole, "xsum", [P, SEQ])
        shift = sb(whole, "shift", [P, SEQ])
        sinks = sb(whole, "sinks", [P, DEPTH * SWA_HEADS])
        PG, PB, PGB, PNG, PLB = 0, 24 * DEPTH, 48 * DEPTH, 56 * DEPTH, 60 * DEPTH

        def semaphores(names, slots=()):
            sems = {n: nc.alloc_semaphore(f"{stage[0]}_{n}") for n in names}
            for n, count in slots:
                sems[n] = [nc.alloc_semaphore(f"{stage[0]}_{n}{k}") for k in range(count)]
            return sems

        def clear(sems):
            singles = [one for s in sems.values() for one in (s if isinstance(s, list) else [s])]
            engines = (nc.sync, nc.gpsimd, nc.scalar, nc.vector)
            for n, one in enumerate(singles):
                engines[n % 4].sem_clear(one)
            nc.all_engine_barrier()
            for one in singles:
                nc.release_semaphore(one)

        STREAM = ["hi_done", "lo_done", "mm_done"]

        def load_chunk(sp, sems, raw, c, slot, src, kt):
            sp.wait_ge(sems["lo_done"], c + 1)
            sp.dma_start(raw[:, slot, 0:kt, :], src).then_inc(sems["raw_in"][slot], 16)

        def arrived(c, slot):
            return (c - slot) * (16 // RAW) + 16

        def split_hi(act, sems, w, c, slot, kt):
            act.wait_ge(sems["raw_in"][slot], arrived(c, slot))
            act.wait_ge(sems["mm_done"], c + 1)
            act.activation(w.hi[:, slot % SPLIT, 0:kt, :], w.raw[:, slot, 0:kt, :], ACT.Copy).then_inc(sems["hi_done"], 1)

        def split_lo(dve, sems, w, c, slot, kt):
            dve.wait_ge(sems["hi_done"], c + 1)
            dve.tensor_tensor(w.lo[:, slot % SPLIT, 0:kt, :], w.raw[:, slot, 0:kt, :], w.hi[:, slot % SPLIT, 0:kt, :],
                              ALU.subtract).then_inc(sems["lo_done"], 1)

        def multiply(pe, sems, w, c, slot, kt, bank, hi, lo, first=True, last=True, ready=None, n=SEQ):
            pe.wait_ge(sems["lo_done"], c + RAW + 1)
            for k in range(kt):
                if ready:
                    ready(k)
                wh, wl = w.hi[:, slot % SPLIT, k, :], w.lo[:, slot % SPLIT, k, :]
                pe.matmul(ps[:, bank, 0:n], wh, hi(k), start=(first and k == 0), stop=False)
                pe.matmul(ps[:, bank, 0:n], wh, lo(k), start=False, stop=False)
                mm = pe.matmul(ps[:, bank, 0:n], wl, hi(k), start=False, stop=(last and k == kt - 1))
            mm.then_inc(sems["mm_done"], 1)

        class Weights:
            def __init__(self, ctx, kt):
                self.raw = sb(ctx, "w_raw", [P, RAW, kt, P])
                self.hi = sb(ctx, "w_hi", [P, SPLIT, kt, P], F32R)
                self.lo = sb(ctx, "w_lo", [P, SPLIT, kt, P], F32R)

        def in_pairs(eng, n, split, consume, next_split=None, before_last=None):
            loops = (n - 1) // 2
            with eng.Fori(0, loops) as i:
                for u in range(2):
                    split(2 * i + u + 1, (u + 1) % 2)
                    consume(2 * i + u, u)
            if before_last:
                before_last()
            for q in range(2 * loops, n):
                if q + 1 < n:
                    split(q + 1, (q + 1) % 2)
                elif next_split:
                    next_split()
                consume(q, q % 2)

        def by_pairs(eng, n, body, first=0):
            with eng.Fori(0, (n - first) // 2) as i:
                for u in range(2):
                    body(2 * i + first + u, (first + u) % 2)
            if (n - first) % 2:
                body(n - 1, (n - 1) % 2)

        def multiply_first(pe, sems, w, kt):
            pe.wait_ge(sems["lo_done"], RAW + 2)
            for k in range(kt):
                pe.wait_ge(sems["x_lo"], k + 1)
                for u in range(2):
                    pe.matmul(ps[:, u, :], w.hi[:, u, k, :], xhi[:, k, :], start=(k == 0), stop=False)
                    pe.matmul(ps[:, u, :], w.hi[:, u, k, :], xlo[:, k, :], start=False, stop=False)
                    mm = pe.matmul(ps[:, u, :], w.lo[:, u, k, :], xhi[:, k, :], start=False, stop=(k == kt - 1))
                    if k == kt - 1:
                        mm.then_inc(sems["mm_done"], 1)

        def at(t, k):
            if isinstance(k, int):
                return t[:, k, :]
            return t[:, bass.ds(k, 1), :].rearrange("p a n -> p (a n)")

        def col(t, k):
            return t[:, k:k + 1] if isinstance(k, int) else t[:, bass.ds(k, 1)]

        def cols_of(w, layer, k0, kt, c0):
            v = w.rearrange("l (t p) n -> l p t n", p=P)
            return v[bass.ds(layer, 1), :, k0:k0 + kt, bass.ds(c0, P)].rearrange("a p t n -> (a p) t n")

        LN_SUM = ["y_done", "acc_done", "m0_mm", "m0_out", "centred", "squared", "sq_mm", "sq_sum"]
        LN = ["delta", "rstd_act", "newton", "scaled", "free_dve", "free_pool", "affine", "x_hi", "x_lo"]
        HALF = DT // 2

        def sum_pool(pool, sems, seed=2, sq=None, sqsum=None):
            pool.memset(xsum[:], 0.0).then_inc(sems["acc_done"], 1)
            for j0, n in ((0, HALF), (HALF, DT - 2 - HALF), (DT - 2, 2)):
                if j0 == HALF:
                    pool.wait_ge(sems["m0_mm"], 1)
                if j0 == DT - 2 and sq:
                    pool.wait_ge(sems["squared"], 2)
                    pool.tensor_tensor(sqsum, sq[0], sq[1], ALU.add).then_inc(sems["sq_sum"], 2)
                    for j in range(2, DT - 2):
                        pool.wait_ge(sems["squared"], j + 1)
                        pool.wait_ge(sems["sq_sum"], j)
                        pool.tensor_tensor(sqsum, sqsum, sq[j % 2], ALU.add).then_inc(sems["sq_sum"], 1)
                with pool.Fori(j0, j0 + n) as j:
                    pool.wait_ge(sems["y_done"], j + seed + 1)
                    pool.wait_ge(sems["acc_done"], j + 1)
                    pool.tensor_tensor(xsum[:], xsum[:], at(xT, j), ALU.add).then_inc(sems["acc_done"], 1)

        def m0_pe(pe, sems):
            pe.wait_ge(sems["acc_done"], HALF + 1)
            pe.matmul(ps[:, 6, :], mean_w[:], xsum[:], start=True, stop=True).then_inc(sems["m0_mm"], 1)

        def squares_pe(pe, sems, sq, tiles):
            for j in tiles:
                pe.wait_ge(sems["squared"], j + 1)
                pe.matmul(ps[:, 7, :], mean_w[:], sq[j % 2], start=(j == 0), stop=(j == DT - 1)).then_inc(sems["sq_mm"], 1)

        def mean_pe(pe, sems):
            pe.wait_ge(sems["m0_out"], 1)
            pe.wait_ge(sems["acc_done"], DT + 1)
            pe.matmul(ps[:, 6, :], mean_w[:], xsum[:], start=True, stop=True).then_inc(sems["sq_mm"], 1)

        def squares_act(act, sems, sq, tiles, used="sq_mm"):
            for j in tiles:
                act.wait_ge(sems["centred"], j + 1)
                if j >= 2:
                    act.wait_ge(sems[used], j - 1)
                src = xT[:, j, :] if j < DT - 1 else sq[j % 2]
                act.activation(sq[j % 2], src, ACT.Square).then_inc(sems["squared"], 1)

        def m0_dve(dve, sems):
            dve.wait_ge(sems["m0_mm"], 1)
            dve.tensor_scalar(shift[:], ps[:, 6, :], float(DT // HALF), None, ALU.mult).then_inc(sems["m0_out"], 1)
            dve.wait_ge(sems["m0_out"], 1)

        def centre_dve(dve, sems, tiles, seed=2):
            for j in tiles:
                dve.wait_ge(sems["y_done"], seed + j + 1)
                dve.wait_ge(sems["acc_done"], j + 2)
                dve.tensor_tensor(xT[:, j, :], xT[:, j, :], shift[:], ALU.subtract).then_inc(sems["centred"], 1)

        def centre_last(dve, sems, sq, seed=2, used="sq_mm"):
            j = DT - 1
            dve.wait_ge(sems["y_done"], seed + j + 1)
            dve.wait_ge(sems[used], j - 1)
            dve.tensor_tensor(sq[j % 2], xT[:, j, :], shift[:], ALU.subtract).then_inc(sems["centred"], 1)
            dve.wait_ge(sems["acc_done"], j + 2)
            dve.tensor_tensor(xT[:, j, :], xT[:, j, :], shift[:], ALU.subtract).then_inc(sems["centred"], 1)

        def ln_act(act, sems, which, r0, split0, split1=None):
            act.preload_act_table_set("natural_log_exp_and_others")
            act.wait_ge(sems["delta"], 3)
            act.activation(r0, xsum[:], ACT.Ln).then_inc(sems["rstd_act"], 1)
            act.wait_ge(sems["rstd_act"], 1)
            act.activation(r0, r0, ACT.Exp, scale=-0.5).then_inc(sems["rstd_act"], 1)
            split0()
            if split1:
                split1()
            for j in range(DT):
                k = which * DT + j
                act.wait_ge(sems["scaled"], j + 1)
                act.activation(xT[:, j, :], xT[:, j, :], ACT.Identity, bias=lnb[:, k:k + 1],
                               scale=lng[:, k:k + 1]).then_inc(sems["affine"], 1)
                act.wait_ge(sems["affine"], j + 1)
                act.activation(xhi[:, j, :], xT[:, j, :], ACT.Copy).then_inc(sems["x_hi"], 1)

        def ln_pool(pool, sems, w=None):
            pool.wait_ge(sems["delta"], 1)
            for j in range(3, DT):
                pool.tensor_tensor(xT[:, j, :], xT[:, j, :], shift[:], ALU.subtract).then_inc(sems["free_pool"], 1)
            if w:
                pool.wait_ge(sems["lo_done"], RAW + 1)
                split_lo(pool, sems, w, 1, 1, DT)

        def ln_dve(dve, sems, eps, r0, split0):
            t = xsum[:]
            dve.tensor_tensor(shift[:], ps[:, 6, :], shift[:], ALU.subtract).then_inc(sems["delta"], 1)
            dve.wait_ge(sems["delta"], 1)
            dve.tensor_tensor(t, shift[:], shift[:], ALU.mult).then_inc(sems["delta"], 1)
            dve.wait_ge(sems["delta"], 2)
            dve.scalar_tensor_tensor(out=t, in0=ps[:, 7, :], scalar=eps, in1=t, op0=ALU.add,
                                     op1=ALU.subtract).then_inc(sems["delta"], 1)
            for j in range(3):
                dve.tensor_tensor(xT[:, j, :], xT[:, j, :], shift[:], ALU.subtract).then_inc(sems["free_dve"], 1)
            dve.wait_ge(sems["rstd_act"], 2)
            dve.wait_ge(sems["delta"], 3)
            dve.tensor_tensor(t, t, r0, ALU.mult).then_inc(sems["newton"], 1)
            dve.wait_ge(sems["newton"], 1)
            dve.scalar_tensor_tensor(out=t, in0=t, scalar=-0.5, in1=r0, op0=ALU.mult, op1=ALU.mult).then_inc(sems["newton"], 1)
            dve.wait_ge(sems["newton"], 2)
            dve.scalar_tensor_tensor(out=t, in0=t, scalar=1.5, in1=r0, op0=ALU.add, op1=ALU.mult).then_inc(sems["newton"], 1)
            dve.wait_ge(sems["newton"], 3)
            for j in range(DT + 1):
                if j < DT:
                    dve.wait_ge(sems["free_dve" if j < 3 else "free_pool"], j + 1 if j < 3 else j - 2)
                    dve.tensor_tensor(xT[:, j, :], xT[:, j, :], t, ALU.mult).then_inc(sems["scaled"], 1)
                if j == 0:
                    split0()
                if j >= 1 and j - 1 < DT:
                    x_low(dve, sems, j - 1)

        def x_low(dve, sems, j):
            dve.wait_ge(sems["x_hi"], j + 1)
            dve.tensor_tensor(xlo[:, j, :], xT[:, j, :], xhi[:, j, :], ALU.subtract).then_inc(sems["x_lo"], 1)

        with scope() as ctx:
            xin = sb(ctx, "xin", [P, QT, D_MODEL])
            rows = sb(ctx, "rows", [P, P])
            lbs = sb(ctx, "lbs", [P, 6, HGRN_HEADS])
            masks = sb(ctx, "masks", [P, C_HG - C_CAUSAL])
            sems = semaphores(["loaded", "x_in", "made", "turned", "emptied", "par_in", "lbt", "lba"])

            with nc.Block() as block:
                @block.sync
                def _(sp):
                    sp.dma_start(ident[:], consts_d[:, C_ID:C_ID + P]).then_inc(sems["loaded"], 16)
                    sp.dma_start(masks[:], consts_d[:, C_CAUSAL:C_HG]).then_inc(sems["loaded"], 16)
                    for src, r0, n in ((ln_g.rearrange("l t (j q) -> (l t j) q", q=P), PG, 24 * DEPTH),
                                       (ln_b.rearrange("l t (j q) -> (l t j) q", q=P), PB, 24 * DEPTH),
                                       (ple_gate_b.rearrange("l (j q) -> (l j) q", q=P), PGB, 8 * DEPTH),
                                       (hgrn_norm_g.rearrange("l (j q) -> (l j) q", q=P), PNG, 4 * DEPTH),
                                       (hgrn_lb_raw.rearrange("l (j q) -> (l j) q", q=P), PLB, 4 * DEPTH)):
                        sp.dma_start(rows[r0:r0 + n, :], src).then_inc(sems["loaded"], 16)
                    sp.dma_start(sinks[:], swa_sinks.rearrange("l h -> (l h)").partition_broadcast(P)).then_inc(sems["loaded"], 16)
                    for t in range(QT):
                        sp.dma_start(xin[:, t, :], x[0, t * P:(t + 1) * P, :]).then_inc(sems["x_in"], 16)
                    sp.wait_ge(sems["loaded"], 16 * 8)

                @block.gpsimd
                def _(pool):
                    pool.memset(mean_w[:], 1.0 / D_MODEL)
                    pool.memset(hgp[:, 0, 1, :], 0.0).then_inc(sems["made"], 1)

                @block.tensor
                def _(pe):
                    pe.wait_ge(sems["loaded"], 16 * 8)
                    pe.transpose(ps[:, 7, 0:P], rows[:], ident[:]).then_inc(sems["par_in"], 1)
                    pe.wait_ge(sems["x_in"], 16 * QT)
                    for j in range(DT):
                        if j >= 4:
                            pe.wait_ge(sems["emptied"], j - 3)
                        for t in range(QT):
                            mm = pe.transpose(ps[:, j % 4, t * P:(t + 1) * P], xin[:, t, j * P:(j + 1) * P], ident[:])
                        mm.then_inc(sems["turned"], 1)

                @block.scalar
                def _(act):
                    act.wait_ge(sems["loaded"], 16 * 8)
                    act.activation(mask_r[:], masks[:], ACT.Copy)
                    act.activation(ident_r[:], ident[:], ACT.Copy)
                    act.wait_ge(sems["lbt"], 3)
                    act.activation(lbs[:, 3, :], lbs[:, 1, :], ACT.Exp)
                    act.activation(lbs[:, 4, :], lbs[:, 2, :], ACT.Exp).then_inc(sems["lba"], 1)
                    act.wait_ge(sems["lbt"], 4)
                    act.activation(lbs[:, 5, :], lbs[:, 5, :], ACT.Ln).then_inc(sems["lba"], 1)

                @block.vector
                def _(dve):
                    dve.wait_ge(sems["par_in"], 1)
                    dve.tensor_copy(par[:], ps[:, 7, 0:P]).then_inc(sems["lbt"], 1)
                    dve.wait_ge(sems["lbt"], 1)
                    r0, r1 = par[:, PLB:PLB + 4], par[:, PLB + 4:PLB + 8]
                    dve.tensor_tensor(lbs[:, 0, :], r0, r1, ALU.max).then_inc(sems["lbt"], 1)
                    dve.wait_ge(sems["lbt"], 2)
                    dve.tensor_tensor(lbs[:, 1, :], r0, lbs[:, 0, :], ALU.subtract)
                    dve.tensor_tensor(lbs[:, 2, :], r1, lbs[:, 0, :], ALU.subtract).then_inc(sems["lbt"], 1)
                    for j in range(DT):
                        dve.wait_ge(sems["turned"], j + 1)
                        dve.tensor_copy(xT[:, j, :], ps[:, j % 4, :]).then_inc(sems["emptied"], 1)
                    dve.wait_ge(sems["lba"], 1)
                    dve.tensor_tensor(lbs[:, 5, :], lbs[:, 3, :], lbs[:, 4, :], ALU.add).then_inc(sems["lbt"], 1)
                    dve.wait_ge(sems["lba"], 2)
                    dve.tensor_tensor(hgp[:, 1, 1, :], lbs[:, 1, :], lbs[:, 5, :], ALU.subtract).then_inc(sems["lbt"], 1)
                    dve.tensor_tensor(hgp[:, 1, 0, :], lbs[:, 2, :], lbs[:, 5, :], ALU.subtract).then_inc(sems["lbt"], 1)
                    dve.wait_ge(sems["lbt"], 6)
                    dve.tensor_scalar(hgp[:, 1, 0, :], hgp[:, 1, 0, :], LN_FLOOR, None, ALU.max)
                    dve.memset(hgp[:, 0, 0, :], LN_FLOOR).then_inc(sems["lbt"], 1)
                    dve.wait_ge(sems["made"], 1)
                    dve.wait_ge(sems["lbt"], 7)
                    for l in range(DEPTH):
                        dve.tensor_tensor(hgp[:, l, 2, :], hgp[:, l, 1, :], hgp[:, l, 0, :], ALU.subtract)
            clear(sems)

        def ffn(layer, half):
            ple = half == 1
            stage[0] = f"ffn{half + 1}"
            with scope() as ctx:
                w = Weights(ctx, KD)
                hhi = sb(ctx, "hhi", [P, FT, SEQ], F32R)
                hlo = sb(ctx, "hlo", [P, FT, SEQ], F32R)
                gate = sb(ctx, "gate", [P, 2, SEQ])
                prod = sb(ctx, "prod", [P, 2, SEQ])
                r0 = prod[:, 0, :]
                sq = [prod[:, 1, :], sb(ctx, "sq1", [P, SEQ])[:]]
                if ple:
                    phi = sb(ctx, "phi", [P, PT_, SEQ], F32R)
                    plo = sb(ctx, "plo", [P, PT_, SEQ], F32R)
                    pin = gate[:, :, :].rearrange("p a (b n) -> p (a b) n", n=PLE_DIM)
                ln2 = semaphores([f"{n}_ple" for n in LN]) if ple else {}
                ln2 = {n: ln2[f"{n}_ple"] for n in LN} if ple else {}
                sems = semaphores(STREAM + LN + LN_SUM + ["gate_done", "h_done", "h_hi", "h_lo", "par_done", "p_in", "p_turned",
                                           "p_hi", "p_lo", "e_act", "e_mul", "e_done"], slots=[("raw_in", RAW)])
                C_DN, C_PLE = 2 * FT, 2 * FT + 2 * DT

                gu = ffn_w_gu.rearrange("l h k n -> (l h) k n")
                dn = ffn_w_down.rearrange("l h k n -> (l h) k n")
                which_w = layer * 2 + half

                with nc.Block() as block:
                    @block.sync
                    def _(sp):
                        def load_p():
                            for t in range(QT):
                                src = p[bass.ds(layer, 1), 0, t * P:(t + 1) * P, :].rearrange("a q n -> (a q) n")
                                sp.dma_start(pin[:, t, :], src).then_inc(sems["p_in"], 16)

                        def up(q, par_):
                            for u in range(2):
                                load_chunk(sp, sems, w.raw, 2 * q + u, 2 * par_ + u,
                                           cols_of(gu, which_w, 0, DT, q * P + u * D_FF), DT)

                        def down(q, par_):
                            for u in range(2):
                                load_chunk(sp, sems, w.raw, C_DN + 2 * q + u, 2 * par_ + u,
                                           cols_of(dn, which_w, u * KD, KD, q * P), KD)

                        def embed(q, par_):
                            load_chunk(sp, sems, w.raw, C_PLE + 2 * q, 2 * par_,
                                       cols_of(ple_gate_w, layer, 0, DT, q * P), DT)
                            load_chunk(sp, sems, w.raw, C_PLE + 2 * q + 1, 2 * par_ + 1,
                                       cols_of(ple_w, layer, 0, PT_, q * P), PT_)
                        by_pairs(sp, FT, up)
                        by_pairs(sp, 2, down)
                        if ple:
                            sp.wait_ge(sems["h_done"], FT + 2)
                            load_p()
                        by_pairs(sp, DT, down, first=2)
                        if ple:
                            by_pairs(sp, DT, embed)

                    def split_with(one, eng):
                        def up(q, par_):
                            for u in range(2):
                                one(eng, sems, w, 2 * q + u, 2 * par_ + u, DT)

                        def down(q, par_):
                            for u in range(2):
                                one(eng, sems, w, C_DN + 2 * q + u, 2 * par_ + u, KD)

                        def embed(q, par_):
                            one(eng, sems, w, C_PLE + 2 * q, 2 * par_, DT)
                            one(eng, sems, w, C_PLE + 2 * q + 1, 2 * par_ + 1, PT_)
                        return up, down, embed

                    @block.gpsimd
                    def _(pool):
                        if ple:
                            ln_pool(pool, sems, w)
                            pool.wait_ge(sems["x_lo"], DT)
                        sum_pool(pool, sems, sq=sq, sqsum=gate[:, 0, :])
                        if ple:
                            ln_pool(pool, ln2)

                    @block.tensor
                    def _(pe):
                        pe.sem_inc(sems["mm_done"], SPLIT)
                        def turn_p():
                            pe.wait_ge(sems["p_in"], 16 * QT)
                            for k in range(PT_):
                                for t in range(QT):
                                    mm = pe.transpose(ps[:, 2 + k, t * P:(t + 1) * P], pin[:, t, k * P:(k + 1) * P], ident[:])
                                mm.then_inc(sems["p_turned"], 1)

                        def up(q, par_):
                            pe.wait_ge(sems["h_done"], q + 1)
                            for u in range(2):
                                multiply(pe, sems, w, 2 * q + u, 2 * par_ + u, DT, 2 * par_ + u,
                                         lambda k: xhi[:, k, :], lambda k: xlo[:, k, :])

                        def down(q, par_):
                            pe.wait_ge(sems["y_done"], q + 1)

                            def ready(k):
                                if k >= KD - 2:
                                    pe.wait_ge(sems["h_lo"], FT - (KD - 1 - k))
                            for u in range(2):
                                multiply(pe, sems, w, C_DN + 2 * q + u, 2 * par_ + u, KD, 4 + par_,
                                         lambda k: hhi[:, u * KD + k, :], lambda k: hlo[:, u * KD + k, :],
                                         first=(u == 0), last=(u == 1), ready=ready if u else None)

                        def embed(q, par_):
                            pe.wait_ge(sems["e_done"], q + 1)

                            def ready(k):
                                pe.wait_ge(ln2["x_lo"], k + 1)
                            first = isinstance(q, int) and q == 0
                            multiply(pe, sems, w, C_PLE + 2 * q, 2 * par_, DT, 2 * par_,
                                     lambda k: xhi[:, k, :], lambda k: xlo[:, k, :], ready=ready if first else None)
                            multiply(pe, sems, w, C_PLE + 2 * q + 1, 2 * par_ + 1, PT_, 2 * par_ + 1,
                                     lambda k: phi[:, k, :], lambda k: plo[:, k, :])
                        multiply_first(pe, sems, w, DT)
                        by_pairs(pe, FT, up, first=1)
                        if ple:
                            by_pairs(pe, 2, down)
                            turn_p()
                        by_pairs(pe, DT - 2, down, first=2 if ple else 0)
                        m0_pe(pe, sems)
                        down(DT - 2, 0)
                        down(DT - 1, 1)
                        pe.wait_ge(sems["sq_sum"], DT - 2)
                        pe.matmul(ps[:, 7, :], mean_w[:], gate[:, 0, :], start=True, stop=False).then_inc(sems["sq_mm"], 1)
                        squares_pe(pe, sems, sq, (DT - 2,))
                        mean_pe(pe, sems)
                        squares_pe(pe, sems, sq, (DT - 1,))
                        if ple:
                            pe.wait_ge(sems["p_lo"], PT_)
                            embed(0, 0)
                            by_pairs(pe, DT, embed, first=1)

                    @block.scalar
                    def _(act):
                        s_up, s_down, s_embed = split_with(split_hi, act)
                        def p_high():
                            for k in range(PT_):
                                act.wait_ge(sems["p_turned"], k + 1)
                                act.activation(phi[:, k, :], ps[:, 2 + k, :], ACT.Copy).then_inc(sems["p_hi"], 1)
                        def first_hi(u):
                            return lambda: split_hi(act, sems, w, u, u, DT)
                        if ple:
                            ln_act(act, sems, 1, r0, first_hi(0), first_hi(1))
                        else:
                            for j in range(DT):
                                act.activation(xhi[:, j, :], xT[:, j, :], ACT.Copy).then_inc(sems["x_hi"], 1)
                                if j in (4, 6):
                                    first_hi(j // 2 - 2)()

                        def gates(q, par_):
                            act.wait_ge(sems["mm_done"], 2 * q + SPLIT + 1)
                            act.wait_ge(sems["h_done"], q + 1)
                            act.activation(gate[:, par_, :], ps[:, 2 * par_, :], ACT.Silu).then_inc(sems["gate_done"], 1)
                            act.wait_ge(sems["h_done"], q + SPLIT + 1)
                            act.activation(at(hhi, q), prod[:, par_, :], ACT.Copy).then_inc(sems["h_hi"], 1)
                        act.preload_act_table_set("silu_and_others")
                        in_pairs(act, FT, s_up, gates, lambda: s_down(0, 0))

                        def before_last():
                            if ple:
                                p_high()
                            squares_act(act, sems, sq, range(DT - 2), "sq_sum")
                        in_pairs(act, DT, s_down, lambda q, par_: None, before_last=before_last)
                        squares_act(act, sems, sq, (DT - 2, DT - 1), "sq_sum")
                        if ple:
                            ln_act(act, ln2, 2, r0, lambda: s_embed(0, 0))

                        def sigm(q, par_):
                            act.wait_ge(sems["mm_done"], C_PLE + 2 * q + SPLIT + 1)
                            act.wait_ge(sems["e_done"], q + 1)
                            act.activation(gate[:, par_, :], ps[:, 2 * par_, :], ACT.Tanh, scale=0.5,
                                           bias=col(gbh, q)).then_inc(sems["e_act"], 1)
                        if ple:
                            act.preload_act_table_set("silu_and_others")
                            in_pairs(act, DT, s_embed, sigm)

                    @block.vector
                    def _(dve):
                        s_up, s_down, s_embed = split_with(split_lo, dve)
                        dve.sem_inc(sems["lo_done"], RAW)
                        dve.sem_inc(sems["h_done"], 2)
                        dve.sem_inc(sems["y_done"], 2)
                        dve.sem_inc(sems["e_done"], 2)
                        if not ple:
                            dve.tensor_copy(lng[:], par[:, bass.ds(layer * 24 + PG, 24)])
                            dve.tensor_copy(lnb[:], par[:, bass.ds(layer * 24 + PB, 24)])
                            dve.tensor_scalar(gbh[:], par[:, bass.ds(layer * 8 + PGB, 8)], 0.5, None,
                                              ALU.mult).then_inc(sems["par_done"], 1)

                        def p_low():
                            for k in range(PT_):
                                dve.wait_ge(sems["p_hi"], k + 1)
                                dve.tensor_tensor(plo[:, k, :], ps[:, 2 + k, :], phi[:, k, :],
                                                  ALU.subtract).then_inc(sems["p_lo"], 1)

                        def first_lo(u):
                            return lambda: split_lo(dve, sems, w, u, u, DT)
                        if ple:
                            ln_dve(dve, sems, LN_EPS, r0, first_lo(0))
                        else:
                            for j in range(DT):
                                x_low(dve, sems, j)
                                if j in (4, 6):
                                    first_lo(j // 2 - 2)()

                        def hidden(q, par_):
                            dve.wait_ge(sems["gate_done"], q + 1)
                            dve.wait_ge(sems["mm_done"], 2 * q + SPLIT + 2)
                            dve.tensor_tensor(prod[:, par_, :], gate[:, par_, :], ps[:, 2 * par_ + 1, :],
                                              ALU.mult).then_inc(sems["h_done"], 1)
                            dve.wait_ge(sems["h_hi"], q + 1)
                            dve.tensor_tensor(at(hlo, q), prod[:, par_, :], at(hhi, q),
                                              ALU.subtract).then_inc(sems["h_lo"], 1)

                        def residual(q, par_):
                            dve.wait_ge(sems["mm_done"], C_DN + 2 * q + SPLIT + 2)
                            dve.scalar_tensor_tensor(out=at(xT, q), in0=at(xT, q), scalar=2.0 * ALPHA,
                                                     in1=ps[:, 4 + par_, :], op0=ALU.mult,
                                                     op1=ALU.add).then_inc(sems["y_done"], 1)
                        in_pairs(dve, FT, s_up, hidden, lambda: s_down(0, 0))

                        def centre():
                            m0_dve(dve, sems)
                            centre_dve(dve, sems, range(DT - 2))
                            if ple:
                                p_low()
                        in_pairs(dve, DT, s_down, residual, before_last=centre)
                        centre_dve(dve, sems, (DT - 2,))
                        centre_last(dve, sems, sq, used="sq_sum")
                        if ple:
                            dve.wait_ge(sems["centred"], DT + 1)
                            dve.wait_ge(sems["sq_mm"], 4)
                            ln_dve(dve, ln2, 4.0 * LN_EPS, r0, lambda: s_embed(0, 0))

                        def embed(q, par_):
                            dve.wait_ge(sems["e_act"], q + 1)
                            dve.wait_ge(sems["mm_done"], C_PLE + 2 * q + SPLIT + 2)
                            dve.scalar_tensor_tensor(out=prod[:, par_, :], in0=gate[:, par_, :], scalar=1.0,
                                                     in1=ps[:, 2 * par_ + 1, :], op0=ALU.add,
                                                     op1=ALU.mult).then_inc(sems["e_mul"], 1)
                            dve.wait_ge(sems["e_mul"], q + 1)
                            dve.scalar_tensor_tensor(out=at(xT, q), in0=prod[:, par_, :], scalar=0.5,
                                                     in1=at(xT, q), op0=ALU.mult, op1=ALU.add).then_inc(sems["e_done"], 1)
                        if ple:
                            in_pairs(dve, DT, s_embed, embed)
                clear(sems)
                clear(ln2)

        def attention(layer, proj, gates):
            stage[0] = "attn"
            NSA_N, SWA_N = NSA_HEADS * QT, SWA_HEADS * QT
            UNITS, PAIRS = NSA_N + SWA_N, DT // 2
            KH = DT // 2
            FIRST_CHUNK = 4
            GROUP_TILE = (2, 3, 0, 1)
            with scope() as ctx:
                w = Weights(ctx, KH)
                anyv = sb(ctx, "anyv", [P, 1])
                prob = sb(ctx, "prob", [P, 2, 2, SEQ])
                prob_t = sb(ctx, "prob_t", [P, 3, 2, SEQ])
                hid_t = proj[0:N_CMP, T_CMP, :]
                hid = sb(ctx, "hid", [P, 4, 32])
                w2k = sb(ctx, "w2k", [P, 2, P])
                w2v = sb(ctx, "w2v", [P, 2, HEAD_DIM])
                kc = sb(ctx, "kc", [P, 32])
                vc = sb(ctx, "vc", [N_CMP, HEAD_DIM])
                p_cmp = sb(ctx, "p_cmp", [P, NSA_N, N_CMP])
                pt_cmp = proj[0:N_CMP, T_CMP:T_CMP + 4, :].rearrange("p a (b n) -> p (a b) n", n=P)
                st_cmp = sb(ctx, "st_cmp", [P, 3, NSA_N])
                mx = sb(ctx, "mx", [P, 2, 2])
                nb = sb(ctx, "nb", [P, 2, 2])
                sums = sb(ctx, "sums", [P, 2, 2])
                rec = sb(ctx, "rec", [P, 2, 2])
                e_sink = sb(ctx, "e_sink", [P, 2])
                sq = [sb(ctx, f"sq{k}", [P, SEQ])[:] for k in range(2)]
                sems = semaphores(STREAM + LN_SUM + ["aux_in",
                                                     "hid_turned", "hid_out", "kc_mm", "kc_out", "vc_out", "half_done",
                                                     "sc_ready", "sc_sub", "sc_exp", "pc_done", "pct_ready",
                                                     "pct_act", "pct_dve", "s_ready", "nb_ready", "exp_done", "step",
                                                     "act_step", "p_norm", "pt_ready", "ev_act", "ev_dve", "pv_done",
                                                     "o_hi", "o_lo"], slots=[("raw_in", RAW)])

                def c_mat(c):
                    return mask_r[:, c - C_CAUSAL:c - C_CAUSAL + P]

                units = [(False, 2 * hp + hh, i, max(i - 1, 0)) for hp in range(2) for i in range(QT) for hh in range(2)]
                units += [(True, 2 * hp + hh, i, 0) for hp in range(2) for i in range(QT) for hh in range(2)]
                ev_a, ev_d, na, nd = [], [], 0, 0
                for n, (nsa, *_r) in enumerate(units):
                    na, nd = na + (nsa or n % 2 == 0), nd + (nsa or n % 2 == 1)
                    ev_a.append(na)
                    ev_d.append(nd)

                def chunks(one):
                    def go(q, par_):
                        for u in range(2):
                            one(DT + 2 * q + u, 2 * par_ + u)
                    return go

                def chunk_of_turn(n):
                    c = (n - FIRST_CHUNK) // 2
                    return c if (n - FIRST_CHUNK) % 2 == 0 and 0 <= c < DT else None

                def split_of_turn(n):
                    c = (n + 1 - FIRST_CHUNK) // 2
                    return c if (n + 1 - FIRST_CHUNK) % 2 == 0 and 0 <= c < DT + 2 else None

                def halves(h):
                    return slice(64 * (h % 2), 64 * (h % 2) + 64)

                with nc.Block() as block:
                    @block.sync
                    def _(sp):
                        def aux(dst, src):
                            sp.dma_start(dst, src).then_inc(sems["aux_in"], 16)

                        one = bass.ds(layer, 1)
                        w2 = cmp_k_w2.rearrange("l (t p) n -> l p t n", p=P)[one, :, :, :].rearrange("a p t n -> (a p) t n")
                        aux(w2k[:, :, 0:64], w2)
                        aux(w2k[:, :, 64:128], w2)
                        aux(w2v[:], cmp_v_w2.rearrange("l (t p) n -> l p t n", p=P)[one, :, :, :].rearrange("a p t n -> (a p) t n"))
                        for c in range(DT):
                            load_chunk(sp, sems, w.raw, c, c % RAW, cols_of(w_out, layer, KH, KH, c * P), KH)
                        by_pairs(sp, PAIRS, chunks(lambda c, s: load_chunk(sp, sems, w.raw, c, s, cols_of(w_out, layer, 0, KH, (c - DT) * P), KH)))

                    @block.gpsimd
                    def _(pool):
                        sum_pool(pool, sems, seed=4)

                    @block.tensor
                    def _(pe):
                        pe.sem_inc(sems["mm_done"], SPLIT)

                        def compressed(n):
                            if n == 0:
                                for q in range(4):
                                    mm = pe.transpose(ps[:, 3, 32 * q:32 * q + N_CMP], hid_t[:, q * P:(q + 1) * P], ident[0:N_CMP, 0:N_CMP])
                                mm.then_inc(sems["hid_turned"], 1)
                            if n == 2:
                                pe.wait_ge(sems["aux_in"], 16 * 3)
                                pe.wait_ge(sems["hid_out"], 1)
                                for m in range(2):
                                    mm = pe.matmul(ps[:, 3, 0:N_CMP], w2k[:, m, :], hid[:, m, 0:N_CMP], start=(m == 0), stop=(m == 1))
                                mm.then_inc(sems["kc_mm"], 1)
                                for m in range(2):
                                    mm = pe.matmul(ps[0:N_CMP, 1, 0:HEAD_DIM], hid[:, 2 + m, 0:N_CMP], w2v[:, m, :], start=(m == 0), stop=(m == 1))
                                mm.then_inc(sems["kc_mm"], 1)
                            if n == 4:
                                pe.wait_ge(sems["kc_out"], 1)
                                pe.wait_ge(sems["vc_out"], 1)
                                masks = mask_r[:, C_CMP - C_CAUSAL:C_HG - C_CAUSAL]
                                for m in range(NSA_N):
                                    if m % QT == 0:
                                        b = 1 + 2 * (m // 8)
                                        pe.matmul(ps[:, b, m % 8 * N_CMP:(m % 8 + QT) * N_CMP], ident_r[:], masks, start=True, stop=False)
                                    h, i = 2 * (m % 8 // QT) + m // 8, m % QT
                                    o = ps[:, 1 + 2 * (h % 2), m % 8 * N_CMP:(m % 8 + 1) * N_CMP]
                                    mm = pe.matmul(o, proj[halves(h), T_Q + h // 2, i * P:(i + 1) * P], kc[halves(h), 0:N_CMP], start=False, stop=(m % QT == QT - 1))
                                mm.then_inc(sems["sc_ready"], 1)
                            if n in (9, 12):
                                pe.wait_ge(sems["pc_done"], 1)
                                for b in range(2):
                                    if n == 12:
                                        pe.wait_ge(sems["pct_dve" if b else "pct_act"], 1)
                                    for m in range(4):
                                        p4 = p_cmp[:, 4 * b + m + (8 if n == 12 else 0), :]
                                        mm = pe.transpose(ps[0:N_CMP, 1 + 2 * b, m * P:(m + 1) * P], p4, ident[:])
                                    mm.then_inc(sems["pct_ready"], 1)

                        def scores(n):
                            nsa, h, i, k0 = units[n]
                            pe.wait_ge(sems["exp_done"], n + 1)
                            if n == SWA_N:
                                pe.wait_ge(sems["pct_act"], 2)
                                pe.wait_ge(sems["pct_dve"], 2)
                            a = 2 * (n % 2)
                            qs = proj[halves(h), (T_HQ if nsa else T_SQ) + h // 2, i * P:(i + 1) * P]
                            for br in range(2 if nsa else 1):
                                ks = T_HF + br if nsa else (T_HQ + 2, T_HF + 2)[h // 2]
                                w_ = (i + 1 - k0) * P
                                pe.matmul(ps[:, a + br, 0:w_], qs, proj[halves(h), ks, k0 * P:(i + 1) * P], start=True, stop=False)
                                if not nsa and i > 0:
                                    pe.matmul(ps[:, a, 0:P], ident_r[:], c_mat(C_BAND), start=False, stop=False)
                                mm = pe.matmul(ps[:, a + br, w_ - P:w_], ident_r[:], c_mat(C_CAUSAL), start=False, stop=True)
                            mm.then_inc(sems["s_ready"], 1)

                        def turn(n):
                            nsa, h, i, k0 = units[n]
                            pe.wait_ge(sems["p_norm"], n + 1)
                            last = n - 1 if n >= SWA_N else n - 2
                            if last >= 0:
                                pe.wait_ge(sems["ev_act"], ev_a[last])
                                if ev_d[last]:
                                    pe.wait_ge(sems["ev_dve"], ev_d[last])
                            for br in range(2 if nsa else 1):
                                b = 4 + (br if nsa else n % 2)
                                for c in range(i + 1 - k0):
                                    mm = pe.transpose(ps[:, b, c * P:(c + 1) * P], prob[:, n % 2, br, c * P:(c + 1) * P], ident[:])
                            mm.then_inc(sems["pt_ready"], 1)

                        def values(n):
                            nsa, h, i, k0 = units[n]
                            pe.wait_ge(sems["ev_act"], ev_a[n])
                            if ev_d[n]:
                                pe.wait_ge(sems["ev_dve"], ev_d[n])
                            if n % 8 == 0 and n:
                                pe.wait_ge(sems["o_lo"], n // 8)
                            o = ps[halves(h), 6, i * P:(i + 1) * P]
                            todo = [(proj[:, V_TILE[br if nsa else 2 + h // 2], (k0 + c) * HEAD_DIM:(k0 + c + 1) * HEAD_DIM],
                                     prob_t[:, n % 3, br, c * P:(c + 1) * P])
                                    for br in range(2 if nsa else 1) for c in range(i + 1 - k0)]
                            if nsa:
                                todo.append((vc[:], pt_cmp[:, (h % 2) * 8 + (h // 2) * QT + i, :]))
                            for k, (v, pr) in enumerate(todo):
                                mm = pe.matmul(o, v, pr, start=(k == 0), stop=(k == len(todo) - 1))
                            mm.then_inc(sems["pv_done"], 1)

                        def first_pair(ks):
                            pe.wait_ge(sems["lo_done"], RAW + DT + 2)
                            for u in range(2):
                                for k in ks:
                                    pe.matmul(ps[:, u, :], w.hi[:, u, k, :], xhi[:, k, :], start=(k == 2), stop=False)
                                    pe.matmul(ps[:, u, :], w.hi[:, u, k, :], xlo[:, k, :], start=False, stop=False)
                                    mm = pe.matmul(ps[:, u, :], w.lo[:, u, k, :], xhi[:, k, :], start=False, stop=(k == 1))
                                if k == 1:
                                    mm.then_inc(sems["mm_done"], 1)

                        scores(0)
                        for n in range(UNITS + 3):
                            if n + 1 < UNITS:
                                scores(n + 1)
                            if n >= 3:
                                values(n - 3)
                            if 1 <= n <= UNITS:
                                turn(n - 1)
                            compressed(n)
                            c = chunk_of_turn(n)
                            if c is not None:
                                if c:
                                    pe.wait_ge(sems["half_done"], c)
                                multiply(pe, sems, w, c, c % RAW, KH, 7, lambda k: xhi[:, KH + k, :], lambda k: xlo[:, KH + k, :])
                            if n == UNITS:
                                pe.wait_ge(sems["exp_done"], UNITS + 2)
                                pe.wait_ge(sems["o_lo"], 3)
                                first_pair((2, 3, 0))
                        pe.wait_ge(sems["o_lo"], 4)
                        first_pair((1,))

                        def two(q, par_, behind=None):
                            pe.wait_ge(sems["y_done"], 2 * q + 2)
                            for u in range(2):
                                multiply(pe, sems, w, DT + 2 * q + u, 2 * par_ + u, KH, 2 * par_ + u,
                                         lambda k: xhi[:, k, :], lambda k: xlo[:, k, :])
                                if behind:
                                    squares_pe(pe, sems, sq, behind[u])
                        by_pairs(pe, PAIRS - 1, two, first=1)
                        m0_pe(pe, sems)
                        two(PAIRS - 1, (PAIRS - 1) % 2, (range(2), range(2, DT - 2)))
                        squares_pe(pe, sems, sq, (DT - 2,))
                        mean_pe(pe, sems)
                        squares_pe(pe, sems, sq, (DT - 1,))

                    def out_hi(act, g):
                        act.wait_ge(sems["pv_done"], 8 * g + 8)
                        act.activation(xhi[:, GROUP_TILE[g], :], ps[:, 6, :], ACT.Copy).then_inc(sems["o_hi"], 1)

                    @block.scalar
                    def _(act):
                        act.sem_inc(sems["exp_done"], 2)
                        def between(n):
                            if n == 1:
                                act.wait_ge(sems["hid_turned"], 1)
                                src = ps[:, 3, 0:P].rearrange("p (q n) -> p q n", n=32)[:, :, 0:N_CMP]
                                act.activation(hid[:, :, 0:N_CMP], src, ACT.Copy).then_inc(sems["hid_out"], 1)
                            if n == 3:
                                act.wait_ge(sems["kc_mm"], 1)
                                act.activation(kc[:, 0:N_CMP], ps[:, 3, 0:N_CMP], ACT.Copy).then_inc(sems["kc_out"], 1)
                            if n == 6:
                                act.wait_ge(sems["sc_sub"], 2)
                                act.activation(p_cmp[:], p_cmp[:], ACT.Exp, scale=SCALE).then_inc(sems["sc_exp"], 1)
                            if n in (10, 13):
                                b = 0 if n == 10 else 2
                                act.wait_ge(sems["pct_ready"], b + 1)
                                act.activation(pt_cmp[:, 4 * b:4 * b + 4, :].rearrange("p a n -> p (a n)"), ps[0:N_CMP, 1, :],
                                               ACT.Copy).then_inc(sems["pct_act"], 1)
                            if split_of_turn(n) is not None:
                                c = split_of_turn(n)
                                split_hi(act, sems, w, c, c % RAW, KH)

                        for n in range(UNITS + 3):
                            if n < UNITS:
                                nsa, h, i, k0 = units[n]
                                w_ = (i + 1 - k0) * P
                                act.wait_ge(sems["nb_ready"], n + 1)
                                if n >= 2:
                                    act.wait_ge(sems["pt_ready"], n - 1)
                                if not nsa:
                                    act.activation(e_sink[:, n % 2:n % 2 + 1], sinks[:, bass.ds(layer * SWA_HEADS + h, 1)], ACT.Exp,
                                                   bias=nb[:, n % 2, 0:1]).then_inc(sems["act_step"], 1)
                                for br in range(2 if nsa else 1):
                                    e = act.activation(prob[:, n % 2, br, 0:w_], ps[:, 2 * (n % 2) + br, 0:w_], ACT.Exp, scale=SCALE,
                                                       bias=nb[:, n % 2, br:br + 1], accum_out=sums[:, n % 2, br:br + 1])
                                e.then_inc(sems["exp_done"], 1)
                            if 2 <= n < UNITS + 2 and (units[n - 2][0] or n % 2 == 0):
                                m = n - 2
                                nsa, h, i, k0 = units[m]
                                w_ = (i + 1 - k0) * P
                                act.wait_ge(sems["pt_ready"], m + 1)
                                if m >= 3:
                                    act.wait_ge(sems["pv_done"], m - 2)
                                act.activation(prob_t[:, m % 3, 0, 0:w_], ps[:, 4 + (0 if nsa else m % 2), 0:w_], ACT.Copy).then_inc(sems["ev_act"], 1)
                            if n >= 10 and n % 8 == 2 and n <= UNITS:
                                out_hi(act, (n - 10) // 8)
                            between(n)
                        out_hi(act, UNITS // 8 - 1)
                        in_pairs(act, PAIRS, chunks(lambda c, s: split_hi(act, sems, w, c, s, KH)), lambda q, par_: None)
                        squares_act(act, sems, sq, range(DT))

                    @block.vector
                    def _(dve):
                        dve.sem_inc(sems["lo_done"], RAW)
                        dve.sem_inc(sems["y_done"], 4)
                        st = [0]

                        def then(ins):
                            ins.then_inc(sems["step"], 1)
                            st[0] += 1
                            dve.wait_ge(sems["step"], st[0])

                        def between(n):
                            if n == 1:
                                then(dve.tensor_scalar(gates[:], gates[:], 0.5, 0.5, ALU.mult, ALU.add))
                                first = mask_r[:, C_CMP - C_CAUSAL:C_CMP - C_CAUSAL + 1]
                                then(dve.tensor_scalar(anyv[:], first, -1.0, None, ALU.is_ge))
                                g0 = gates[:, 0, :].rearrange("p (h b) -> p b h", b=3)[:, 0]
                                then(dve.tensor_scalar(g0, g0, anyv[:, 0:1], None, ALU.mult))
                            if n == 3:
                                dve.wait_ge(sems["kc_mm"], 2)
                                dve.tensor_copy(vc[:], ps[0:N_CMP, 1, 0:HEAD_DIM]).then_inc(sems["vc_out"], 1)
                            if n == 5:
                                dve.wait_ge(sems["sc_ready"], 1)
                                wide = [P, 8, N_CMP]
                                for b in range(2):
                                    sc = ps[:, 1 + 2 * b, 0:8 * N_CMP].rearrange("p (u n) -> p u n", n=N_CMP)
                                    m8 = st_cmp[:, 0, 8 * b:8 * b + 8]
                                    then(dve.tensor_reduce(m8, sc, AX.X, ALU.max))
                                    dve.tensor_tensor(p_cmp[:, 8 * b:8 * b + 8, :], sc, m8[:, :, None].broadcast_to(wide),
                                                      ALU.subtract).then_inc(sems["sc_sub"], 1)
                            if n == 7:
                                dve.wait_ge(sems["sc_exp"], 1)
                                then(dve.tensor_reduce(st_cmp[:, 1, :], p_cmp[:], AX.X, ALU.add))
                                then(dve.reciprocal(st_cmp[:, 2, :], st_cmp[:, 1, :]))
                                for b in range(2):
                                    gc = gates[:, :, :].rearrange("p i (g s b) -> p s b g i", s=2, b=3)[:, b, 0]
                                    rc = st_cmp[:, 2, 8 * b:8 * b + 8].rearrange("p (g i) -> p g i", i=QT)
                                    then(dve.tensor_tensor(rc, rc, gc, ALU.mult))
                                dve.tensor_tensor(p_cmp[:], p_cmp[:], st_cmp[:, 2, :, None].broadcast_to([P, NSA_N, N_CMP]),
                                                  ALU.mult).then_inc(sems["pc_done"], 1)
                            if n in (10, 13):
                                b = 1 if n == 10 else 3
                                dve.wait_ge(sems["pct_ready"], b + 1)
                                dve.tensor_copy(pt_cmp[:, 4 * b:4 * b + 4, :].rearrange("p a n -> p (a n)"), ps[0:N_CMP, 3, :]).then_inc(sems["pct_dve"], 1)
                            if split_of_turn(n) is not None:
                                c = split_of_turn(n)
                                split_lo(dve, sems, w, c, c % RAW, KH)
                            if n and chunk_of_turn(n - 1) is not None:
                                c = chunk_of_turn(n - 1)
                                dve.wait_ge(sems["mm_done"], c + SPLIT + 1)
                                dve.scalar_tensor_tensor(out=xT[:, c, :], in0=xT[:, c, :], scalar=ALPHA, in1=ps[:, 7, :],
                                                         op0=ALU.mult, op1=ALU.add).then_inc(sems["half_done"], 1)

                        def row_max(n):
                            nsa, h, i, k0 = units[n]
                            w_ = (i + 1 - k0) * P
                            br = 2 if nsa else 1
                            dve.wait_ge(sems["s_ready"], n + 1)
                            then(dve.tensor_reduce(mx[:, n % 2, 0:br], ps[:, 2 * (n % 2):2 * (n % 2) + br, 0:w_], AX.X, ALU.max))
                            if nsa:
                                dve.tensor_scalar(nb[:, n % 2, 0:br], mx[:, n % 2, 0:br], -SCALE, None, ALU.mult).then_inc(sems["nb_ready"], 1)
                            else:
                                then(dve.tensor_scalar(mx[:, n % 2, 0:1], mx[:, n % 2, 0:1], SCALE,
                                                       sinks[:, bass.ds(layer * SWA_HEADS + h, 1)], ALU.mult, ALU.max))
                                dve.tensor_scalar(nb[:, n % 2, 0:1], mx[:, n % 2, 0:1], -1.0, None, ALU.mult).then_inc(sems["nb_ready"], 1)

                        def normalise(n):
                            nsa, h, i, k0 = units[n]
                            w_ = (i + 1 - k0) * P
                            br = 2 if nsa else 1
                            dve.wait_ge(sems["exp_done"], n + 3)
                            if not nsa:
                                then(dve.tensor_tensor(sums[:, n % 2, 0:1], sums[:, n % 2, 0:1], e_sink[:, n % 2:n % 2 + 1], ALU.add))
                            then(dve.reciprocal(rec[:, n % 2, 0:br], sums[:, n % 2, 0:br]))
                            if nsa:
                                then(dve.tensor_tensor(rec[:, n % 2, :], rec[:, n % 2, :], gates[:, i, 3 * h + 1:3 * h + 3], ALU.mult))
                            for b in range(br):
                                d = dve.tensor_scalar(prob[:, n % 2, b, 0:w_], prob[:, n % 2, b, 0:w_], rec[:, n % 2, b:b + 1], None, ALU.mult)
                            d.then_inc(sems["p_norm"], 1)

                        def out_lo(g):
                            dve.wait_ge(sems["o_hi"], g + 1)
                            j = GROUP_TILE[g]
                            dve.tensor_tensor(xlo[:, j, :], ps[:, 6, :], xhi[:, j, :], ALU.subtract).then_inc(sems["o_lo"], 1)

                        for n in range(UNITS + 3):
                            if n < UNITS:
                                row_max(n)
                            if 1 <= n <= UNITS:
                                normalise(n - 1)
                            if 2 <= n < UNITS + 2 and (units[n - 2][0] or (n - 2) % 2 == 1):
                                m = n - 2
                                nsa, h, i, k0 = units[m]
                                w_ = (i + 1 - k0) * P
                                dve.wait_ge(sems["pt_ready"], m + 1)
                                if m >= 3:
                                    dve.wait_ge(sems["pv_done"], m - 2)
                                dve.tensor_copy(prob_t[:, m % 3, 1 if nsa else 0, 0:w_], ps[:, 5, 0:w_]).then_inc(sems["ev_dve"], 1)
                            if n >= 10 and n % 8 == 2 and n <= UNITS:
                                out_lo((n - 10) // 8)
                            between(n)
                        out_lo(UNITS // 8 - 1)

                        def residual(q, par_):
                            for u in range(2):
                                dve.wait_ge(sems["mm_done"], DT + 2 * q + u + SPLIT + 1)
                                dve.tensor_tensor(at(xT, 2 * q + u), at(xT, 2 * q + u), ps[:, 2 * par_ + u, :],
                                                  ALU.add).then_inc(sems["y_done"], 1)
                        dve.wait_ge(sems["half_done"], DT)

                        def pair(q, par_):
                            residual(q, par_)
                            if isinstance(q, int) and q == PAIRS - 2:
                                m0_dve(dve, sems)
                                centre_dve(dve, sems, range(DT - 2), seed=4)
                        in_pairs(dve, PAIRS, chunks(lambda c, s: split_lo(dve, sems, w, c, s, KH)), pair)
                        centre_dve(dve, sems, (DT - 2,), seed=4)
                        centre_last(dve, sems, sq, seed=4)
                clear(sems)

        ORDER = [T_HF, T_HQ, T_HI, T_HF + 1, T_HQ + 1, T_HI + 1, T_HF + 2, T_HQ + 2, T_HI + 2, T_HF + 3, T_HQ + 3,
                 T_HI + 3, T_CMP, T_Q, T_Q + 1, T_SLC, T_WIN, T_SQ, T_SQ + 1, T_SK, T_SV, T_GATE, T_HG, T_HG + 1,
                 T_HG + 2, T_HG + 3]
        FIRST_STEP = 6
        FIRST_ROPE = FIRST_STEP + HGRN_HEADS * QT
        CMP_CHUNKS = 4
        ROPE = [("q", T_Q, 0, T_HQ), ("q", T_Q + 1, 0, T_HQ + 1), ("k", T_SLC, 0, T_HF), ("k", T_WIN, 0, T_HF + 1),
                ("q", T_SQ, 0, T_SQ), ("q", T_SQ + 1, 0, T_SQ + 1), ("k", T_SK, 0, T_HQ + 2), ("k", T_SK, 64, T_HF + 2)]
        rope_pool = [1, 2, 2, 2, 3, 4, 4, 4]
        BLK = (T_HQ + 3, T_HF + 3)
        V_TILE = (T_SK, T_SV, T_HQ + 3, T_HF + 3)

        def project_hgrn2(layer, proj, gates):
            stage[0] = "hgrn"
            H, STEPS = HGRN_HEADS, HGRN_HEADS * QT
            with scope() as ctx:
                w = Weights(ctx, DT)
                hmask = sb(ctx, "hmask", [P, (LEVELS + 1) * P])
                reset = sb(ctx, "reset", [P, SEQ])
                lsp = sb(ctx, "lsp", [P, SEQ])
                lsg = sb(ctx, "lsg", [P, SEQ])
                karg = sb(ctx, "karg", [P, SEQ])
                logf = sb(ctx, "logf", [P, SEQ])
                cum = sb(ctx, "cum", [P, SEQ])
                lev = sb(ctx, "lev", [P, 2, LEVELS, SEQ])
                qd = sb(ctx, "qd", [P, 2, SEQ])
                kd = sb(ctx, "kd", [P, 2, SEQ])
                dec = sb(ctx, "dec", [P, 2, QT])
                v_tok = sb(ctx, "v_tok", [P, 2, QT, P])
                masked = sb(ctx, "masked", [P, (LEVELS + 1) * P])
                att = sb(ctx, "att", [P, P])
                kd_t = sb(ctx, "kd_t", [P, P])
                state = sb(ctx, "state", [P, 2, P])
                var = sb(ctx, "var", [P, SEQ])
                rms = sb(ctx, "rms", [P, SEQ])
                r0 = lev[:, 0, 0, :]
                rotm = sb(ctx, "rotm", [P, 3 * P])
                pos2 = var[0:CMP_LEN, 0:P]
                pos_t = sb(ctx, "pos_t", [P, CMP_LEN])
                cos, sin, sin_part = lsp, lsg, (karg, logf)
                ngc = sb(ctx, "ngc", [P, HGRN_HEADS])
                hgc = sb(ctx, "hgc", [P, 3, HGRN_HEADS])
                sems = semaphores(STREAM + LN + ["out_act", "out_dve", "aux_in", "reset_done", "step", "act_step", "a0", "d0",
                                            "a1", "d1", "d2", "p2", "a2", "d3", "p3", "c_mm", "c_read", "att_done", "b4_mm",
                                            "b4_out", "st_mm", "st_out", "pv_done", "o_raw", "sq_done", "ms_mm",
                                            "ms_out", "rs_act", "o_done", "mask_in", "rope_in", "pos_turned", "pos_out",
                                            "blk_done", "rope_mm", "rope_cos", "rope_step", "rope_out", "cmp_mm",
                                            "v_turned", "hg_silu", "hg_gated", "hg_hi"], slots=[("raw_in", RAW)])

                def projected(eng, tile):
                    s = ORDER.index(tile)
                    eng.wait_ge(sems["out_dve" if s % 2 else "out_act"], s // 2 + 1)

                def pairs(t, lv, side):
                    m = 1 << lv
                    return t.rearrange("p (b s m) -> p s b m", s=2, m=m)[:, side]

                def last_of(t, lv):
                    m = 1 << lv
                    v = t.rearrange("p (b s m) -> p s b m", s=2, m=m)[:, 0, :, m - 1:m]
                    return v.broadcast_to([P, SEQ // (2 * m), m])

                def b4_before_v(h):
                    return 4 * h

                def b4_before_k(h, c):
                    return 4 * h + 1 + c

                def blocks_of(kv):
                    return proj[:, BLK[kv], :].rearrange("p (l n) -> p l n", n=32)

                def value_tile(n):
                    return proj[:, V_TILE[n], 0:QT * HEAD_DIM].rearrange("p (c d) -> p c d", d=HEAD_DIM)

                def squares_step(h):
                    return min(QT * h + 5, STEPS + 1)

                def w_cmp(c):
                    return w.raw[:, c % RAW].rearrange("p k n -> p (k n)").rearrange("p (a m) -> p a m", m=CMP_HID)

                with nc.Block() as block:
                    @block.sync
                    def _(sp):
                        for s, tile in enumerate(ORDER):
                            c0 = tile * P if tile < T_SQ else NSA_COLS + (tile - T_SQ) * P
                            load_chunk(sp, sems, w.raw, s, s % RAW, cols_of(w_in, layer, 0, DT, c0), DT)
                            if s == 3:
                                sp.dma_start(hmask[:], consts_d[:, C_HG:C_END]).then_inc(sems["mask_in"], 16)
                                for half in (0, 64):
                                    sp.dma_start(pos2[:, half:half + 64], cmp_pos[bass.ds(layer, 1), :, :].rearrange(
                                        "a l d -> (a l) d")).then_inc(sems["aux_in"], 16)
                                sp.dma_start(rotm[:], consts_d[:, C_ROT:C_ROT + 3 * P]).then_inc(sems["aux_in"], 16)
                            if s == 20:
                                sp.wait_ge(sems["d1"], H)
                                sp.wait_ge(sems["a1"], H)
                                sp.dma_start(cos[:], rope_d[:, 0:SEQ]).then_inc(sems["rope_in"], 16)
                                sp.dma_start(sin[:], rope_d[:, SEQ:2 * SEQ]).then_inc(sems["rope_in"], 16)
                        for j in range(2 * CMP_CHUNKS):
                            c = N_PM + j
                            sp.wait_ge(sems["lo_done"], min(c, N_PM + RAW - 1) + 1)
                            if j >= RAW:
                                sp.wait_ge(sems["cmp_mm"], j - RAW + 1)
                            src = (cmp_k_w1, cmp_v_w1)[j // CMP_CHUNKS].rearrange("l (t p) n -> l p t n", p=P)
                            t = j % CMP_CHUNKS * 4
                            sp.dma_start(w_cmp(c), src[bass.ds(layer, 1), :, t:t + 4, :].rearrange("a p t n -> (a p) t n")
                                         ).then_inc(sems["raw_in"][c % RAW], 16)

                    @block.tensor
                    def _(pe):
                        pe.sem_inc(sems["mm_done"], SPLIT)

                        def values_turned(h):
                            if b4_before_v(h):
                                pe.wait_ge(sems["b4_out"], b4_before_v(h))
                            projected(pe, T_HI + h)
                            for c in range(QT):
                                mm = pe.transpose(ps[:, 4, c * P:(c + 1) * P], proj[:, T_HI + h, c * P:(c + 1) * P], ident[:])
                            mm.then_inc(sems["b4_mm"], 1)

                        def products(n):
                            h, c, tok = n // QT, n % QT, slice(n % QT * P, n % QT * P + P)
                            if c == 0:
                                pe.wait_ge(sems["d3"], h + 1)
                                pe.wait_ge(sems["p3"], h + 1)
                            if n:
                                pe.wait_ge(sems["c_read"], n)
                            for lv in range(LEVELS + 1):
                                o = ps[:, 2 + lv // 4, (lv % 4) * P:(lv % 4 + 1) * P]
                                if lv < LEVELS:
                                    both = lev[:, h % 2, lv, tok]
                                    mm = pe.matmul(o, both, both, start=True, stop=True)
                                else:
                                    mm = pe.matmul(o, proj[:, T_HF + h, tok], proj[:, T_HQ + h, tok], start=True, stop=True)
                            mm.then_inc(sems["c_mm"], 1)
                            if c < QT - 1:
                                pe.wait_ge(sems["b4_out"], b4_before_k(h, c))
                                pe.transpose(ps[:, 4, 0:P], kd[:, h % 2, tok], ident[:]).then_inc(sems["b4_mm"], 1)
                            elif h + 1 < H:
                                values_turned(h + 1)

                        def outputs(n):
                            h, c, tok = n // QT, n % QT, slice(n % QT * P, n % QT * P + P)
                            if c < QT - 1:
                                pe.wait_ge(sems["b4_out"], b4_before_k(h, c) + 1)
                                if 3 * h + c:
                                    pe.wait_ge(sems["st_out"], 3 * h + c)
                                pe.matmul(ps[:, 5, 0:P], kd_t[:], v_tok[:, h % 2, c, :], start=True,
                                          stop=True).then_inc(sems["st_mm"], 1)
                            if c == 0 and h:
                                pe.wait_ge(sems["o_raw"], h)
                            if c > 0:
                                pe.wait_ge(sems["st_out"], 3 * h + c)
                                pe.matmul(ps[:, 6, tok], state[:, (c - 1) % 2, :], qd[:, h % 2, tok], start=True, stop=False)
                            pe.wait_ge(sems["att_done"], n + 1)
                            pe.matmul(ps[:, 6, tok], v_tok[:, h % 2, c, :], att[:], start=(c == 0),
                                      stop=True).then_inc(sems["pv_done"], 1)

                        def rotate(r):
                            a, b = 2 + 2 * (r % 2), 3 + 2 * (r % 2)
                            kind, src, half, _dst = ROPE[r]
                            if r == 0:
                                pe.wait_ge(sems["c_read"], STEPS)
                            if r == 1:
                                pe.wait_ge(sems["b4_out"], 4 * H)
                                pe.wait_ge(sems["st_out"], 3 * H)
                            if r >= 2:
                                pe.wait_ge(sems["rope_out"], r - 1)
                            projected(pe, src)
                            if kind == "q":
                                pe.matmul(ps[:, a, :], rotm[:, 0:P], proj[:, src, :], start=True, stop=True).then_inc(sems["rope_mm"], 1)
                            else:
                                rows_ = slice(half, half + 64)
                                pe.matmul(ps[:, a, :], rotm[rows_, 2 * P:3 * P], proj[rows_, src, :], start=True, stop=True)
                                pe.matmul(ps[:, b, :], rotm[rows_, P:2 * P], proj[rows_, src, :], start=True,
                                          stop=True).then_inc(sems["rope_mm"], 1)

                        multiply_first(pe, sems, w, DT)
                        for s in range(2, N_PM):
                            pe.wait_ge(sems["out_dve" if s % 2 else "out_act"], s // 2)
                            multiply(pe, sems, w, s, s % RAW, DT, s % 2, lambda k: xhi[:, k, :], lambda k: xlo[:, k, :])
                            n = s - FIRST_STEP
                            if s == 4:
                                pe.wait_ge(sems["aux_in"], 16 * 3)
                                pe.transpose(ps[:, 7, 0:CMP_LEN], pos2, ident[0:CMP_LEN, 0:CMP_LEN]).then_inc(sems["pos_turned"], 1)
                            if n == -1:
                                values_turned(0)
                            if 1 <= n <= STEPS:
                                outputs(n - 1)
                            for h in range(H):
                                if n == squares_step(h) + 1:
                                    pe.wait_ge(sems["sq_done"], h + 1)
                                    pe.wait_ge(sems["pos_out"], 1)
                                    if h:
                                        pe.wait_ge(sems["ms_out"], h)
                                    pe.matmul(ps[:, 7, :], mean_w[:], rms[:], start=True, stop=True).then_inc(sems["ms_mm"], 1)
                            if 0 <= n < STEPS:
                                products(n)
                            if s >= FIRST_ROPE:
                                rotate(2 * (s - FIRST_ROPE))
                                rotate(2 * (s - FIRST_ROPE) + 1)

                        pe.wait_ge(sems["blk_done"], 2)
                        pe.wait_ge(sems["ms_out"], H)
                        for j in range(2 * CMP_CHUNKS):
                            kv, c = j // CMP_CHUNKS, N_PM + j
                            pe.wait_ge(sems["raw_in"][c % RAW], 16 * (c // RAW + 1))
                            for k in range(4):
                                l = j % CMP_CHUNKS * 4 + k
                                mm = pe.matmul(ps[0:N_CMP, 7, kv * CMP_HID:(kv + 1) * CMP_HID], blocks_of(kv)[:, l, 0:N_CMP],
                                               w_cmp(c)[:, k, :], start=(l == 0), stop=(l == 4 * CMP_CHUNKS - 1))
                            mm.then_inc(sems["cmp_mm"], 1)

                        pe.wait_ge(sems["rope_out"], 8)
                        for n, t in enumerate((T_SLC, T_WIN, T_SV, T_GATE)):
                            projected(pe, t)
                            for c in range(QT):
                                mm = pe.transpose(ps[:, 2 + n, c * P:(c + 1) * P], proj[:, t, c * P:(c + 1) * P], ident[:])
                            mm.then_inc(sems["v_turned"], 1)

                    @block.scalar
                    def _(act):
                        st = [0]

                        def then(ins):
                            ins.then_inc(sems["act_step"], 1)
                            st[0] += 1
                            act.wait_ge(sems["act_step"], st[0])

                        def part(h, k):
                            if k == 0:
                                projected(act, T_HF + h)
                                if h:
                                    act.wait_ge(sems["d0"], h)
                                then(act.activation(lsp[:], proj[:, T_HF + h, :], ACT.Abs))
                                then(act.activation(lsp[:], lsp[:], ACT.Exp, scale=-1.0))
                                act.activation(lsp[:], lsp[:], ACT.Ln, bias=1.0).then_inc(sems["a0"], 1)
                            if k == 1:
                                act.wait_ge(sems["d0"], h + 1)
                                act.activation(proj[:, T_HF + h, :], karg[:], ACT.Exp, scale=-1.0, bias=hgc[:, 1, h:h + 1])
                                then(act.activation(lsg[:], lsg[:], ACT.Abs))
                                then(act.activation(lsg[:], lsg[:], ACT.Exp, scale=-1.0))
                                act.activation(lsg[:], lsg[:], ACT.Ln, bias=1.0).then_inc(sems["a1"], 1)
                            if k == 2:
                                act.wait_ge(sems["d2"], h + 1)
                                act.wait_ge(sems["p2"], h + 1)
                                l2 = lev[:, h % 2].rearrange("p l n -> p (l n)")
                                act.activation(l2, l2, ACT.Exp)
                                act.activation(kd[:, h % 2, :], kd[:, h % 2, :], ACT.Exp)
                                act.activation(dec[:, h % 2, :], cum[:, :].rearrange("p (c n) -> p c n", n=P)[:, :, P - 1], ACT.Exp)
                                act.activation(qd[:, h % 2, :], cum[:], ACT.Exp).then_inc(sems["a2"], 1)

                        def values_out(h):
                            act.wait_ge(sems["b4_mm"], b4_before_v(h) + 1)
                            if h >= 2:
                                act.wait_ge(sems["pv_done"], QT * (h - 1))
                            act.activation(v_tok[:, h % 2].rearrange("p c d -> p (c d)"), ps[:, 4, :], ACT.Copy).then_inc(sems["b4_out"], 1)

                        ln_act(act, sems, 0, r0, lambda: split_hi(act, sems, w, 0, 0, DT), lambda: split_hi(act, sems, w, 1, 1, DT))
                        for s in range(1, N_PM + 1):
                            n, h, c = s - FIRST_STEP, (s - FIRST_STEP) // QT, (s - FIRST_STEP) % QT
                            if s + 1 < N_PM:
                                split_hi(act, sems, w, s + 1, (s + 1) % RAW, DT)
                            if s % 2 and s <= N_PM:
                                act.wait_ge(sems["mm_done"], s - 1 + SPLIT + 1)
                                act.activation(proj[:, ORDER[s - 1], :], ps[:, 0, :], ACT.Copy).then_inc(sems["out_act"], 1)
                            if -4 <= n < STEPS and c < 3 and h + 1 < H:
                                part(h + 1, c)
                            if n == -1:
                                values_out(0)
                            if 0 <= n < STEPS and c < QT - 1:
                                act.wait_ge(sems["b4_mm"], b4_before_k(h, c) + 1)
                                if 3 * h + c:
                                    act.wait_ge(sems["st_mm"], 3 * h + c)
                                act.activation(kd_t[:], ps[:, 4, 0:P], ACT.Copy).then_inc(sems["b4_out"], 1)
                            elif 0 <= n < STEPS - 1:
                                values_out(h + 1)
                            for g in range(H):
                                if n == squares_step(g):
                                    act.wait_ge(sems["o_raw"], g + 1)
                                    if g:
                                        act.wait_ge(sems["o_done"], g)
                                    act.activation(rms[:], proj[:, T_HI + g, :], ACT.Square).then_inc(sems["sq_done"], 1)
                                if n == squares_step(g) + 1:
                                    act.wait_ge(sems["ms_out"], g + 1)
                                    then(act.activation(rms[:], var[:], ACT.Ln))
                                    act.activation(rms[:], rms[:], ACT.Exp, scale=-0.5).then_inc(sems["rs_act"], 1)
                        act.preload_act_table_set("silu_and_others")
                        for h in range(H):
                            projected(act, T_HG + h)
                            act.activation(proj[:, T_HG + h, :], proj[:, T_HG + h, :], ACT.Silu).then_inc(sems["hg_silu"], 1)
                        act.wait_ge(sems["mm_done"], N_PM + SPLIT)
                        for h in range(H):
                            act.wait_ge(sems["hg_gated"], h + 1)
                            act.activation(xhi[:, 4 + h, :], proj[:, T_HI + h, :], ACT.Copy).then_inc(sems["hg_hi"], 1)
                        act.wait_ge(sems["cmp_mm"], 2 * CMP_CHUNKS)
                        act.activation(proj[0:N_CMP, T_CMP, :], ps[0:N_CMP, 7, :], ACT.Silu)
                        act.wait_ge(sems["v_turned"], 4)
                        src = ps[:, 5, :].rearrange("p (c d) -> p c d", d=P)[:, :, 0:3 * NSA_HEADS]
                        act.activation(gates[:], src, ACT.Tanh, scale=0.5)
                        for n in range(2):
                            src = ps[:, 2 + n, :].rearrange("p (c d) -> p c d", d=P)[:, :, HEAD_DIM:2 * HEAD_DIM]
                            act.activation(value_tile(n), src, ACT.Copy)
                        act.preload_act_table_set("natural_log_exp_and_others")

                    @block.vector
                    def _(dve):
                        dve.sem_inc(sems["lo_done"], RAW)
                        st = [0]

                        def then(ins):
                            ins.then_inc(sems["step"], 1)
                            st[0] += 1
                            dve.wait_ge(sems["step"], st[0])

                        def part(h, k):
                            z, hp = proj[:, T_HF + h, :], h % 2
                            if k == 0:
                                dve.wait_ge(sems["a0"], h + 1)
                                dve.scalar_tensor_tensor(out=karg[:], in0=z, scalar=0.0, in1=lsp[:], op0=ALU.max, op1=ALU.add)
                                then(dve.scalar_tensor_tensor(out=lsg[:], in0=z, scalar=0.0, in1=lsp[:], op0=ALU.min, op1=ALU.subtract))
                                dve.tensor_scalar(logf[:], lsg[:], hgc[:, 1, h:h + 1], hgc[:, 0, h:h + 1], ALU.add, ALU.max)
                                dve.tensor_scalar(lsg[:], lsg[:], hgc[:, 2, h:h + 1], None, ALU.add).then_inc(sems["d0"], 1)
                            if k == 1:
                                dve.wait_ge(sems["a1"], h + 1)
                                dve.wait_ge(sems["reset_done"], 2)
                                then(dve.tensor_tensor(logf[:], logf[:], lsg[:], ALU.add))
                                if h:
                                    dve.wait_ge(sems["a2"], h)
                                    dve.wait_ge(sems["p2"], h)
                                dve.tensor_tensor_scan(cum[:], reset[:], logf[:], 0.0, ALU.mult, ALU.add).then_inc(sems["d1"], 1)
                            if k == 2:
                                dve.wait_ge(sems["d1"], h + 1)
                                if h >= 2:
                                    dve.wait_ge(sems["pv_done"], QT * (h - 1))
                                for lv in range(LEVELS):
                                    dve.tensor_tensor(pairs(lev[:, hp, lv, :], lv, 1), pairs(cum[:], lv, 1),
                                                      last_of(cum[:], lv), ALU.subtract)
                                cv = cum[:, :].rearrange("p (c n) -> p c n", n=P)
                                dve.tensor_tensor(kd[:, hp, :].rearrange("p (c n) -> p c n", n=P), cv[:, :, P - 1:P].broadcast_to([P, QT, P]),
                                                  cv, ALU.subtract).then_inc(sems["d2"], 1)
                            if k == 3:
                                dve.wait_ge(sems["a2"], h + 1)
                                projected(dve, T_HQ + h)
                                for lv in range(LEVELS):
                                    r = pairs(lev[:, hp, lv, :], lv, 1)
                                    d = dve.tensor_tensor(r, r, pairs(proj[:, T_HQ + h, :], lv, 1), ALU.mult)
                                d.then_inc(sems["d3"], 1)

                        def rotate(r):
                            kind, src, half, dst = ROPE[r]
                            a, b = 2 + 2 * (r % 2), 3 + 2 * (r % 2)
                            dst, part_ = proj[:, dst, :], sin_part[r % 2][:]
                            if r == 0:
                                dve.wait_ge(sems["rope_in"], 32)
                            dve.wait_ge(sems["rope_mm"], r + 1)
                            if kind == "q":
                                dve.tensor_tensor(part_, ps[:, a, :], sin[:], ALU.mult).then_inc(sems["rope_step"], 1)
                                dve.wait_ge(sems["rope_cos"], rope_pool[r])
                            else:
                                dve.tensor_tensor(dst, ps[:, b, :], cos[:], ALU.mult)
                                dve.tensor_tensor(part_, ps[:, a, :], sin[:], ALU.mult).then_inc(sems["rope_step"], 1)
                            dve.wait_ge(sems["rope_step"], r + 1)
                            dve.tensor_tensor(dst, dst, part_, ALU.add).then_inc(sems["rope_out"], 1)

                        def cut_blocks(kv):
                            if kv == 0:
                                dve.wait_ge(sems["pos_out"], 1)
                                dve.wait_ge(sems["c_mm"], STEPS)
                                projected(dve, T_CMP)
                            rows_ = slice(64 * kv, 64 * kv + 64)
                            full = proj[rows_, T_CMP, :]
                            for s_ in range(2):
                                for hi_l in range(2):
                                    src = (full[:, 16 * hi_l:16 * hi_l + 16 * N_CMP].rearrange("p (n l s) -> p s l n", l=8, s=2)[:, s_])
                                    pos = pos_t[rows_, 16 * hi_l:16 * hi_l + 16].rearrange("p (l s) -> p s l", s=2)[:, s_]
                                    d = dve.tensor_tensor(blocks_of(kv)[64 * s_:64 * s_ + 64, 8 * hi_l:8 * hi_l + 8, 0:N_CMP], src,
                                                          pos[:, :, None].broadcast_to([64, 8, N_CMP]), ALU.add)
                            d.then_inc(sems["blk_done"], 1)

                        dve.tensor_copy(ngc[:], par[:, bass.ds(layer * HGRN_HEADS + PNG, HGRN_HEADS)])
                        src = hgp[:, bass.ds(layer, 1), :, :].rearrange("p a k h -> p (a k h)")
                        then(dve.tensor_copy(hgc[:, :, :].rearrange("p k h -> p (k h)"), src))
                        ln_dve(dve, sems, 4.0 * LN_EPS, r0, lambda: split_lo(dve, sems, w, 0, 0, DT))
                        for s in range(1, N_PM + 1):
                            n, h, c = s - FIRST_STEP, (s - FIRST_STEP) // QT, (s - FIRST_STEP) % QT
                            if s + 1 < N_PM:
                                split_lo(dve, sems, w, s + 1, (s + 1) % RAW, DT)
                            if s % 2 == 0 and s >= 2:
                                dve.wait_ge(sems["mm_done"], s - 1 + SPLIT + 1)
                                dve.tensor_copy(proj[:, ORDER[s - 1], :], ps[:, 1, :]).then_inc(sems["out_dve"], 1)
                            if -4 <= n < STEPS and h + 1 < H:
                                part(h + 1, c)
                            if n >= 1 and (n - 1) % QT < QT - 1 and n <= STEPS:
                                g, b = (n - 1) // QT, (n - 1) % QT
                                dve.wait_ge(sems["st_mm"], 3 * g + b + 1)
                                if b == 0:
                                    if g:
                                        dve.wait_ge(sems["pv_done"], n - 1)
                                    dve.tensor_copy(state[:, 0, :], ps[:, 5, 0:P]).then_inc(sems["st_out"], 1)
                                else:
                                    dve.wait_ge(sems["pv_done"], n - 1)
                                    dve.wait_ge(sems["st_out"], 3 * g + b)
                                    dve.scalar_tensor_tensor(out=state[:, b % 2, :], in0=state[:, (b - 1) % 2, :],
                                                             scalar=dec[:, g % 2, b:b + 1], in1=ps[:, 5, 0:P],
                                                             op0=ALU.mult, op1=ALU.add).then_inc(sems["st_out"], 1)
                            if n == 0:
                                dve.wait_ge(sems["mask_in"], 16)
                            if 0 <= n < STEPS:
                                dve.wait_ge(sems["c_mm"], n + 1)
                                both = ps[:, 2:4, :].rearrange("p a n -> p (a n)")
                                dve.tensor_tensor(masked[:], both, hmask[:], ALU.mult).then_inc(sems["c_read"], 1)
                                dve.wait_ge(sems["c_read"], n + 1)
                                if n:
                                    dve.wait_ge(sems["pv_done"], n)
                                dve.tensor_reduce(att[:], masked[:, :].rearrange("p (l t) -> p t l", t=P), AX.X,
                                                  ALU.add).then_inc(sems["att_done"], 1)
                            for g in range(H):
                                if n == QT * g + QT:
                                    dve.wait_ge(sems["pv_done"], n)
                                    dve.tensor_copy(proj[:, T_HI + g, :], ps[:, 6, :]).then_inc(sems["o_raw"], 1)
                                if n == squares_step(g) + 1:
                                    dve.wait_ge(sems["ms_mm"], g + 1)
                                    dve.tensor_scalar(var[:], ps[:, 7, :], float(D_MODEL // P), RMS_EPS, ALU.mult, ALU.add).then_inc(sems["ms_out"], 1)
                                if n == squares_step(g) + 2:
                                    o = proj[:, T_HI + g, :]
                                    dve.wait_ge(sems["rs_act"], g + 1)
                                    then(dve.tensor_tensor(var[:], var[:], rms[:], ALU.mult))
                                    then(dve.scalar_tensor_tensor(out=var[:], in0=var[:], scalar=-0.5, in1=rms[:],
                                                                  op0=ALU.mult, op1=ALU.mult))
                                    then(dve.scalar_tensor_tensor(out=var[:], in0=var[:], scalar=1.5, in1=rms[:],
                                                                  op0=ALU.add, op1=ALU.mult))
                                    dve.scalar_tensor_tensor(out=o, in0=var[:], scalar=ngc[:, g:g + 1], in1=o,
                                                             op0=ALU.mult, op1=ALU.mult).then_inc(sems["o_done"], 1)
                            if s == 5:
                                dve.wait_ge(sems["pos_turned"], 1)
                                dve.tensor_copy(pos_t[:], ps[:, 7, 0:CMP_LEN]).then_inc(sems["pos_out"], 1)
                            if FIRST_ROPE <= s < N_PM:
                                rotate(2 * (s - FIRST_ROPE))
                                rotate(2 * (s - FIRST_ROPE) + 1)
                            if s in (FIRST_ROPE + 1, FIRST_ROPE + 2):
                                cut_blocks(s - FIRST_ROPE - 1)
                        for h in range(H):
                            dve.wait_ge(sems["hg_silu"], h + 1)
                            dve.wait_ge(sems["o_done"], h + 1)
                            o = proj[:, T_HI + h, :]
                            dve.tensor_tensor(o, o, proj[:, T_HG + h, :], ALU.mult).then_inc(sems["hg_gated"], 1)
                        for h in range(H):
                            dve.wait_ge(sems["hg_hi"], h + 1)
                            dve.tensor_tensor(xlo[:, 4 + h, :], proj[:, T_HI + h, :], xhi[:, 4 + h, :], ALU.subtract)
                        dve.wait_ge(sems["v_turned"], 3)
                        dve.wait_ge(sems["cmp_mm"], 2 * CMP_CHUNKS)
                        for n in range(2):
                            src = ps[:, 4, :].rearrange("p (c k d) -> p c k d", d=HEAD_DIM, k=2)[:, :, n]
                            dve.tensor_copy(value_tile(2 + n), src)

                    @block.gpsimd
                    def _(pool):
                        ln_pool(pool, sems, w)
                        pool.memset(reset[:], 1.0).then_inc(sems["reset_done"], 1)
                        pool.wait_ge(sems["reset_done"], 1)
                        pool.memset(reset[:, :].rearrange("p (c n) -> p c n", n=P)[:, :, 0:1], 0.0).then_inc(sems["reset_done"], 1)
                        for h in range(H):
                            hp = h % 2
                            pool.wait_ge(sems["d1"], h + 1)
                            if h >= 2:
                                pool.wait_ge(sems["pv_done"], QT * (h - 1))
                            for lv in range(LEVELS):
                                d = pool.tensor_tensor(pairs(lev[:, hp, lv, :], lv, 0), last_of(cum[:], lv),
                                                       pairs(cum[:], lv, 0), ALU.subtract)
                            d.then_inc(sems["p2"], 1)
                            pool.wait_ge(sems["a2"], h + 1)
                            for lv in range(LEVELS):
                                left = pairs(lev[:, hp, lv, :], lv, 0)
                                pool.tensor_tensor(left, left, pairs(proj[:, T_HF + h, :], lv, 0), ALU.mult)
                            pool.tensor_tensor(kd[:, hp, :], kd[:, hp, :], proj[:, T_HF + h, :], ALU.mult)
                            projected(pool, T_HQ + h)
                            pool.tensor_tensor(qd[:, hp, :], qd[:, hp, :], proj[:, T_HQ + h, :], ALU.mult).then_inc(sems["p3"], 1)
                        pool.wait_ge(sems["rope_in"], 32)
                        for r in range(8):
                            kind, src, half, dst = ROPE[r]
                            if kind == "q":
                                pool.wait_ge(sems["rope_mm"], r + 1)
                                pool.tensor_tensor(proj[:, dst, :], proj[:, src, :], cos[:], ALU.mult).then_inc(sems["rope_cos"], 1)
                clear(sems)

        def mixer(layer):
            stage[0] = "mix"
            with scope() as ctx:
                proj = sb(ctx, "proj", [P, N_PM, SEQ])
                gates = sb(ctx, "gates", [P, QT, 3 * NSA_HEADS])
                project_hgrn2(layer, proj, gates)
                attention(layer, proj, gates)

        with nc.Fori(0, DEPTH) as layer:
            ffn(layer, 0)
            mixer(layer)
            ffn(layer, 1)

        stage[0] = "end"
        with scope() as ctx:
            xo = sb(ctx, "xo", [P, QT, D_MODEL])
            sems = semaphores(["turned", "emptied", "stored"])
            with nc.Block() as block:
                @block.tensor
                def _(pe):
                    n = 0
                    for t in range(QT):
                        for h in range(2):
                            if n >= 4:
                                pe.wait_ge(sems["emptied"], n - 3)
                            for j in range(4):
                                mm = pe.transpose(ps[:, n % 4, j * P:(j + 1) * P],
                                                  xT[:, 4 * h + j, t * P:(t + 1) * P], ident[:])
                            mm.then_inc(sems["turned"], 1)
                            n += 1

                @block.vector
                def _(dve):
                    for n in range(2 * QT):
                        dve.wait_ge(sems["turned"], n + 1)
                        dve.tensor_copy(xo[:, n // 2, (n % 2) * 512:(n % 2 + 1) * 512], ps[:, n % 4, :]).then_inc(sems["emptied"], 1)

                @block.sync
                def _(sp):
                    for t in range(QT):
                        sp.wait_ge(sems["emptied"], 2 * t + 2)
                        sp.dma_start(out[0, t * P:(t + 1) * P, :], xo[:, t, :]).then_inc(sems["stored"], 16)
                    sp.wait_ge(sems["stored"], 16 * QT)


_INS = ['x', 'p', 'ln_g', 'ln_b', 'ffn_w_gu', 'ffn_w_down', 'w_in', 'w_out', 'cmp_pos', 'cmp_k_w1', 'cmp_k_w2',
        'cmp_v_w1', 'cmp_v_w2', 'swa_sinks', 'hgrn_lb_raw', 'hgrn_norm_g', 'ple_w', 'ple_gate_w', 'ple_gate_b']


def kernel(**inputs):
    import concourse.bacc as bacc
    from concourse.bass_utils import run_bass_kernel_spmd

    nc = bacc.Bacc("TRN2", target_bir_lowering=False, num_devices=1)
    consts, rope = shape_constants()
    named = {f"in_{name}_dram": np.ascontiguousarray(inputs[name]) for name in _INS}
    named["in_consts_dram"] = consts
    named["in_rope_dram"] = rope
    args = [nc.dram_tensor(name, a.shape, mybir.dt.from_np(a.dtype), kind="ExternalInput").ap()
            for name, a in named.items()]
    out = nc.dram_tensor("out_0_dram", (1, SEQ, D_MODEL), F32, kind="ExternalOutput").ap()
    build(nc, *args, out)
    r = run_bass_kernel_spmd(nc, [named], core_ids=[0])
    return r.results[0]["out_0_dram"]
```
